# Optimizing a Trainium2 kernel written in Bass

```python
import math
import jax
import jax.numpy as jnp
from jax import lax
import numpy as np

D_MODEL = 1024
BATCH = 1
SEQ = 256
DEPTH = 2

D_MIX = 2 * D_MODEL
CONV_WIDTH = 4
EPS = 1e-6
N_ADA = 6
SSD_INNER = D_MIX // 2
SSD_HEADDIM = 64
SSD_HEADS = SSD_INNER // SSD_HEADDIM
SSD_GROUPS = 2
SSD_HPG = SSD_HEADS // SSD_GROUPS
SSD_STATE = 128
SSD_CHUNK = 128
SSD_CONV_DIM = SSD_INNER + 2 * SSD_GROUPS * SSD_STATE
HG_WIDTH = D_MIX // 4
HG_EXPAND = 128
HG_HEADS = HG_WIDTH // HG_EXPAND
HG_CHUNK = 64
LRU_WIDTH = D_MIX // 4
LRU_BLOCKS = 8
LRU_BLOCK_W = LRU_WIDTH // LRU_BLOCKS
LRU_C = 8.0
N_EXPERTS = 64
TOP_K = 8
N_EXPERT_GROUPS = 8
E_PER_GROUP = N_EXPERTS // N_EXPERT_GROUPS
TOPK_GROUPS = 4
D_EXPERT = 256
D_SHARED = 256
ROUTED_SCALE = 2.5
MASK_SCORE = -1.0e4
MOE_BLOCK = 256
IN_SIZES = (SSD_INNER, SSD_CONV_DIM, SSD_HEADS, HG_WIDTH, HG_WIDTH, HG_WIDTH, HG_WIDTH, LRU_WIDTH, LRU_WIDTH)
IN_SPLITS = tuple(int(s) for s in np.cumsum(IN_SIZES)[:-1])
D_IN = int(sum(IN_SIZES))

kernel_name = 'hybrid_ssd_hgrn2_rglru_moe_adaln'

def rms_norm(x, w):
    xf = x.astype(jnp.float32)
    y = xf * lax.rsqrt(jnp.mean(xf * xf, axis=-1, keepdims=True) + EPS)
    return (y * w.astype(jnp.float32)).astype(x.dtype)

def modulate(h, shift, scale):
    return h * (1 + scale[:, None, :]) + shift[:, None, :]

def causal_conv(x, w, b):
    y = lax.conv_general_dilated(x, w[:, None, :].astype(x.dtype), window_strides=(1,),
                                 padding=((w.shape[0] - 1, 0),),
                                 dimension_numbers=('NWC', 'WIO', 'NWC'),
                                 feature_group_count=x.shape[-1])
    return y + b.astype(x.dtype)

def segsum_exp(a):
    q = a.shape[-1]
    x = jnp.broadcast_to(a[..., None], a.shape + (q,))
    x = jnp.where(jnp.tril(jnp.ones((q, q), bool), -1), x, 0.0)
    s = jnp.cumsum(x, axis=-2)
    lower = jnp.tril(jnp.ones((q, q), bool))
    return jnp.where(lower, jnp.exp(jnp.where(lower, s, 0.0)), 0.0)

def ssd_mixer(z, xbc, dt_raw, conv_w, conv_b, dt_bias, a_log, d_skip, norm_w):
    bsz, t_len, _ = z.shape
    nc = t_len // SSD_CHUNK
    xbc = jax.nn.silu(causal_conv(xbc, conv_w, conv_b))
    xs, b_in, c_in = jnp.split(xbc, [SSD_INNER, SSD_INNER + SSD_GROUPS * SSD_STATE], axis=-1)
    dt = jax.nn.softplus(dt_raw + dt_bias.astype(jnp.float32))
    a_head = -jnp.exp(a_log.astype(jnp.float32))
    xh = xs.reshape(bsz, t_len, SSD_HEADS, SSD_HEADDIM)
    xdt = (xh * dt[..., None]).reshape(bsz, nc, SSD_CHUNK, SSD_GROUPS, SSD_HPG, SSD_HEADDIM)
    bc = b_in.reshape(bsz, nc, SSD_CHUNK, SSD_GROUPS, SSD_STATE)
    cc = c_in.reshape(bsz, nc, SSD_CHUNK, SSD_GROUPS, SSD_STATE)
    a = (dt * a_head).reshape(bsz, nc, SSD_CHUNK, SSD_GROUPS, SSD_HPG).transpose(0, 3, 4, 1, 2)
    a_cum = jnp.cumsum(a, axis=-1)
    decay_in = segsum_exp(a)
    cb = jnp.einsum('bclgn,bcsgn->bgcls', cc, bc)
    y_diag = jnp.einsum('bgrcls,bcsgrp->bclgrp', cb[:, :, None] * decay_in, xdt)
    decay_states = jnp.exp(a_cum[..., -1:] - a_cum)
    states = jnp.einsum('bclgn,bgrcl,bclgrp->bcgrpn', bc, decay_states, xdt)
    chunk_decay = jnp.pad(a_cum[..., -1], ((0, 0), (0, 0), (0, 0), (1, 0)))
    decay_chunk = segsum_exp(chunk_decay)
    states = jnp.concatenate([jnp.zeros_like(states[:, :1]), states], axis=1)
    states = jnp.einsum('bgrzc,bcgrpn->bzgrpn', decay_chunk, states)[:, :-1]
    y_off = jnp.einsum('bclgn,bcgrpn,bgrcl->bclgrp', cc, states, jnp.exp(a_cum))
    y = (y_diag + y_off).reshape(bsz, t_len, SSD_HEADS, SSD_HEADDIM) + xh * d_skip.astype(jnp.float32)[:, None]
    y = y.reshape(bsz, t_len, SSD_INNER) * jax.nn.silu(z)
    y = rms_norm(y.reshape(bsz, t_len, SSD_GROUPS, SSD_INNER // SSD_GROUPS),
                 norm_w.reshape(SSD_GROUPS, SSD_INNER // SSD_GROUPS))
    return y.reshape(bsz, t_len, SSD_INNER)

def hgrn2_mixer(q, f, v, g, lb, norm_w):
    bsz, t_len, _ = q.shape
    nc = t_len // HG_CHUNK
    q = jax.nn.silu(q)
    lb = lb.astype(jnp.float32)
    k = (1.0 - lb) * jax.nn.sigmoid(-f)
    log_f = jnp.log1p(-k)

    def to_chunks(t):
        return t.reshape(bsz, nc, HG_CHUNK, HG_HEADS, HG_EXPAND).transpose(1, 0, 3, 2, 4)

    causal = jnp.tril(jnp.ones((HG_CHUNK, HG_CHUNK), bool))[:, :, None]

    def step(state, inp):
        qc, kc, vc, lc = inp
        b = jnp.cumsum(lc, axis=2)
        o_inter = jnp.einsum('bhtk,bhkv->bhtv', qc * jnp.exp(b), state)
        diff = b[:, :, :, None, :] - b[:, :, None, :, :]
        decay = jnp.where(causal, jnp.exp(jnp.where(causal, diff, 0.0)), 0.0)
        attn = jnp.einsum('bhtsk,bhsk->bhts', decay * qc[:, :, :, None, :], kc)
        o = o_inter + jnp.einsum('bhts,bhsv->bhtv', attn, vc)
        b_last = b[:, :, -1:, :]
        state = jnp.exp(b_last[:, :, 0, :, None]) * state + jnp.einsum('bhsk,bhsv->bhkv', kc * jnp.exp(b_last - b), vc)
        return state, o

    s0 = jnp.zeros((bsz, HG_HEADS, HG_EXPAND, HG_EXPAND), jnp.float32)
    _, o = lax.scan(step, s0, (to_chunks(q), to_chunks(k), to_chunks(v), to_chunks(log_f)))
    o = o.transpose(1, 0, 3, 2, 4).reshape(bsz, t_len, HG_HEADS, HG_EXPAND)
    o = rms_norm(o, norm_w.reshape(HG_HEADS, HG_EXPAND)).reshape(bsz, t_len, HG_WIDTH)
    return o * jax.nn.silu(g)

def rglru_mixer(gate, xb, conv_w, conv_b, wa, ba, wx, bx, lam, norm_w):
    bsz, t_len, _ = xb.shape
    xb = causal_conv(xb, conv_w, conv_b)
    xblk = xb.reshape(bsz, t_len, LRU_BLOCKS, LRU_BLOCK_W)
    r = jax.nn.sigmoid(jnp.einsum('btgi,gij->btgj', xblk, wa).reshape(bsz, t_len, LRU_WIDTH) + ba)
    i = jax.nn.sigmoid(jnp.einsum('btgi,gij->btgj', xblk, wx).reshape(bsz, t_len, LRU_WIDTH) + bx)
    log_a = -LRU_C * r * jax.nn.softplus(-lam.astype(jnp.float32))
    a = jnp.exp(log_a)
    u = jnp.sqrt(-jnp.expm1(2.0 * log_a)) * (i * xb)

    def combine(lhs, rhs):
        a1, b1 = lhs
        a2, b2 = rhs
        return a1 * a2, a2 * b1 + b2

    _, h = lax.associative_scan(combine, (a, u), axis=1)
    y = h * jax.nn.gelu(gate)
    return rms_norm(y, norm_w)

def hybrid_mixer(h, w_in, ssd_conv_w, ssd_conv_b, ssd_dt_bias, ssd_a_log, ssd_d, ssd_norm_w,
                 hg_lb, hg_norm_w, lru_conv_w, lru_conv_b, lru_wa, lru_ba, lru_wx, lru_bx,
                 lru_lambda, lru_norm_w, w_out):
    u = (h @ w_in).astype(jnp.float32)
    z, xbc, dt_raw, hq, hf, hv, hg, lgate, lx = jnp.split(u, IN_SPLITS, axis=-1)
    y_ssd = ssd_mixer(z, xbc, dt_raw, ssd_conv_w, ssd_conv_b, ssd_dt_bias, ssd_a_log, ssd_d, ssd_norm_w)
    y_hg = hgrn2_mixer(hq, hf, hv, hg, hg_lb, hg_norm_w)
    y_lru = rglru_mixer(lgate, lx, lru_conv_w, lru_conv_b, lru_wa, lru_ba, lru_wx, lru_bx, lru_lambda, lru_norm_w)
    y = jnp.concatenate([y_ssd, y_hg, y_lru], axis=-1).astype(h.dtype)
    return y @ w_out

def swiglu(x, wg, wu, wd):
    return (jax.nn.silu(x @ wg) * (x @ wu)) @ wd

def moe_ffn(h, router_w, router_bias, exp_gate, exp_up, exp_down, sh_gate, sh_up, sh_down):
    bsz, t_len, d = h.shape
    tokens = h.reshape(-1, d)
    n_tok = tokens.shape[0]
    scores = jax.nn.sigmoid((tokens @ router_w).astype(jnp.float32))
    sel = scores + router_bias.astype(jnp.float32)
    grp_score = lax.top_k(sel.reshape(n_tok, N_EXPERT_GROUPS, E_PER_GROUP), 2)[0].sum(-1)
    _, top_g = lax.top_k(grp_score, TOPK_GROUPS)
    group_mask = jnp.any(top_g[:, :, None] == jnp.arange(N_EXPERT_GROUPS)[None, None, :], axis=1)
    expert_mask = jnp.repeat(group_mask, E_PER_GROUP, axis=1)
    _, idx = lax.top_k(jnp.where(expert_mask, sel, MASK_SCORE), TOP_K)
    w = jnp.take_along_axis(scores, idx, axis=1)
    w = w / jnp.sum(w, axis=-1, keepdims=True) * ROUTED_SCALE
    n_assign = n_tok * TOP_K
    flat_e = idx.reshape(-1).astype(jnp.int32)
    flat_w = w.reshape(-1)
    flat_tok = jnp.arange(n_assign, dtype=jnp.int32) // TOP_K
    order = jnp.argsort(flat_e)
    sorted_e = flat_e[order]
    counts = jnp.bincount(flat_e, length=N_EXPERTS)
    padded = (counts + MOE_BLOCK - 1) // MOE_BLOCK * MOE_BLOCK
    pad_end = jnp.cumsum(padded)
    pad_start = pad_end - padded
    start = jnp.cumsum(counts) - counts
    dest = pad_start[sorted_e] + jnp.arange(n_assign, dtype=jnp.int32) - start[sorted_e]
    n_slots = n_assign + N_EXPERTS * MOE_BLOCK
    n_blocks = n_slots // MOE_BLOCK
    slot_tok = jnp.full((n_slots,), n_tok, jnp.int32).at[dest].set(flat_tok[order])
    slot_w = jnp.zeros((n_slots,), tokens.dtype).at[dest].set(flat_w[order].astype(tokens.dtype))
    block_e = jnp.minimum(jnp.searchsorted(pad_end, jnp.arange(n_blocks) * MOE_BLOCK, side='right'),
                          N_EXPERTS - 1).astype(jnp.int32)
    tok_pad = jnp.concatenate([tokens, jnp.zeros((1, d), tokens.dtype)], axis=0)

    def run_block(args):
        t_idx, e, wt = args
        xb = tok_pad[t_idx]
        return swiglu(xb, exp_gate[e], exp_up[e], exp_down[e]) * wt[:, None]

    y_slots = lax.map(run_block, (slot_tok.reshape(n_blocks, MOE_BLOCK), block_e,
                                  slot_w.reshape(n_blocks, MOE_BLOCK)))
    routed = jax.ops.segment_sum(y_slots.reshape(n_slots, d), slot_tok, num_segments=n_tok + 1)[:n_tok]
    shared = swiglu(tokens, sh_gate, sh_up, sh_down)
    return (routed + shared).reshape(bsz, t_len, d)

def setup_inputs(seed: int = 0) -> dict:
    key = jax.random.key(seed)
    ks = iter(jax.random.split(key, 48))
    f32 = jnp.float32
    L = DEPTH

    def nrm(shape, scale):
        return jax.random.normal(next(ks), shape, f32) * scale

    def gain(shape):
        return 1.0 + nrm(shape, 0.02)

    dt = jnp.exp(jax.random.uniform(next(ks), (L, SSD_HEADS), f32, math.log(1e-3), math.log(1e-1)))
    a_c = jax.random.uniform(next(ks), (L, LRU_WIDTH), f32, 0.9, 0.999)
    sig = a_c ** (1.0 / LRU_C)
    return {
        'x': nrm((BATCH, SEQ, D_MODEL), 1.0),
        'c': nrm((BATCH, D_MODEL), 1.0),
        'ada_w': nrm((L, D_MODEL, N_ADA * D_MODEL), 0.5 * D_MODEL ** -0.5),
        'ada_b': nrm((L, N_ADA * D_MODEL), 0.02),
        'norm_mix_w': gain((L, D_MODEL)),
        'norm_ffn_w': gain((L, D_MODEL)),
        'w_in': nrm((L, D_MODEL, D_IN), D_MODEL ** -0.5),
        'ssd_conv_w': nrm((L, CONV_WIDTH, SSD_CONV_DIM), CONV_WIDTH ** -0.5),
        'ssd_conv_b': nrm((L, SSD_CONV_DIM), 0.02),
        'ssd_dt_bias': dt + jnp.log(-jnp.expm1(-dt)),
        'ssd_a_log': jnp.log(jax.random.uniform(next(ks), (L, SSD_HEADS), f32, 1.0, 16.0)),
        'ssd_d': gain((L, SSD_HEADS)),
        'ssd_norm_w': gain((L, SSD_INNER)),
        'hg_lower_bounds': nrm((L, HG_WIDTH), 0.5),
        'hg_norm_w': gain((L, HG_WIDTH)),
        'lru_conv_w': nrm((L, CONV_WIDTH, LRU_WIDTH), CONV_WIDTH ** -0.5),
        'lru_conv_b': nrm((L, LRU_WIDTH), 0.02),
        'lru_wa': nrm((L, LRU_BLOCKS, LRU_BLOCK_W, LRU_BLOCK_W), LRU_BLOCK_W ** -0.5),
        'lru_ba': nrm((L, LRU_WIDTH), 0.02),
        'lru_wx': nrm((L, LRU_BLOCKS, LRU_BLOCK_W, LRU_BLOCK_W), LRU_BLOCK_W ** -0.5),
        'lru_bx': nrm((L, LRU_WIDTH), 0.02),
        'lru_lambda': jnp.log(sig) - jnp.log1p(-sig),
        'lru_norm_w': gain((L, LRU_WIDTH)),
        'w_out': nrm((L, D_MIX, D_MODEL), D_MIX ** -0.5),
        'router_w': nrm((L, D_MODEL, N_EXPERTS), D_MODEL ** -0.5),
        'router_bias': nrm((L, N_EXPERTS), 0.01),
        'exp_gate': nrm((L, N_EXPERTS, D_MODEL, D_EXPERT), D_MODEL ** -0.5),
        'exp_up': nrm((L, N_EXPERTS, D_MODEL, D_EXPERT), D_MODEL ** -0.5),
        'exp_down': nrm((L, N_EXPERTS, D_EXPERT, D_MODEL), D_EXPERT ** -0.5),
        'sh_gate': nrm((L, D_MODEL, D_SHARED), D_MODEL ** -0.5),
        'sh_up': nrm((L, D_MODEL, D_SHARED), D_MODEL ** -0.5),
        'sh_down': nrm((L, D_SHARED, D_MODEL), D_SHARED ** -0.5),
        'final_norm_w': gain((D_MODEL,)),
    }

def reference(x, c, ada_w, ada_b, norm_mix_w, norm_ffn_w, w_in, ssd_conv_w, ssd_conv_b,
              ssd_dt_bias, ssd_a_log, ssd_d, ssd_norm_w, hg_lower_bounds, hg_norm_w,
              lru_conv_w, lru_conv_b, lru_wa, lru_ba, lru_wx, lru_bx, lru_lambda, lru_norm_w,
              w_out, router_w, router_bias, exp_gate, exp_up, exp_down, sh_gate, sh_up,
              sh_down, final_norm_w):
    lb_soft = jax.nn.softmax(hg_lower_bounds.astype(jnp.float32), axis=0)
    lower_bounds = jnp.cumsum(lb_soft, axis=0) - lb_soft[0]
    c_act = jax.nn.silu(c)
    for l in range(DEPTH):
        mod = c_act @ ada_w[l] + ada_b[l]
        sh_m, sc_m, g_m, sh_f, sc_f, g_f = jnp.split(mod, N_ADA, axis=-1)
        h = modulate(rms_norm(x, norm_mix_w[l]), sh_m, sc_m)
        mix = hybrid_mixer(h, w_in[l], ssd_conv_w[l], ssd_conv_b[l], ssd_dt_bias[l], ssd_a_log[l],
                           ssd_d[l], ssd_norm_w[l], lower_bounds[l], hg_norm_w[l], lru_conv_w[l],
                           lru_conv_b[l], lru_wa[l], lru_ba[l], lru_wx[l], lru_bx[l], lru_lambda[l],
                           lru_norm_w[l], w_out[l])
        x = x + g_m[:, None, :] * mix
        h = modulate(rms_norm(x, norm_ffn_w[l]), sh_f, sc_f)
        ffn = moe_ffn(h, router_w[l], router_bias[l], exp_gate[l], exp_up[l], exp_down[l],
                      sh_gate[l], sh_up[l], sh_down[l])
        x = x + g_f[:, None, :] * ffn
    return rms_norm(x, final_norm_w)


_drawn_inputs = setup_inputs


def setup_inputs(seed=0):
    import zlib

    import numpy as np

    out = dict(_drawn_inputs(seed))
    spreads = {}
    factors = {'ssd_d': 3.296,
     'ssd_norm_w': 2.897,
     'hg_lower_bounds': 5.476,
     'hg_norm_w': 3.184,
     'lru_ba': 8.0,
     'lru_bx': 8.0,
     'lru_norm_w': 2.767,
     'final_norm_w': 2.724}
    for name, (base, spread) in spreads.items():
        noise = np.random.default_rng([zlib.crc32(name.encode()), seed]).standard_normal(out[name].shape)
        drawn = base * np.exp(spread * noise) if base else spread * noise
        out[name] = jnp.asarray(drawn.astype(out[name].dtype))
    for name, factor in factors.items():
        out[name] = (out[name] * factor).astype(out[name].dtype)
    return out
```

```python
import concourse.bass as bass
from concourse import mybir
from contextlib import ExitStack

fp32 = mybir.dt.float32
fp32r = mybir.dt.float32r
uint32 = mybir.dt.uint32
ALU = mybir.AluOpType
ACT = mybir.ActivationFunctionType
AXL = mybir.AxisListType

P = 128
L, T, D = 2, 256, 1024
TT = T // P
KD = D // P
EPS = 1e-6
SSD_IN, SSD_HEADS, SSD_HD, SSD_N = 1024, 16, 64, 128
CH_XBC = (SSD_IN + 4 * SSD_N) // P
HG_H = 4
LRU_J = 4
D_IN = 5648
C_Z, C_XBC, C_DT = 0, SSD_IN, SSD_IN + CH_XBC * P
C_HQ = C_DT + SSD_HEADS
C_HF, C_HV, C_HG, C_LG, C_LX = (C_HQ + 512 * i for i in range(1, 6))
KY = 16
E, DE = 64, 256
SCALE = 2.5
NEG = -1.0e30

RING = 9
W_COLS = ([C_XBC + 256 * i for i in range(6)] + [C_DT] + [C_HF, C_HF + 256, C_HQ, C_HQ + 256]
          + [C_Z + 256 * i for i in range(4)] + [C_LX, C_LX + 256, C_HV, C_HV + 256, C_LG, C_LG + 256,
                                                 C_HG, C_HG + 256])
N_W = len(W_COLS)
U_ADA_MIX = 0
U_W = U_ADA_MIX + 12
U_ADA_FFN = U_W + N_W
U_OUT = U_ADA_FFN + 12
U_MOE = U_OUT + 8 + 2
UNITS = U_MOE + 3 * (E + 1)
PADS = (U_OUT + 8, U_OUT + 9)
assert UNITS % RING == 0
(W_XBC, W_DT, W_HF, W_HQ, W_Z, W_LX, W_HV, W_LG, W_HG) = 0, 6, 7, 9, 11, 15, 17, 19, 21
DVE_UNITS = list(range(W_XBC, W_DT + 1)) + [W_LX, W_LX + 1]
W_BANKS = 3

R_CW, R_CB, R_LCW, R_LCB, R_BA, R_BX, R_LAM, R_LNW, R_HNW, R_SNW, R_LB, R_END = (
    0, 48, 60, 76, 80, 84, 88, 92, 96, 100, 108, 116)
LEVELS = 8


N_PE = U_OUT + 8
N_X = E + 1
X_IT = 3


def slot_of(u):
    return u % RING


def weight_of(u):
    return 0 if u in PADS else 32 if u >= U_MOE and (u - U_MOE) % 3 < 2 else 16


def filled(u):
    return sum(weight_of(q) for q in range(slot_of(u), u + 1, RING))


def per_layer(s):
    return sum(weight_of(q) for q in range(s, UNITS, RING))


def build(nc, a, out):
    ctx = ExitStack()
    with ctx:
        def sem(name):
            return ctx.enter_context(nc.semaphore(name))

        def sb(name, shape, dt=fp32, stack=ctx):
            return stack.enter_context(nc.sbuf_tensor(name, [P] + shape, dt))

        def bcast(ap, axis, n):
            shape = list(ap.shape)
            shape.insert(axis, n)
            return ap.unsqueeze(axis).broadcast_to(shape)

        ring = sb("ring", [RING, 2048])
        x = sb("x", [TT, D])
        ident = sb("ident", [P])
        tri = sb("tri", [P])
        neg = sb("neg", [P])
        ones = sb("ones", [P])
        lt8 = sb("lt8", [64])
        masks = sb("masks", [LEVELS, P], uint32)
        cact = sb("cact", [KD])
        craw = sb("craw", [KD])
        prow = sb("prow", [P])
        pcol = sb("pcol", [R_END])
        colp = sb("colp", [6, KD])
        hb = sb("hb", [3, SSD_HEADS])
        rbias = sb("rbias", [E])
        gates = sb("gates", [2, D])
        modc = sb("modc", [2, 2, KD])
        lbs = sb("lbs", [L, HG_H])
        lbt = sb("lbt", [4, HG_H])
        omlb = sb("omlb", [HG_H])
        lruc = sb("lruc", [4, LRU_J])
        ss = sb("ss", [4])
        rstd = sb("rstd", [2])
        eps = sb("eps", [1])

        mix = ExitStack()
        hT = sb("hT", [KD, T], stack=mix)
        yT = sb("yT", [KY, T], stack=mix)
        z = sb("z", [TT, SSD_IN], stack=mix)
        xbcT = sb("xbcT", [CH_XBC, T], stack=mix)
        xh = sb("xh", [TT, SSD_IN], stack=mix)
        xdt = sb("xdt", [TT, SSD_IN], stack=mix)
        y = sb("y", [TT, SSD_IN], stack=mix)
        xdec = sb("xdec", [SSD_IN], stack=mix)
        mdec = sb("mdec", [2, 4, P], stack=mix)
        cb = sb("cb", [4, P], stack=mix)
        btok = sb("btok", [2, P], stack=mix)
        stT = sb("stT", [2, 512], stack=mix)
        dts = sb("dts", [6, 32], stack=mix)
        qkg = sb("qkg", [3, HG_H, T], stack=mix)
        v = sb("v", [TT, 512], stack=mix)
        bd = sb("bd", [2, LRU_J, P], stack=mix)
        xn = z
        bT = xdec[:, :].rearrange("p (h t) -> p h t", h=HG_H)
        lev_e, lev_q, lev_k = ([buf[:, i, :].rearrange("p (h t) -> p h t", h=HG_H) for i in range(2)]
                               for buf in (xh, xdt, y))
        attn = z[:, 0, :].rearrange("p (g t) -> p g t", g=8)
        cross = z[:, 1, 0:512].rearrange("p (h t) -> p h t", h=HG_H)
        lru_x = stT[:, :, :].rearrange("p g (j t) -> p (g j) t", t=T)
        lru_g = mdec[:, :, :, :].rearrange("p i j c -> p (i j c)").rearrange("p (j t) -> p j t", t=T)
        lru_r, lru_i, lru_v = (xbcT[:, 4 * i:4 * i + 4, :] for i in range(3))
        lru_a, lru_u = hT[:, 0:4, :], hT[:, 4:8, :]
        tmp = sb("tmp", [512], stack=mix)
        sqj = yT[:, :, :].rearrange("p (i k) t -> p i (k t)", k=4)
        mix.close()
        moe = ExitStack()
        xhi = sb("xhi", [KD, T], fp32r, moe)
        xlo = sb("xlo", [KD, T], fp32r, moe)
        h2T = sb("h2T", [KD, T], stack=moe)
        xn2 = sb("xn2", [TT, D], stack=moe)
        whi = [sb(f"whi{i}", [2048], fp32r, moe) for i in range(3)]
        wlo = [sb(f"wlo{i}", [2048], fp32r, moe) for i in range(3)]
        hTh = sb("hTh", [2, T], fp32r, moe)
        hTl = sb("hTl", [2, T], fp32r, moe)
        sg = sb("sg", [TT, DE], stack=moe)
        h = sb("h", [TT, DE], stack=moe)
        rw = sb("rw", [KD, E], stack=moe)
        sc = sb("sc", [TT, E], stack=moe)
        sel = sb("sel", [TT, E], stack=moe)
        rep = sb("rep", [TT, E], stack=moe)
        wts = sb("wts", [TT, E + 1], stack=moe)
        m8 = sb("m8", [TT, 8, 8], stack=moe)
        gsc = sb("gsc", [TT, 8], stack=moe)
        cmp_ = sb("cmp", [2, TT * 64], stack=moe)
        gm = sb("gm", [2, TT, 8], stack=moe)
        t8 = sb("t8", [TT, 8], stack=moe)
        wsum = sb("wsum", [2, TT], stack=moe)
        tmp2 = sb("tmp2", [512], stack=moe)
        moe.close()
        fin = ExitStack()
        fnw = sb("fnw", [D], stack=fin)
        xo = sb("xo", [TT, D], stack=fin)
        fin.close()

        pb = [ctx.enter_context(nc.psum_tensor(f"pb{i}", [P, 512], fp32)) for i in range(8)]

        full = [sem(f"slot_full{i}") for i in range(RING)]
        pe_unit = sem("pe_unit")
        x_lo = [sem(f"x_lo{j}") for j in range(3)]
        slots_taken = sem("slots_taken")
        layer_done = sem("layer_done")
        const_in = sem("const_in")
        silu_c = sem("silu_c")
        out_sem = sem("out_stored")
        eps_ready = sem("eps_ready")
        fin_sq = sem("fin_sq")
        fin_in = sem("fin_in")
        fin_dve = sem("fin_dve")

        S = {n: sem(n) for n in SIGNALS}

        def ring_unit(u):
            return ring[:, slot_of(u), :]

        def wait_unit(eng, l, u, it=0):
            eng.wait_ge(full[slot_of(u)], l * per_layer(slot_of(u)) + filled(u) + it * weight_of(u))

        def wait_pe_unit(eng, l, u):
            eng.wait_ge(pe_unit, l * N_PE + u + 1)

        def wait_split(eng, l, j, n):
            eng.wait_ge(x_lo[j], l * N_X + (N_X + 1) + n)

        block = ctx.enter_context(nc.Block())

        @block.sync
        def _(sp):
            ada = a["ada_w"].rearrange("l (p k) (g c) -> l g p k c", p=P, g=6)
            w_in = a["w_in"].rearrange("l (p k) n -> l p k n", p=P)
            w_out = a["w_out"].rearrange("l (k p) n -> l p k n", p=P)
            gate_w, up_w = (a[n].rearrange("l e (p k) n -> (l e) p (k n)", p=P) for n in ("exp_gate", "exp_up"))
            down_w = a["exp_down"].rearrange("l e (k p) n -> (l e) p k n", p=P)
            sh_g, sh_u = (a[n].rearrange("l (p k) n -> l p (k n)", p=P) for n in ("sh_gate", "sh_up"))
            sh_d = a["sh_down"].rearrange("l (k p) n -> l p k n", p=P)

            def slot_free(l, u, it=0):
                q = u - RING
                while q in PADS:
                    q -= RING
                before = l
                if q < 0:
                    q, before = q + UNITS, l - 1
                if not isinstance(it, int):
                    n, j = divmod(u - U_MOE, 3)
                    wait_split(sp, l, j, X_IT * it + (n - X_IT))
                elif q < N_PE:
                    wait_pe_unit(sp, l, q)
                else:
                    n, j = divmod(q - U_MOE, 3)
                    wait_split(sp, before, j, n)
                sp.sem_inc(slots_taken, 1)

            def pair_unit(l, u, src):
                slot_free(l, u)
                sp.dma_start(ring_unit(u).rearrange("p (k c) -> p k c", k=2), src).then_inc(full[slot_of(u)], 16)

            def expert_units(l, n, it, g, up, down):
                u = U_MOE + 3 * n
                for half in range(2):
                    slot_free(l, u + half, it)
                    dst, c = ring_unit(u + half), 1024 * half
                    sp.dma_start(dst[:, 0:1024], g[:, c:c + 1024]).then_inc(full[slot_of(u + half)], 16)
                    sp.dma_start(dst[:, 1024:2048], up[:, c:c + 1024]).then_inc(full[slot_of(u + half)], 16)
                slot_free(l, u + 2, it)
                sp.dma_start(ring_unit(u + 2).rearrange("p (k c) -> p k c", k=2),
                             down).then_inc(full[slot_of(u + 2)], 16)

            def routed(l, n, it=0):
                e = l * E + X_IT * it + (n - 1)
                expert_units(l, n, it, gate_w[e], up_w[e], down_w[e])

            for j in range(3):
                sp.sem_inc(x_lo[j], N_X)
            with sp.Fori(0, L) as l:
                for q in range(12):
                    pair_unit(l, U_ADA_MIX + q, ada[l, q // 4, :, 2 * (q % 4):2 * (q % 4) + 2, :])
                for i, c in enumerate(W_COLS):
                    n = SSD_HEADS if c == C_DT else 256
                    slot_free(l, U_W + i)
                    sp.dma_start(ring_unit(U_W + i)[:, 0:KD * n].rearrange("p (k c) -> p k c", k=KD),
                                 w_in[l, :, :, c:c + n]).then_inc(full[slot_of(U_W + i)], 16)
                for q in range(12):
                    pair_unit(l, U_ADA_FFN + q, ada[l, 3 + q // 4, :, 2 * (q % 4):2 * (q % 4) + 2, :])
                for i in range(8):
                    pair_unit(l, U_OUT + i, w_out[l, :, 2 * i:2 * i + 2, :])
                expert_units(l, 0, 0, sh_g[l], sh_u[l], sh_d[l])
                for n in range(1, X_IT + 1):
                    routed(l, n)
                with sp.Fori(1, E // X_IT) as it:
                    for n in range(1, X_IT + 1):
                        routed(l, n, it)
                routed(l, E)
            sp.wait_ge(fin_dve, 5)
            sp.dma_start(out.rearrange("b (t p) d -> p (b t) d", p=P), xo[:, :, :]).then_inc(out_sem, 16)
            sp.wait_ge(out_sem, 16)

        @block.scalar
        def _(act):
            A = nc.scalar.activation
            for i, t in enumerate((ident, tri, neg, ones)):
                act.dma_start(t[:, :], a["consts"][:, P * i:P * i + P]).then_inc(const_in, 16)
            act.dma_start(lt8[:, :], a["consts"][:, 4 * P:4 * P + 64]).then_inc(const_in, 16)
            act.dma_start(masks[:, :, :], a["masks"].rearrange("p (l t) -> p l t", l=LEVELS)).then_inc(const_in, 16)
            act.dma_start(craw[:, :], a["c"].rearrange("b (p k) -> (b p) k", p=P)).then_inc(const_in, 16)
            act.dma_start(x[:, :, :], a["x"].rearrange("b (t p) d -> p (b t) d", p=P)).then_inc(const_in, 16)
            act.wait_ge(const_in, 16 * 8)
            A(cact[:, :], craw[:, :], ACT.Silu).then_inc(silu_c, 1)

            def small_params(l):
                rows = [(R_CW, 48, a["ssd_conv_w"][l].rearrange("w (c p) -> (w c) p", p=P)),
                        (R_CB, 12, a["ssd_conv_b"][l].rearrange("(c p) -> c p", p=P)),
                        (R_LCW, 16, a["lru_conv_w"][l].rearrange("w (c p) -> (w c) p", p=P))]
                rows += [(r, n, a[k][l].rearrange("(c p) -> c p", p=P)) for r, n, k in (
                    (R_LCB, 4, "lru_conv_b"), (R_BA, 4, "lru_ba"), (R_BX, 4, "lru_bx"), (R_LAM, 4, "lru_lambda"),
                    (R_LNW, 4, "lru_norm_w"), (R_HNW, 4, "hg_norm_w"), (R_SNW, 8, "ssd_norm_w"))]
                rows.append((R_LB, 4 * L, a["hg_lower_bounds"].rearrange("l (c p) -> (l c) p", p=P)))
                for r, n, src in rows:
                    act.dma_start(prow[r:r + n, :], src).then_inc(S["rows_in"], 16)
                ab = a["ada_b"].rearrange("l (g p k) -> l g p k", g=6, p=P)
                for i, src in enumerate((a["norm_mix_w"][l].rearrange("(p k) -> p k", p=P),
                                         a["norm_ffn_w"][l].rearrange("(p k) -> p k", p=P),
                                         ab[l, 0], ab[l, 1], ab[l, 3], ab[l, 4])):
                    act.dma_start(colp[:, i, :], src).then_inc(S["cols_in"], 16)
                for i in range(2):
                    act.dma_start(gates[:, i, :], a["ada_b"][l, (3 * i + 2) * D:(3 * i + 3) * D]
                                  .partition_broadcast(P)).then_inc(S["cols_in"], 16)
                for i, k in enumerate(("ssd_dt_bias", "ssd_a_log", "ssd_d")):
                    act.dma_start(hb[:, i, :], a[k][l].partition_broadcast(P)).then_inc(S["cols_in"], 16)
                act.dma_start(rbias[:, :], a["router_bias"][l].partition_broadcast(P)).then_inc(S["cols_in"], 16)
                act.wait_ge(S["bd_zero"], 1)
                for i, k in enumerate(("lru_wa", "lru_wx")):
                    w = a[k][l].rearrange("(j b) i o -> b i j o", b=2)
                    for b in range(2):
                        act.dma_start(bd[64 * b:64 * b + 64, i, :, 64 * b:64 * b + 64], w[b]).then_inc(S["bd_in"], 16)

            def rms(src, done, root):
                for t in range(TT):
                    A(sqj[:, t, :], src[:, t, :], ACT.Square, accum_out=ss[:, t:t + 1]).then_inc(done, 1)
                act.wait_ge(done, TT)
                A(ss[:, 2:4], ss[:, 0:2], ACT.Sqrt, scale=1.0 / D, bias=eps[:, :]).then_inc(root, 1)

            def split_hi(l, j, n, n0, it):
                u = U_MOE + 3 * n0 + j
                wait_unit(act, l, u, it)
                if not (isinstance(n, int) and n == 0):
                    act.wait_ge(S[f"x_used{j}"], n)
                A(whi[j][:, :], ring_unit(u), ACT.Copy).then_inc(S[f"x_hi{j}"], 1)

            def silu_gate(n):
                act.wait_ge(S["x_used1"], n + 1)
                for t in range(TT):
                    A(sg[:, t, :], pb[4 + t][:, 0:DE], ACT.Silu).then_inc(S["silu_g"], 1)

            def hidden_hi(n):
                act.wait_ge(S["h_turned"], n + 1)
                A(hTh[:, :, :], pb[6][:, :].rearrange("p (k t) -> p k t", k=2), ACT.Copy).then_inc(S["h_hi"], 1)

            act.wait_ge(eps_ready, 1)
            with act.Fori(0, L) as l:
                small_params(l)
                rms(x, S["ss_mix"], S["root_mix"])
                def from_unit(i, dst, func, **kw):
                    wait_pe_unit(act, l, U_W + i)
                    return A(dst, pb[i % W_BANKS][:, :], func, **kw)

                for i in range(6):
                    act.wait_ge(S["conv"], 2 * i + 2)
                    A(xbcT[:, 2 * i:2 * i + 2, :], xbcT[:, 2 * i:2 * i + 2, :], ACT.Silu).then_inc(S["xbc_ready"], 1)
                act.wait_ge(S["dt_in"], 2)
                A(dts[:, 1, :], dts[:, 1, :], ACT.Exp).then_inc(S["dt_exp"], 1)
                act.wait_ge(S["cols_in"], 16 * 12)
                A(hb[:, 1, :], hb[:, 1, :], ACT.Exp).then_inc(S["dt_exp"], 1)
                act.wait_ge(S["lb_in"], L)
                A(lbs[:, :, :], lbs[:, :, :], ACT.Exp).then_inc(S["lb_exp"], 1)
                act.wait_ge(S["lam_in"], 1)
                A(lruc[:, 1, :], lruc[:, 0, :], ACT.Exp).then_inc(S["lam_exp"], 1)
                act.wait_ge(S["dt_exp"], 2)
                A(dts[:, 1, :], dts[:, 1, :], ACT.Ln, bias=1.0).then_inc(S["dt_ln"], 1)
                act.wait_ge(S["lam_exp"], 1)
                A(lruc[:, 1, :], lruc[:, 1, :], ACT.Ln, bias=1.0).then_inc(S["lam_ln"], 1)
                for i in range(2):
                    from_unit(W_HF + i, qkg[:, 1, 2 * i:2 * i + 2, :], ACT.Sigmoid, scale=-1.0).then_inc(S["w_act"], 1)
                for i in range(2):
                    from_unit(W_HQ + i, qkg[:, 0, 2 * i:2 * i + 2, :], ACT.Silu).then_inc(S["w_act"], 1)
                act.wait_ge(S["dec_in"], 1)
                A(dts[:, 0, :], dts[:, 4, :], ACT.Exp).then_inc(S["eacum"], 1)
                A(dts[:, 5, :], dts[:, 5, :], ACT.Exp).then_inc(S["dec"], 1)
                act.wait_ge(S["cb_done"], 1)
                A(cb[:, :, :], pb[4][:, :], ACT.Copy).then_inc(S["cb_ready"], 1)
                act.wait_ge(S["btok_done"], 1)
                A(btok[:, :, :], pb[5][:, 0:2 * P], ACT.Copy).then_inc(S["btok_ready"], 1)
                for i in range(4):
                    act.wait_ge(S["xs_turned"], i + 1)
                    A(xh[:, i // 2, 512 * (i % 2):512 * (i % 2) + 512], pb[(6, 7, 4, 5)[i]][:, :],
                      ACT.Copy).then_inc(S["xh_ready"], 1)
                for i in range(4):
                    wait_pe_unit(act, l, U_W + W_Z + i)
                    A(z[:, :, 256 * i:256 * i + 256], pb[(W_Z + i) % W_BANKS][:, :].rearrange("p (t c) -> p t c", t=TT),
                      ACT.Silu).then_inc(S["w_act"], 1)
                for g in range(2):
                    act.wait_ge(S["st_done"], g + 1)
                    A(stT[:, g, :], pb[3][:, :], ACT.Copy).then_inc(S["st_ready"], 1)
                for q in range(8):
                    act.wait_ge(S["diff_sub"], q + 1)
                    A(mdec[:, q % 2, :, :], mdec[:, q % 2, :, :], ACT.Exp).then_inc(S["diff_exp"], 1)
                for i in range(2):
                    wait_pe_unit(act, l, U_W + W_HV + i)
                    A(v[:, :, 256 * i:256 * i + 256], pb[(W_HV + i) % W_BANKS][:, :].rearrange("p (t c) -> p t c", t=TT),
                      ACT.Copy).then_inc(S["w_act"], 1)
                for i in range(2):
                    from_unit(W_LG + i, lru_g[:, 2 * i:2 * i + 2, :], ACT.Gelu_apprx_tanh).then_inc(S["w_act"], 1)
                for i in range(2):
                    from_unit(W_HG + i, qkg[:, 2, 2 * i:2 * i + 2, :], ACT.Silu).then_inc(S["w_act"], 1)
                act.wait_ge(S["y_gated"], 2)
                for i in range(4):
                    half = slice(512 * (i % 2), 512 * (i % 2) + 512)
                    A(xh[:, i // 2, half], y[:, i // 2, half], ACT.Square,
                      accum_out=ss[:, i:i + 1]).then_inc(S["y_sq"], 1)
                act.wait_ge(S["y_sq"], 4)
                A(ss[:, :], ss[:, :], ACT.Sqrt, scale=1.0 / 512, bias=eps[:, :]).then_inc(S["y_root"], 1)
                act.wait_ge(S["k_ready"], 1)
                act.wait_ge(S["st_done"], 2)
                A(bT, qkg[:, 1, :, :], ACT.Ln, scale=-1.0, bias=1.0).then_inc(S["logf"], 1)
                for i in range(1, LEVELS + 1):
                    act.wait_ge(S["lev_in"], 2 * i)
                    A(lev_e[i % 2], lev_e[i % 2], ACT.Exp).then_inc(S["lev_exp"], 1)
                act.wait_ge(S["cross_done"], 1)
                A(cross, pb[3][:, :], ACT.Copy).then_inc(S["cross_ready"], 1)
                act.wait_ge(S["o_done"], 1)
                for i in range(2):
                    A(lev_e[0][:, 2 * i:2 * i + 2, :], pb[4 + i][:, :], ACT.Square).then_inc(S["o_sq"], 1)
                act.wait_ge(S["o_sum"], 1)
                for i in range(2):
                    A(lev_e[1][:, 2 * i:2 * i + 2, :], pb[6 + i][:, :], ACT.Sqrt, scale=1.0 / P,
                      bias=eps[:, :]).then_inc(S["o_root"], 1)
                act.wait_ge(S["gate_mm"], 1)
                for k, dst, r in ((0, lru_r, R_BA), (1, lru_i, R_BX)):
                    for j in range(LRU_J):
                        A(dst[:, j, :], pb[4 + 2 * k + j // 2][:, T * (j % 2):T * (j % 2) + T], ACT.Sigmoid,
                          bias=pcol[:, r + j:r + j + 1]).then_inc(S["gate_sig"], 1)
                act.wait_ge(S["gate_sig"], 8)
                act.wait_ge(S["lruc_ready"], 1)
                for j in range(LRU_J):
                    A(lru_v[:, j, :], lru_r[:, j, :], ACT.Tanh, scale=lruc[:, 2, j:j + 1]).then_inc(S["lru_tanh"], 1)
                for j in range(LRU_J):
                    A(lru_a[:, j, :], lru_r[:, j, :], ACT.Exp, scale=lruc[:, 3, j:j + 1]).then_inc(S["lru_exp"], 1)
                act.wait_ge(S["lru_w"], 1)
                A(lru_u, lru_u, ACT.Sqrt).then_inc(S["lru_sqrt"], 1)
                act.wait_ge(S["lru_y"], 1)
                A(lru_v, lru_r, ACT.Square).then_inc(S["lru_sq"], 1)
                act.wait_ge(S["lru_sum"], 1)
                A(tmp[:, 0:T], pb[3][:, 0:T], ACT.Sqrt, scale=1.0 / 512, bias=eps[:, :]).then_inc(S["lru_root"], 1)

                act.wait_ge(S["x_mid"], 4)
                act.dma_start(rw[:, :, :], a["router_w"][l].rearrange("(p k) e -> p k e", p=P)).then_inc(S["router_in"], 16)
                rms2 = S["ss_ffn"]
                for t in range(TT):
                    A(xn2[:, t, :], x[:, t, :], ACT.Square, accum_out=ss[:, t:t + 1]).then_inc(rms2, 1)
                act.wait_ge(rms2, TT)
                A(ss[:, 2:4], ss[:, 0:2], ACT.Sqrt, scale=1.0 / D, bias=eps[:, :]).then_inc(S["root_ffn"], 1)
                for j in range(4):
                    act.wait_ge(S["h2_ready"], 2 * j + 2)
                    A(xhi[:, 2 * j:2 * j + 2, :], h2T[:, 2 * j:2 * j + 2, :], ACT.Copy).then_inc(S["x_hi"], 1)
                act.wait_ge(S["logits"], 1)
                A(sc[:, :, :], pb[7][:, 0:TT * E], ACT.Sigmoid).then_inc(S["scores"], 1)
                split_hi(l, 0, 0, 0, 0)
                split_hi(l, 1, 0, 0, 0)
                split_hi(l, 0, 1, 1, 0)

                def expert_step(n, n0, it, last=False):
                    silu_gate(n - 1)
                    split_hi(l, 1, n, n0, it)
                    split_hi(l, 2, n - 1, n0 - 1, it)
                    hidden_hi(n - 1)
                    if not last:
                        split_hi(l, 0, n + 1, n0 + 1, it)

                expert_step(1, 1, 0)
                for r in range(1, X_IT):
                    expert_step(1 + r, 1 + r, 0)
                with act.Fori(1, E // X_IT) as it:
                    for r in range(X_IT):
                        expert_step(X_IT * it + 1 + r, 1 + r, it)
                expert_step(E, E, 0, last=True)
                silu_gate(E)
                split_hi(l, 2, E, E, 0)
                hidden_hi(E)
                act.sem_inc(S["end_act"], 1)
                act.wait_ge(layer_done, l + 1)

            act.dma_start(fnw[:, :], a["final_norm_w"].partition_broadcast(P)).then_inc(fin_in, 16)
            for t in range(TT):
                A(xo[:, t, :], x[:, t, :], ACT.Square, accum_out=ss[:, t:t + 1]).then_inc(fin_sq, 1)
            act.wait_ge(fin_sq, TT)
            A(ss[:, 2:4], ss[:, 0:2], ACT.Sqrt, scale=1.0 / D, bias=eps[:, :]).then_inc(fin_sq, 1)

        @block.vector
        def _(dve):
            V = nc.vector
            order = [0]

            def link(ins):
                order[0] += 1
                ins.then_inc(S["dve_order"], 1)
                dve.wait_ge(S["dve_order"], order[0])

            def own(ins, s, value):
                ins.then_inc(s, 1)
                dve.wait_ge(s, value)

            def normed(src, dst, root, ready):
                dve.wait_ge(root, 1)
                link(V.reciprocal(rstd[:, :], ss[:, 2:4]))
                for t in range(TT):
                    V.tensor_scalar(dst[:, t, :], src[:, t, :], rstd[:, t:t + 1], None, ALU.mult).then_inc(ready, 1)

            def modulation(i, bank):
                V.tensor_tensor(modc[:, i, 1, :], bank[:, 0:KD], colp[:, 2 + 2 * i, :], ALU.add).then_inc(S["modc_s"], 1)
                link(V.tensor_tensor(modc[:, i, 0, :], bank[:, KD:2 * KD], colp[:, 3 + 2 * i, :], ALU.add))
                own(V.scalar_tensor_tensor(modc[:, i, 0, :], modc[:, i, 0, :], 1.0, colp[:, i, :], ALU.add, ALU.mult),
                    S["modc"], i + 1)
                dve.wait_ge(S["modc_s"], i + 1)

            def conv(i, dst, w_row, chunks, b_row, done):
                for s in range(4):
                    for c in range(2):
                        ch = chunks + c
                        src = pb[i % W_BANKS][:, T * c:T * c + T]
                        acc = dst[:, ch, :]
                        wc = w_row[0] + w_row[1] * (3 - s) + ch
                        w = pcol[:, wc:wc + 1]
                        if s == 0:
                            ins = V.tensor_scalar(acc, src, w, pcol[:, b_row + ch:b_row + ch + 1], ALU.mult, ALU.add)
                        else:
                            ins = V.scalar_tensor_tensor(acc[:, s:T], src[:, 0:T - s], w, acc[:, s:T], ALU.mult, ALU.add)
                        if s < 3:
                            order[0] += 1
                            ins.then_inc(S["dve_order"], 1)
                        else:
                            ins.then_inc(done, 1)
                    if s < 3:
                        dve.wait_ge(S["dve_order"], order[0])

            def split_lo(l, j, n, n0, it):
                dve.wait_ge(S[f"x_hi{j}"], n + 1)
                V.tensor_tensor(wlo[j][:, :], ring_unit(U_MOE + 3 * n0 + j), whi[j][:, :].bitcast(fp32),
                                ALU.subtract).then_inc(x_lo[j], 1)

            def hidden(n):
                dve.wait_ge(S["silu_g"], TT * n + TT)
                for t in range(TT):
                    V.scalar_tensor_tensor(h[:, t, :], sg[:, t, :], wts[:, t, n:n + 1] if isinstance(n, int)
                                           else wts[:, t, bass.ds(n, 1)], pb[4 + t][:, DE:2 * DE],
                                           ALU.mult, ALU.mult).then_inc(S["h_ready"], 1)

            def hidden_lo(n):
                dve.wait_ge(S["h_hi"], n + 1)
                V.tensor_tensor(hTl[:, :, :], pb[6][:, :].rearrange("p (k t) -> p k t", k=2), hTh[:, :, :].bitcast(fp32),
                                ALU.subtract).then_inc(S["h_lo"], 1)

            V.memset(eps[:, :], EPS).then_inc(eps_ready, 1)
            dve.wait_ge(const_in, 16 * 8)
            with dve.Fori(0, L) as l:
                order[0] = 0
                V.memset(bd[:, :, :, :], 0.0).then_inc(S["bd_zero"], 1)
                dve.wait_ge(S["params_turned"], 1)
                own(V.tensor_copy(pcol[:, :], pb[1][:, 0:R_END]), S["pcol"], 1)
                dve.wait_ge(S["cols_in"], 16 * 12)
                wait_pe_unit(dve, l, U_ADA_MIX + 7)
                modulation(0, pb[0])
                normed(x, xn, S["root_mix"], S["xn_ready"])
                for kk in range(KD):
                    dve.wait_ge(S["h_chunks"], kk // 2 + 1)
                    V.tensor_scalar(hT[:, kk, :], pb[4 + kk // 2][:, T * (kk % 2):T * (kk % 2) + T],
                                    modc[:, 0, 0, kk:kk + 1], modc[:, 0, 1, kk:kk + 1], ALU.mult,
                                    ALU.add).then_inc(S["hT_ready"], 1)
                wait_pe_unit(dve, l, U_ADA_MIX + 11)
                for i in range(2):
                    part = gates[:, 0, 512 * i:512 * i + 512]
                    V.tensor_tensor(part, part, pb[2 + i][:, :], ALU.add).then_inc(S["gates_m"], 1)

                lb = pcol[:, R_LB:R_LB + L * HG_H].rearrange("p (l h) -> p l h", l=L)
                link(V.tensor_copy(lbt[:, 0, :], lb[:, 0, :]))
                for i in range(1, L):
                    link(V.tensor_tensor(lbt[:, 0, :], lbt[:, 0, :], lb[:, i, :], ALU.max))
                for i in range(L):
                    V.tensor_tensor(lbs[:, i, :], lb[:, i, :], lbt[:, 0, :], ALU.subtract).then_inc(S["lb_in"], 1)
                lam = pcol[:, R_LAM:R_LAM + LRU_J]
                V.scalar_tensor_tensor(lruc[:, 0, :], lam, -1.0, lam, ALU.mult, ALU.min).then_inc(S["lam_in"], 1)

                for i in range(6):
                    wait_pe_unit(dve, l, U_W + i)
                    conv(i, xbcT, (R_CW, CH_XBC), 2 * i, R_CB, S["conv"])
                wait_pe_unit(dve, l, U_W + W_DT)
                s2 = lambda i: dts[:, i, :].rearrange("p (t h) -> p t h", t=TT)
                own(V.tensor_tensor(s2(0), pb[W_DT % W_BANKS][:, 0:32].rearrange("p (t h) -> p t h", t=TT),
                                    bcast(hb[:, 0, :], 1, TT), ALU.add), S["dt_in"], 1)
                V.scalar_tensor_tensor(dts[:, 1, :], dts[:, 0, :], -1.0, dts[:, 0, :], ALU.mult,
                                       ALU.min).then_inc(S["dt_in"], 1)
                dve.wait_ge(S["lb_exp"], 1)
                link(V.tensor_copy(lbt[:, 1, :], lbs[:, 0, :]))
                link(V.tensor_copy(lbt[:, 2, :], lbs[:, 0, :]))
                for i in range(1, L):
                    link(V.tensor_tensor(lbt[:, 1, :], lbt[:, 1, :], lbs[:, i, :], ALU.add))
                link(V.reciprocal(lbt[:, 1, :], lbt[:, 1, :]))
                link(V.tensor_tensor(lbs[:, :, :], lbs[:, :, :], bcast(lbt[:, 1, :], 1, L), ALU.mult))
                link(V.tensor_copy(lbt[:, 2, :], lbs[:, 0, :]))
                for i in range(1, L):
                    link(V.tensor_tensor(lbs[:, i, :], lbs[:, i, :], lbs[:, i - 1, :], ALU.add))
                link(V.tensor_tensor(lbs[:, :, :], lbs[:, :, :], bcast(lbt[:, 2, :], 1, L), ALU.subtract))
                link(V.tensor_scalar(lbs[:, :, :], lbs[:, :, :], -1.0, 1.0, ALU.mult, ALU.add))
                link(V.tensor_copy(omlb[:, :], lbs[:, bass.ds(l, 1), :].rearrange("p l h -> p (l h)")))
                dve.wait_ge(S["lam_ln"], 1)
                link(V.tensor_scalar(lruc[:, 0, :], lam, -1.0, 0.0, ALU.mult, ALU.max))
                link(V.tensor_tensor(lruc[:, 1, :], lruc[:, 0, :], lruc[:, 1, :], ALU.add))
                link(V.tensor_scalar(lruc[:, 2, :], lruc[:, 1, :], 8.0, None, ALU.mult))
                V.tensor_scalar(lruc[:, 3, :], lruc[:, 1, :], -8.0, None, ALU.mult).then_inc(S["lruc_ready"], 1)
                dve.wait_ge(S["dt_ln"], 1)
                link(V.scalar_tensor_tensor(dts[:, 2, :], dts[:, 0, :], 0.0, dts[:, 1, :], ALU.max, ALU.add))
                V.scalar_tensor_tensor(s2(3), s2(2), -1.0, bcast(hb[:, 1, :], 1, TT), ALU.mult,
                                       ALU.mult).then_inc(S["a_ready"], 1)
                dve.wait_ge(S["acum_done"], 1)
                link(V.tensor_copy(dts[:, 4, :], pb[3][:, 0:32]))
                V.tensor_tensor(dts[:, 5, :], pb[3][:, 32:64], dts[:, 4, :], ALU.subtract).then_inc(S["dec_in"], 1)
                dve.wait_ge(S["w_act"], 2)
                V.tensor_tensor(qkg[:, 1, :, :], qkg[:, 1, :, :], bcast(omlb[:, :], 2, T), ALU.mult).then_inc(S["k_ready"], 1)
                heads = lambda ap: ap.rearrange("p (h d) -> p h d", d=SSD_HD)
                for c in range(2):
                    dve.wait_ge(S["xh_ready"], 2 * c + 2)
                    own(V.tensor_tensor(heads(xdt[:, c, :]), heads(xh[:, c, :]),
                                        bcast(dts[:, 2, 16 * c:16 * c + 16], 2, SSD_HD), ALU.mult), S["xdt_ready"], c + 1)
                    if c == 0:
                        dve.wait_ge(S["dec"], 1)
                        V.tensor_tensor(heads(xdec[:, :]), heads(xdt[:, 0, :]), bcast(dts[:, 5, 0:16], 2, SSD_HD),
                                        ALU.mult).then_inc(S["xdec_ready"], 1)
                    link(V.tensor_tensor(heads(y[:, c, :]), heads(xh[:, c, :]), bcast(hb[:, 2, :], 2, SSD_HD), ALU.mult))

                dve.wait_ge(S["cb_ready"], 1)

                def diff(q):
                    c, h0 = q // 4, 4 * (q % 4)
                    dve.wait_ge(S["diff_done"], q + 1)
                    if q >= 2:
                        dve.wait_ge(S["ydiag"], q - 1)
                    V.tensor_tensor(mdec[:, q % 2, :, :], pb[4 + q % 2][:, :].rearrange("p (h t) -> p h t", h=4),
                                    bcast(dts[:, 4, 16 * c + h0:16 * c + h0 + 4], 2, P), ALU.subtract).then_inc(S["diff_sub"], 1)

                def masked(q):
                    c, g = q // 4, (q % 4) // 2
                    dve.wait_ge(S["diff_exp"], q + 1)
                    V.tensor_tensor(mdec[:, q % 2, :, :], mdec[:, q % 2, :, :], bcast(cb[:, 2 * c + g, :], 1, 4),
                                    ALU.mult).then_inc(S["m_ready"], 1)

                def y_group(i):
                    c, g = divmod(i, 2)
                    part = y[:, c, 512 * g:512 * g + 512]
                    dve.wait_ge(S["ydiag"], 2 * i + 2)
                    own(V.tensor_tensor(part, part, pb[6 + i % 2][:, :], ALU.add), S["y_taken"], i + 1)
                    if c == 1:
                        dve.wait_ge(S["yoff"], g + 1)
                        dve.wait_ge(S["eacum"], 1)
                        own(V.tensor_tensor(heads(tmp[:, :]), heads(pb[3][:, :]),
                                            bcast(dts[:, 0, 16 + 8 * g:24 + 8 * g], 2, SSD_HD), ALU.mult), S["yoff_taken"], g + 1)
                        link(V.tensor_tensor(part, part, tmp[:, :], ALU.add))

                for q in range(9):
                    if q < 8:
                        diff(q)
                    if q:
                        masked(q - 1)
                    if q in (3, 5, 7):
                        y_group((q - 3) // 2)
                y_group(3)
                for i in range(2):
                    wait_pe_unit(dve, l, U_W + W_LX + i)
                    conv(W_LX + i, lru_x, (R_LCW, LRU_J), 2 * i, R_LCB, S["conv_lx"])
                dve.wait_ge(S["w_act"], 8)
                for c in range(2):
                    own(V.tensor_tensor(y[:, c, :], y[:, c, :], z[:, c, :], ALU.mult), S["y_gated"], c + 1)
                link(V.memset(attn, 0.0))
                dve.wait_ge(S["y_root"], 1)
                link(V.reciprocal(ss[:, :], ss[:, :]))
                for i in range(4):
                    part = y[:, i // 2, 512 * (i % 2):512 * (i % 2) + 512]
                    V.tensor_scalar(part, part, ss[:, i:i + 1], None, ALU.mult).then_inc(S["y_norm"], 1)
                for i in range(4):
                    c, g = divmod(i, 2)
                    dve.wait_ge(S["y_turned"], i + 1)
                    V.tensor_tensor(yT[:, 4 * g:4 * g + 4, P * c:P * c + P],
                                    pb[4 + i][:, :].rearrange("p (k t) -> p k t", k=4),
                                    bcast(pcol[:, R_SNW + 4 * g:R_SNW + 4 * g + 4], 2, P), ALU.mult).then_inc(S["yT_ready"], 1)

                q_, k_, g_ = (qkg[:, i, :, :] for i in range(3))
                dve.wait_ge(S["logf"], 1)
                for hd in range(HG_H):
                    for t in range(TT):
                        seg = bT[:, hd, P * t:P * t + P]
                        order[0] += 1
                        V.tensor_tensor_scan(seg, ones[:, :], seg, 0.0, ALU.mult, ALU.add).then_inc(S["dve_order"], 1)
                dve.wait_ge(S["w_act"], 4)
                for i in range(2):
                    for src, buf in ((q_, lev_q), (k_, lev_k)):
                        order[0] += 1
                        V.tensor_copy(buf[i], src).then_inc(S["dve_order"], 1)
                dve.wait_ge(S["dve_order"], order[0])
                halves = lambda ap, m: ap.rearrange("p h (b s m) -> p (h b) s m", s=2, m=m)

                def level_in(i):
                    m = 1 << (i - 1)
                    e, b = halves(lev_e[i % 2], m), halves(bT, m)
                    r = b[:, :, 0, m - 1:m]
                    r = r.broadcast_to(list(r.shape[:2]) + [m])
                    V.tensor_tensor(e[:, :, 1, :], b[:, :, 1, :], r, ALU.subtract).then_inc(S["lev_in"], 1)
                    V.tensor_tensor(e[:, :, 0, :], r, b[:, :, 0, :], ALU.subtract).then_inc(S["lev_in"], 1)

                def level_out(i):
                    m = 1 << (i - 1)
                    e, lq, lk = (halves(ap, m) for ap in (lev_e[i % 2], lev_q[i % 2], lev_k[i % 2]))
                    dve.wait_ge(S["lev_exp"], i)
                    if i >= 3:
                        dve.wait_ge(S["att_done"], i - 1)
                    V.tensor_tensor(lq[:, :, 1, :], halves(q_, m)[:, :, 1, :], e[:, :, 1, :], ALU.mult).then_inc(S["lev_ready"], 1)
                    V.tensor_tensor(lk[:, :, 0, :], halves(k_, m)[:, :, 0, :], e[:, :, 0, :], ALU.mult).then_inc(S["lev_ready"], 1)

                def take(i):
                    dve.wait_ge(S["att_done"], i + 1)
                    for j in range(2):
                        V.copy_predicated(attn[:, 4 * j:4 * j + 4, :], bcast(masks[:, i, :], 1, 4),
                                          pb[4 + 2 * (i % 2) + j][:, :].rearrange("p (g t) -> p g t", g=4)).then_inc(S["att_taken"], 1)

                for i in range(1, LEVELS):
                    level_in(i)
                    take(i - 1)
                    level_out(i)
                e, lq, lk = lev_e[0], lev_q[0], lev_k[0]
                r = bT[:, :, P - 1:P].broadcast_to([P, HG_H, P])
                V.tensor_copy(e[:, :, P:T], bT[:, :, P:T]).then_inc(S["lev_in"], 1)
                V.tensor_tensor(e[:, :, 0:P], r, bT[:, :, 0:P], ALU.subtract).then_inc(S["lev_in"], 1)
                take(LEVELS - 1)
                dve.wait_ge(S["lev_exp"], LEVELS)
                dve.wait_ge(S["att_done"], LEVELS - 1)
                V.tensor_tensor(lq[:, :, P:T], q_[:, :, P:T], e[:, :, P:T], ALU.mult).then_inc(S["lev_ready"], 1)
                V.tensor_tensor(lk[:, :, 0:P], k_[:, :, 0:P], e[:, :, 0:P], ALU.mult).then_inc(S["lev_ready"], 1)
                for i in range(2):
                    e2 = lev_e[1][:, 2 * i:2 * i + 2, :]
                    dve.wait_ge(S["o_root"], i + 1)
                    link(V.reciprocal(e2, e2))
                    link(V.tensor_tensor(lev_q[0][:, 2 * i:2 * i + 2, :], pb[4 + i][:, :].rearrange("p (h t) -> p h t", h=2),
                                         e2, ALU.mult))
                dve.wait_ge(S["w_act"], 14)
                for hd in range(HG_H):
                    V.scalar_tensor_tensor(yT[:, 8 + hd, :], lev_q[0][:, hd, :], pcol[:, R_HNW + hd:R_HNW + hd + 1],
                                           g_[:, hd, :], ALU.mult, ALU.mult).then_inc(S["yT_ready"], 1)

                dve.wait_ge(S["lru_tanh"], LRU_J)
                link(V.tensor_scalar(lru_u, lru_v, 1.0, None, ALU.add))
                link(V.reciprocal(lru_u, lru_u))
                flat = lambda ap: ap.rearrange("p j t -> p (j t)")
                V.scalar_tensor_tensor(flat(lru_u), flat(lru_v), 2.0, flat(lru_u), ALU.mult, ALU.mult).then_inc(S["lru_w"], 1)
                dve.wait_ge(S["gate_sig"], 8)
                link(V.tensor_tensor(lru_i, lru_i, lru_x[:, :, :], ALU.mult))
                dve.wait_ge(S["lru_sqrt"], 1)
                link(V.tensor_tensor(lru_u, lru_u, lru_i, ALU.mult))
                dve.wait_ge(S["lru_exp"], LRU_J)
                link(V.memset(lru_a[:, :, 0:1], 0.0))
                link(V.tensor_tensor_scan(flat(lru_r), flat(lru_a), flat(lru_u), 0.0, ALU.mult, ALU.add))
                own(V.tensor_tensor(lru_r, lru_r, lru_g[:, :, :], ALU.mult), S["lru_y"], 1)
                dve.wait_ge(S["lru_root"], 1)
                link(V.reciprocal(tmp[:, 0:T], tmp[:, 0:T]))
                link(V.tensor_tensor(lru_i, lru_r, bcast(tmp[:, 0:T], 1, LRU_J), ALU.mult))
                V.tensor_tensor(yT[:, 12:16, :], lru_i, bcast(pcol[:, R_LNW:R_LNW + LRU_J], 2, T),
                                ALU.mult).then_inc(S["yT_ready"], 1)

                wait_pe_unit(dve, l, U_ADA_FFN + 7)
                modulation(1, pb[0])
                wait_pe_unit(dve, l, U_ADA_FFN + 11)
                for i in range(2):
                    part = gates[:, 1, 512 * i:512 * i + 512]
                    V.tensor_tensor(part, part, pb[1 + i][:, :], ALU.add).then_inc(S["gates_f"], 1)
                wait_pe_unit(dve, l, U_OUT + 7)
                dve.wait_ge(S["gates_m"], 2)
                for i in range(4):
                    t, half = divmod(i, 2)
                    cols = slice(512 * half, 512 * half + 512)
                    link(V.tensor_tensor(tmp[:, :], pb[4 + i][:, :], gates[:, 0, cols], ALU.mult))
                    own(V.tensor_tensor(x[:, t, cols], x[:, t, cols], tmp[:, :], ALU.add), S["x_mid"], i + 1)

                normed(x, xn2, S["root_ffn"], S["xn2_ready"])
                for kk in range(KD):
                    dve.wait_ge(S["h2_chunks"], kk // 2 + 1)
                    V.tensor_scalar(h2T[:, kk, :], pb[kk // 2][:, T * (kk % 2):T * (kk % 2) + T],
                                    modc[:, 1, 0, kk:kk + 1], modc[:, 1, 1, kk:kk + 1], ALU.mult,
                                    ALU.add).then_inc(S["h2_ready"], 1)
                for j in range(4):
                    dve.wait_ge(S["x_hi"], j + 1)
                    V.tensor_tensor(xlo[:, 2 * j:2 * j + 2, :], h2T[:, 2 * j:2 * j + 2, :],
                                    xhi[:, 2 * j:2 * j + 2, :].bitcast(fp32), ALU.subtract).then_inc(S["x_lo"], 1)
                split_lo(l, 0, 0, 0, 0)
                split_lo(l, 1, 0, 0, 0)
                split_lo(l, 0, 1, 1, 0)
                dve.wait_ge(S["scores"], 1)
                link(V.tensor_tensor(sel[:, :, :], sc[:, :, :], bcast(rbias[:, :], 1, TT), ALU.add))
                for t in range(TT):
                    for g in range(8):
                        order[0] += 1
                        V.max(m8[:, t, g, :], sel[:, t, 8 * g:8 * g + 8]).then_inc(S["dve_order"], 1)
                dve.wait_ge(S["dve_order"], order[0])
                link(V.tensor_tensor(gsc[:, :, :], m8[:, :, :, 0], m8[:, :, :, 1], ALU.add))
                c0, c1 = (cmp_[:, i, :].rearrange("p (t i j) -> p t i j", t=TT, i=8) for i in range(2))
                other, self_ = bcast(gsc[:, :, :], 2, 8), bcast(gsc[:, :, :], 3, 8)
                link(V.tensor_tensor(c0, other, self_, ALU.is_equal))
                link(V.tensor_tensor(c0, c0, bcast(lt8[:, :].rearrange("p (i j) -> p i j", i=8), 1, TT), ALU.mult))
                link(V.tensor_tensor(c1, other, self_, ALU.is_gt))
                link(V.tensor_tensor(c0, c0, c1, ALU.add))
                link(V.tensor_reduce(gm[:, 0, :, :], c0, AXL.X, ALU.add))
                link(V.tensor_scalar(gm[:, 0, :, :], gm[:, 0, :, :], 3.5, None, ALU.is_lt))
                link(V.tensor_scalar(gm[:, 1, :, :], gm[:, 0, :, :], 1.0e4, -1.0e4, ALU.mult, ALU.add))
                by_group = lambda ap: ap.rearrange("p t (g e) -> p (t g) e", g=8)
                flat_g = lambda i: bcast(gm[:, i, :, :].rearrange("p t g -> p (t g)"), 2, 8)
                link(V.tensor_tensor(by_group(sel[:, :, :]), by_group(sel[:, :, :]), flat_g(0), ALU.mult))
                link(V.tensor_tensor(by_group(sel[:, :, :]), by_group(sel[:, :, :]), flat_g(1), ALU.add))
                for t in range(TT):
                    link(V.max(t8[:, t, :], sel[:, t, :]))
                    link(V.match_replace(rep[:, t, :], in_to_replace=t8[:, t, :], in_values=sel[:, t, :], imm_value=-3.0e4))
                link(V.tensor_tensor(rep[:, :, :], rep[:, :, :], sel[:, :, :], ALU.not_equal))
                link(V.tensor_tensor(rep[:, :, :], rep[:, :, :], sc[:, :, :], ALU.mult))
                link(V.tensor_reduce(wsum[:, 0, :], rep[:, :, :], AXL.X, ALU.add))
                link(V.reciprocal(wsum[:, 1, :], wsum[:, 0, :]))
                for t in range(TT):
                    link(V.tensor_scalar(wts[:, t, 1:E + 1], rep[:, t, :], wsum[:, 1, t:t + 1], SCALE, ALU.mult, ALU.mult))
                link(V.memset(wts[:, :, 0:1], 1.0))

                def expert_step(n, n0, it, last=False):
                    hidden(n - 1)
                    split_lo(l, 1, n, n0, it)
                    split_lo(l, 2, n - 1, n0 - 1, it)
                    hidden_lo(n - 1)
                    if not last:
                        split_lo(l, 0, n + 1, n0 + 1, it)

                for r in range(X_IT):
                    expert_step(1 + r, 1 + r, 0)
                with dve.Fori(1, E // X_IT) as it:
                    for r in range(X_IT):
                        expert_step(X_IT * it + 1 + r, 1 + r, it)
                expert_step(E, E, 0, last=True)
                hidden(E)
                split_lo(l, 2, E, E, 0)
                hidden_lo(E)
                dve.wait_ge(S["gates_f"], 2)
                dve.wait_ge(S["x_used2"], N_X)
                for i in range(4):
                    t, half = divmod(i, 2)
                    cols = slice(512 * half, 512 * half + 512)
                    link(V.tensor_tensor(tmp2[:, :], pb[i][:, :], gates[:, 1, cols], ALU.mult))
                    link(V.tensor_tensor(x[:, t, cols], x[:, t, cols], tmp2[:, :], ALU.add))
                dve.wait_ge(S["end_pe"], 1)
                dve.wait_ge(S["end_act"], 1)
                for s in S.values():
                    dve.sem_clear(s)
                dve.sem_inc(layer_done, 1)

            dve.wait_ge(fin_sq, TT + 1)
            V.reciprocal(rstd[:, :], ss[:, 2:4]).then_inc(fin_dve, 1)
            dve.wait_ge(fin_dve, 1)
            for t in range(TT):
                V.tensor_scalar(xo[:, t, :], x[:, t, :], rstd[:, t:t + 1], None, ALU.mult).then_inc(fin_dve, 1)
            dve.wait_ge(fin_dve, 3)
            dve.wait_ge(fin_in, 16)
            for t in range(TT):
                V.tensor_tensor(xo[:, t, :], xo[:, t, :], fnw[:, :], ALU.mult).then_inc(fin_dve, 1)

        @block.tensor
        def _(pe):
            M, TR = nc.tensor.matmul, nc.tensor.transpose

            def ada(l, u0, cols_bank, row_banks):
                for part in range(2):
                    for q in range(4):
                        u = u0 + 4 * part + q
                        wait_unit(pe, l, u)
                        w = ring_unit(u)
                        for k2 in range(2):
                            for kk in range(KD):
                                c = part * KD + kk
                                ins = M(cols_bank[:, c:c + 1], w[:, 1024 * k2 + kk:1024 * k2 + 1024:KD],
                                        cact[:, 2 * q + k2:2 * q + k2 + 1], start=part + q + k2 + kk == 0,
                                        stop=part == 1 and q == 3 and k2 == 1 and kk == KD - 1, skip_group_check=True)
                        ins.then_inc(pe_unit, 1)
                for q in range(4):
                    u = u0 + 8 + q
                    wait_unit(pe, l, u)
                    for k2 in range(2):
                        lhs = cact[:, 2 * q + k2:2 * q + k2 + 1].broadcast_to([P, P])
                        for half in range(2):
                            c = 1024 * k2 + 512 * half
                            ins = M(row_banks[half][:, :], lhs, ring_unit(u)[:, c:c + 512], start=q + k2 == 0,
                                    stop=q == 3 and k2 == 1)
                    ins.then_inc(pe_unit, 1)

            def turn(src, dst_banks, ready, done):
                pe.wait_ge(ready, TT)
                for kk in range(KD):
                    for t in range(TT):
                        c = T * (kk % 2) + P * t
                        ins = TR(dst_banks[kk // 2][:, c:c + P], src[:, t, kk::KD], ident[:, :])
                    if kk % 2:
                        ins.then_inc(done, 1)

            emptied = []
            n_act = 0
            for i in range(N_W):
                if i < W_DT:
                    emptied.append(("conv", 2 * i + 2))
                elif i == W_DT:
                    emptied.append(("dt_in", 1))
                elif W_LX <= i < W_HV:
                    emptied.append(("conv_lx", 2 * (i - W_LX) + 2))
                else:
                    n_act += 1
                    emptied.append(("w_act", n_act))

            def project(l, i):
                u = U_W + i
                bank = pb[i % W_BANKS]
                if i >= W_BANKS:
                    pe.wait_ge(S[emptied[i - W_BANKS][0]], emptied[i - W_BANKS][1])
                wait_unit(pe, l, u)
                if W_COLS[i] in range(C_Z, C_Z + SSD_IN) or W_COLS[i] in range(C_HV, C_HV + 512) or i == W_DT:
                    n = SSD_HEADS if i == W_DT else 256
                    for t in range(TT):
                        for k in range(KD):
                            ins = M(bank[:, n * t:n * t + n], hT[:, k, P * t:P * t + P],
                                    ring_unit(u)[:, n * k:n * k + n], start=k == 0, stop=k == KD - 1)
                else:
                    for c in range(2):
                        for k in range(KD):
                            w = ring_unit(u)[:, 256 * k + P * c:256 * k + P * c + P]
                            ins = M(bank[:, T * c:T * c + T], w, hT[:, k, :], start=k == 0, stop=k == KD - 1)
                ins.then_inc(pe_unit, 1)

            def gate_up(l, n, half):
                wait_split(pe, l, half, n)
                wh, wl = (w[half][:, :].rearrange("p (g k c) -> p g k c", g=2, k=4) for w in (whi, wlo))
                for k in range(4):
                    for t in range(TT):
                        xs = slice(P * t, P * t + P)
                        kk = 4 * half + k
                        first, last = half == 0 and k == 0, half == 1 and k == 3
                        bank = pb[4 + t][:, :]
                        M(bank, xhi[:, kk, xs], wh[:, :, k, :], start=first, stop=False)
                        M(bank, xhi[:, kk, xs], wl[:, :, k, :], start=False, stop=False)
                        ins = M(bank, xlo[:, kk, xs], wh[:, :, k, :], start=False, stop=last)
                ins.then_inc(S[f"x_used{half}"], 1)

            def turn_hidden(n):
                pe.wait_ge(S["h_ready"], TT * n + TT)
                for hc in range(2):
                    for t in range(TT):
                        ins = TR(pb[6][:, T * hc + P * t:T * hc + P * t + P], h[:, t, P * hc:P * hc + P], ident[:, :])
                ins.then_inc(S["h_turned"], 1)

            def down(l, n, first=False, last=False):
                wait_split(pe, l, 2, n)
                pe.wait_ge(S["h_lo"], n + 1)
                wh, wl = (w[2][:, :].rearrange("p (k c) -> p k c", k=2) for w in (whi, wlo))
                for hc in range(2):
                    for t in range(TT):
                        for half in range(2):
                            ts, cs = slice(P * t, P * t + P), slice(512 * half, 512 * half + 512)
                            acc = pb[2 * t + half][:, :]
                            M(acc, hTh[:, hc, ts], wh[:, hc, cs], start=first and hc == 0, stop=False)
                            M(acc, hTh[:, hc, ts], wl[:, hc, cs], start=False, stop=False)
                            ins = M(acc, hTl[:, hc, ts], wh[:, hc, cs], start=False, stop=last and hc == 1)
                ins.then_inc(S["x_used2"], 1)

            pe.wait_ge(const_in, 16 * 8)
            pe.wait_ge(silu_c, 1)
            with pe.Fori(0, L) as l:
                pe.wait_ge(S["rows_in"], 16 * 11)
                TR(pb[1][:, 0:R_END], prow[0:R_END, :], ident[0:R_END, 0:R_END]).then_inc(S["params_turned"], 1)
                pe.wait_ge(S["cols_in"], 16 * 12)
                ada(l, U_ADA_MIX, pb[0], (pb[2], pb[3]))
                turn(xn, pb[4:8], S["xn_ready"], S["h_chunks"])
                pe.wait_ge(S["modc_s"], 1)
                pe.wait_ge(S["modc"], 1)
                pe.wait_ge(S["pcol"], 1)
                pe.wait_ge(S["hT_ready"], KD)
                pe.wait_ge(S["gates_m"], 2)
                for i in range(W_HQ + 2):
                    project(l, i)

                pe.wait_ge(S["a_ready"], 1)
                M(pb[3][:, 0:32], tri[:, :], dts[:, 3, :], start=True, stop=True)
                M(pb[3][:, 32:64], ones[:, :], dts[:, 3, :], start=True, stop=True).then_inc(S["acum_done"], 1)
                pe.wait_ge(S["xbc_ready"], 6)
                chunk = lambda c: slice(P * c, P * c + P)
                for c in range(2):
                    for g in range(2):
                        i = 2 * c + g
                        ins = M(pb[4][:, P * i:P * i + P], xbcT[:, 8 + g, chunk(c)], xbcT[:, 10 + g, chunk(c)],
                                start=True, stop=True)
                ins.then_inc(S["cb_done"], 1)
                for g in range(2):
                    ins = TR(pb[5][:, P * g:P * g + P], xbcT[:, 8 + g, chunk(0)], ident[:, :])
                ins.then_inc(S["btok_done"], 1)
                for i in range(4):
                    c, half = divmod(i, 2)
                    if i == 2:
                        pe.wait_ge(S["cb_ready"], 1)
                    if i == 3:
                        pe.wait_ge(S["btok_ready"], 1)
                    for j in range(4):
                        ins = TR(pb[(6, 7, 4, 5)[i]][:, P * j:P * j + P], xbcT[:, 4 * half + j, chunk(c)], ident[:, :])
                    ins.then_inc(S["xs_turned"], 1)
                for i in range(W_Z, W_Z + 4):
                    project(l, i)
                pe.wait_ge(S["xdec_ready"], 1)
                pe.wait_ge(S["btok_ready"], 1)
                pe.wait_ge(S["dec_in"], 1)
                for g in range(2):
                    if g:
                        pe.wait_ge(S["st_ready"], g)
                    M(pb[3][:, :], btok[:, g, :], xdec[:, 512 * g:512 * g + 512], start=True,
                      stop=True).then_inc(S["st_done"], 1)
                pe.wait_ge(S["xh_ready"], 4)

                def diff(q):
                    c, h0 = q // 4, 4 * (q % 4)
                    bank = pb[4 + q % 2]
                    if q >= 2:
                        pe.wait_ge(S["diff_sub"], q - 1)
                    M(bank[:, :].rearrange("p (h t) -> p h t", h=4), ident[:, :], bcast(neg[:, :], 1, 4), start=True,
                      stop=False, skip_group_check=True)
                    for j in range(4):
                        ac = dts[:, 3, 16 * c + h0 + j:16 * c + h0 + j + 1].broadcast_to([P, P])
                        ins = M(bank[:, P * j:P * j + P], ac, tri[:, :], start=False, stop=True, skip_group_check=True)
                    ins.then_inc(S["diff_done"], 1)

                def y_diag(q):
                    c, h0, i = q // 4, 4 * (q % 4), q // 2
                    if i >= 2 and q % 2 == 0:
                        pe.wait_ge(S["y_taken"], i - 1)
                    pe.wait_ge(S["m_ready"], q + 1)
                    pe.wait_ge(S["xdt_ready"], c + 1)
                    for j in range(4):
                        hd = h0 + j
                        o = SSD_HD * (hd % 8)
                        ins = M(pb[6 + i % 2][:, o:o + SSD_HD], mdec[:, q % 2, j, :],
                                xdt[:, c, SSD_HD * hd:SSD_HD * hd + SSD_HD], start=True, stop=True)
                    ins.then_inc(S["ydiag"], 1)

                def y_off(g):
                    pe.wait_ge(S["st_ready"], 2)
                    if g:
                        pe.wait_ge(S["yoff_taken"], g)
                    M(pb[3][:, :], xbcT[:, 10 + g, chunk(1)], stT[:, g, :], start=True, stop=True).then_inc(S["yoff"], 1)

                rest = list(range(W_LX, N_W))
                for q in range(9):
                    if q < 8:
                        diff(q)
                    if q == 5:
                        y_off(0)
                    if q:
                        y_diag(q - 1)
                    if q in (2, 6):
                        pass
                y_off(1)
                for i in rest:
                    project(l, i)
                for i in range(4):
                    c, g = divmod(i, 2)
                    pe.wait_ge(S["y_norm"], i + 1)
                    pe.wait_ge(S["y_taken"], 4)
                    for j in range(4):
                        o = 512 * g + P * j
                        ins = TR(pb[4 + i][:, P * j:P * j + P], y[:, c, o:o + P], ident[:, :])
                    ins.then_inc(S["y_turned"], 1)

                pe.wait_ge(S["k_ready"], 1)
                pe.wait_ge(S["w_act"], 4)
                for i in range(LEVELS):
                    lq, lk = (qkg[:, 0, :, :], qkg[:, 1, :, :]) if i == 0 else (lev_q[i % 2], lev_k[i % 2])
                    if i:
                        pe.wait_ge(S["lev_ready"], 2 * i)
                    if i < 2:
                        pe.wait_ge(S["yT_ready"], 4)
                    else:
                        pe.wait_ge(S["att_taken"], 2 * i - 2)
                    for hd in range(HG_H):
                        for t in range(TT):
                            o = P * (2 * (hd % 2) + t)
                            ins = M(pb[4 + 2 * (i % 2) + hd // 2][:, o:o + P], lk[:, hd, chunk(t)], lq[:, hd, chunk(t)],
                                    start=True, stop=True)
                    ins.then_inc(S["att_done"], 1)
                pe.wait_ge(S["lev_ready"], 2 * LEVELS)
                pe.wait_ge(S["yoff_taken"], 2)
                for hd in range(HG_H):
                    ins = M(pb[3][:, P * hd:P * hd + P], lev_k[0][:, hd, chunk(0)], lev_q[0][:, hd, chunk(1)],
                            start=True, stop=True)
                ins.then_inc(S["cross_done"], 1)
                pe.wait_ge(S["att_taken"], 2 * LEVELS)
                pe.wait_ge(S["cross_ready"], 1)
                for hd in range(HG_H):
                    vh = v[:, :, P * hd:P * hd + P]
                    o = T * (hd % 2)
                    bank = pb[4 + hd // 2]
                    M(bank[:, o:o + P], vh[:, 0, :], attn[:, 2 * hd, :], start=True, stop=True)
                    M(bank[:, o + P:o + T], vh[:, 1, :], attn[:, 2 * hd + 1, :], start=True, stop=False)
                    ins = M(bank[:, o + P:o + T], vh[:, 0, :], cross[:, hd, :], start=False, stop=True)
                ins.then_inc(S["o_done"], 1)
                for i in range(2):
                    pe.wait_ge(S["o_sq"], i + 1)
                    ins = M(pb[6 + i][:, :].rearrange("p (h t) -> p h t", h=2), ones[:, :], lev_e[0][:, 2 * i:2 * i + 2, :],
                            start=True, stop=True)
                ins.then_inc(S["o_sum"], 1)

                pe.wait_ge(S[emptied[-1][0]], emptied[-1][1])
                ada(l, U_ADA_FFN, pb[0], (pb[1], pb[2]))

                pe.wait_ge(S["conv_lx"], 4)
                pe.wait_ge(S["bd_in"], 16 * 4)
                pe.wait_ge(S["o_root"], 2)
                pe.wait_ge(S["yT_ready"], 8)
                for k in range(2):
                    for j in range(LRU_J):
                        o = T * (j % 2)
                        ins = M(pb[4 + 2 * k + j // 2][:, o:o + T], bd[:, k, j, :], lru_x[:, j, :], start=True, stop=True)
                ins.then_inc(S["gate_mm"], 1)
                pe.wait_ge(S["lru_sq"], 1)
                for j in range(LRU_J):
                    ins = M(pb[3][:, 0:T], ones[:, :], lru_v[:, j, :], start=j == 0, stop=j == LRU_J - 1)
                ins.then_inc(S["lru_sum"], 1)

                pe.wait_ge(S["gate_sig"], 8)
                pe.wait_ge(S["yT_ready"], 9)
                for i in range(8):
                    wait_unit(pe, l, U_OUT + i)
                    for k2 in range(2):
                        k = 2 * i + k2
                        for t in range(TT):
                            for half in range(2):
                                c = 1024 * k2 + 512 * half
                                ins = M(pb[4 + 2 * t + half][:, :], yT[:, k, chunk(t)], ring_unit(U_OUT + i)[:, c:c + 512],
                                        start=k == 0, stop=k == KY - 1)
                    ins.then_inc(pe_unit, 1)

                pe.wait_ge(S["modc_s"], 2)
                pe.wait_ge(S["gates_f"], 2)
                pe.wait_ge(S["lru_root"], 1)
                turn(xn2, pb[0:4], S["xn2_ready"], S["h2_chunks"])
                pe.wait_ge(S["router_in"], 16)
                pe.wait_ge(S["h2_ready"], KD)
                pe.wait_ge(S["x_mid"], 4)
                for t in range(TT):
                    for k in range(KD):
                        ins = M(pb[7][:, E * t:E * t + E], h2T[:, k, chunk(t)], rw[:, k, :], start=k == 0, stop=k == KD - 1)
                ins.then_inc(S["logits"], 1)
                pe.wait_ge(S["x_lo"], 4)
                gate_up(l, 0, 0)
                gate_up(l, 0, 1)

                def expert_step(n, first=False):
                    pe.wait_ge(S["h_ready"], TT * n)
                    gate_up(l, n, 0)
                    turn_hidden(n - 1)
                    gate_up(l, n, 1)
                    down(l, n - 1, first=first)

                for n in range(1, X_IT + 1):
                    expert_step(n, first=n == 1)
                with pe.Fori(1, E // X_IT) as it:
                    for r in range(X_IT):
                        expert_step(X_IT * it + 1 + r)
                expert_step(E)
                turn_hidden(E)
                down(l, E, last=True)
                pe.sem_inc(S["end_pe"], 1)
                pe.wait_ge(layer_done, l + 1)


SIGNALS = """rows_in cols_in bd_zero bd_in params_turned pcol modc_s modc ss_mix root_mix xn_ready h_chunks hT_ready
    gates_m gates_f lb_in lb_exp lam_in lam_exp lam_ln lruc_ready conv xbc_ready conv_lx w_act
    dt_in dt_exp dt_ln a_ready acum_done dec_in dec eacum k_ready cb_done cb_ready btok_done btok_ready
    xs_turned xh_ready xdt_ready xdec_ready st_done st_ready diff_done diff_sub diff_exp m_ready ydiag yoff
    y_taken yoff_taken y_gated y_sq y_root y_norm y_turned yT_ready logf lev_in lev_exp lev_ready att_done att_taken
    cross_done cross_ready o_done o_sq o_sum o_root gate_mm gate_sig lru_tanh lru_exp lru_w lru_sqrt lru_y lru_sq
    lru_sum lru_root x_mid router_in ss_ffn root_ffn xn2_ready h2_chunks h2_ready x_hi x_lo logits scores
    x_hi0 x_hi1 x_hi2 x_used0 x_used1 x_used2 silu_g h_ready h_turned h_hi h_lo dve_order end_pe end_act""".split()


def kernel(**inputs):
    import numpy as np
    import concourse.bacc as bacc
    from concourse.bass_utils import run_bass_kernel_spmd

    i = np.arange(P)
    part, col = i[:, None], i[None, :]
    consts = np.concatenate([
        (part == col).astype(np.float32),
        (part <= col).astype(np.float32),
        np.where(col < part, np.float32(NEG), np.float32(0)),
        np.ones((P, P), np.float32),
        np.broadcast_to((np.arange(8)[None, :] < np.arange(8)[:, None]).astype(np.float32).reshape(1, 64), (P, 64)),
    ], axis=1)
    masks = [part == col]
    for level in range(1, LEVELS):
        m = 1 << (level - 1)
        masks.append((part // (2 * m) == col // (2 * m)) & (part // m % 2 == 0) & (col // m % 2 == 1))
    masks = np.concatenate(masks, axis=1).astype(np.uint32)

    nc = bacc.Bacc("TRN2", target_bir_lowering=False, num_devices=1)
    arrays = {f"in_{k}": np.ascontiguousarray(v) for k, v in inputs.items()}
    arrays["in_consts"] = np.ascontiguousarray(consts)
    arrays["in_masks"] = np.ascontiguousarray(masks)
    aps = {k[3:]: nc.dram_tensor(k, v.shape, mybir.dt.from_np(v.dtype), kind="ExternalInput").ap()
           for k, v in arrays.items()}
    out = nc.dram_tensor("out", (1, T, D), fp32, kind="ExternalOutput").ap()
    build(nc, aps, out)
    got = run_bass_kernel_spmd(nc, [arrays], core_ids=[0])
    return got.results[0]["out"]
```

```python
import concourse.bass as bass
from concourse import mybir
from contextlib import ExitStack

fp32 = mybir.dt.float32
fp32r = mybir.dt.float32r
uint32 = mybir.dt.uint32
ALU = mybir.AluOpType
ACT = mybir.ActivationFunctionType
AXL = mybir.AxisListType

P = 128
L, T, D = 2, 256, 1024
TT = T // P
KD = D // P
EPS = 1e-6
SSD_IN, SSD_HEADS, SSD_HD, SSD_N = 1024, 16, 64, 128
CH_XBC = (SSD_IN + 4 * SSD_N) // P
HG_H = 4
LRU_J = 4
D_IN = 5648
C_Z, C_XBC, C_DT = 0, SSD_IN, SSD_IN + CH_XBC * P
C_HQ = C_DT + SSD_HEADS
C_HF, C_HV, C_HG, C_LG, C_LX = (C_HQ + 512 * i for i in range(1, 6))
KY = 16
E, DE = 64, 256
SCALE = 2.5
NEG = -1.0e30

RING = 6
W_COLS = ([C_XBC + 256 * i for i in range(6)] + [C_DT] + [C_HF, C_HF + 256, C_HQ, C_HQ + 256]
          + [C_Z + 256 * i for i in range(4)] + [C_LX, C_LX + 256, C_HV, C_HV + 256, C_LG, C_LG + 256,
                                                 C_HG, C_HG + 256])
N_W = len(W_COLS)
U_W = 0
U_OUT = U_W + N_W
U_MOE = U_OUT + 8 + 2
UNITS = U_MOE + 3 * (E + 1)
PADS = (U_OUT + 8, U_OUT + 9)
assert UNITS % RING == 0
(W_XBC, W_DT, W_HF, W_HQ, W_Z, W_LX, W_HV, W_LG, W_HG) = 0, 6, 7, 9, 11, 15, 17, 19, 21
DVE_UNITS = list(range(W_XBC, W_DT + 1)) + [W_LX, W_LX + 1]
W_BANKS = 3

R_CW, R_CB, R_LCW, R_LCB, R_BA, R_BX, R_LAM, R_LNW, R_HNW, R_SNW, R_LB, R_END = (
    0, 48, 60, 76, 80, 84, 88, 92, 96, 100, 108, 116)
LEVELS = 8


N_PE = U_OUT + 8
N_X = E + 1
SLOTS = P
X_IT = 2
assert 3 * X_IT == RING
N_IT = (E - 1) // X_IT
LAST = X_IT * N_IT + 1
ADA_STEPS = 3 * KD
ADA_BUFS = 3


def slot_of(u):
    return u % RING


def weight_of(u):
    return 0 if u in PADS else 32 if u >= U_MOE and (u - U_MOE) % 3 < 2 else 16


def filled(u):
    return sum(weight_of(q) for q in range(slot_of(u), u + 1, RING))


def per_layer(s):
    return sum(weight_of(q) for q in range(s, UNITS, RING))


def build(nc, a, out):
    ctx = ExitStack()
    with ctx:
        def sem(name):
            return ctx.enter_context(nc.semaphore(name))

        def sb(name, shape, dt=fp32, stack=ctx):
            return stack.enter_context(nc.sbuf_tensor(name, [P] + shape, dt))

        def bcast(ap, axis, n):
            shape = list(ap.shape)
            shape.insert(axis, n)
            return ap.unsqueeze(axis).broadcast_to(shape)

        ring = sb("ring", [RING, 2048])
        x = sb("x", [TT, D])
        ident = sb("ident", [P])
        tri = sb("tri", [P])
        neg = sb("neg", [P])
        ones = sb("ones", [P])
        lt8 = sb("lt8", [64])
        iota = sb("iota", [SLOTS])
        masks = sb("masks", [LEVELS, P], uint32)
        cact = sb("cact", [KD])
        craw = sb("craw", [KD])
        prow = sb("prow", [L, P])
        prow_now = sb("prow_now", [P])
        pcol = sb("pcol", [R_END])
        pall = sb("pall", [L, P])
        pnow = sb("pnow", [P])
        norm_w = pnow[:, 0:2 * KD].rearrange("p (i k) -> p i k", i=2)
        hb = pnow[:, 2 * KD:2 * KD + 3 * SSD_HEADS].rearrange("p (i h) -> p i h", i=3)
        rbias = pnow[:, P - E:P]
        ada_w = sb("ada_w", [ADA_BUFS, D])
        ada_acc = sb("ada_acc", [3, D])
        gates = sb("gates", [2, D])
        modc = sb("modc", [2, 2, KD])
        lbs = sb("lbs", [L, HG_H])
        lbt = sb("lbt", [4, HG_H])
        omlb = sb("omlb", [HG_H])
        lruc = sb("lruc", [4, LRU_J])
        ss = sb("ss", [4])
        rstd = sb("rstd", [2])
        eps = sb("eps", [1])

        mix = ExitStack()
        hT = sb("hT", [KD, T], stack=mix)
        yT = sb("yT", [KY, T], stack=mix)
        z = sb("z", [TT, SSD_IN], stack=mix)
        start = ExitStack()
        ada_first = sb("ada_first", [2, KD, D], stack=start)
        start.close()
        xbcT = sb("xbcT", [CH_XBC, T], stack=mix)
        xh = sb("xh", [TT, SSD_IN], stack=mix)
        xdt = sb("xdt", [TT, SSD_IN], stack=mix)
        y = sb("y", [TT, SSD_IN], stack=mix)
        xdec = sb("xdec", [SSD_IN], stack=mix)
        mdec = sb("mdec", [2, 4, P], stack=mix)
        cb = sb("cb", [4, P], stack=mix)
        btok = sb("btok", [2, P], stack=mix)
        stT = sb("stT", [2, 512], stack=mix)
        dts = sb("dts", [6, 32], stack=mix)
        qkg = sb("qkg", [3, HG_H, T], stack=mix)
        v = sb("v", [TT, 512], stack=mix)
        bd = sb("bd", [2, LRU_J, P], stack=mix)
        xn = z
        bT = xdec[:, :].rearrange("p (h t) -> p h t", h=HG_H)
        lev_e, lev_q, lev_k = ([buf[:, i, :].rearrange("p (h t) -> p h t", h=HG_H) for i in range(2)]
                               for buf in (xh, xdt, y))
        attn = z[:, 0, :].rearrange("p (g t) -> p g t", g=8)
        cross = z[:, 1, 0:512].rearrange("p (h t) -> p h t", h=HG_H)
        lru_x = stT[:, :, :].rearrange("p g (j t) -> p (g j) t", t=T)
        lru_g = mdec[:, :, :, :].rearrange("p i j c -> p (i j c)").rearrange("p (j t) -> p j t", t=T)
        lru_r, lru_i, lru_v = (xbcT[:, 4 * i:4 * i + 4, :] for i in range(3))
        lru_a, lru_u = hT[:, 0:4, :], hT[:, 4:8, :]
        tmp = sb("tmp", [512], stack=mix)
        sqj = yT[:, :, :].rearrange("p (i k) t -> p i (k t)", k=4)
        mix.close()
        moe = ExitStack()
        xhi = sb("xhi", [KD, T], fp32r, moe)
        xlo = sb("xlo", [KD, T], fp32r, moe)
        h2T = sb("h2T", [KD, T], stack=moe)
        before = ExitStack()
        xn2 = sb("xn2", [TT, D], stack=before)
        before.close()
        whi = [sb(f"whi{i}", [2048], fp32r, moe) for i in range(3)]
        wlo = [sb(f"wlo{i}", [2048], fp32r, moe) for i in range(3)]
        hTh = sb("hTh", [2, T], fp32r, moe)
        hTl = sb("hTl", [2, T], fp32r, moe)
        sg = sb("sg", [TT, DE], stack=moe)
        h = sb("h", [TT, DE], stack=moe)
        rw = sb("rw", [KD, E], stack=moe)
        sc = sb("sc", [TT, E], stack=moe)
        sel = sb("sel", [TT, E], stack=moe)
        rep = sb("rep", [TT, E], stack=moe)
        chosen = sb("chosen", [TT, E], stack=moe)
        wts = sb("wts", [TT, E + 2], stack=moe)
        place = sb("place", [TT, E + 2], stack=moe)
        place2 = sb("place2", [TT, E + 2], stack=moe)
        counts = sb("counts", [E + 2], stack=moe)
        over = sb("over", [1], uint32, moe)
        xth = sb("xth", [TT, D], fp32r, moe)
        xtl = sb("xtl", [TT, D], fp32r, moe)
        pick = sb("pick", [TT, SLOTS], fp32r, moe)
        put = sb("put", [T], fp32r, moe)
        hhi = sb("hhi", [DE], fp32r, moe)
        hlo = sb("hlo", [DE], fp32r, moe)
        wslot = sb("wslot", [1], stack=moe)
        m8 = sb("m8", [TT, 8, 8], stack=moe)
        gsc = sb("gsc", [TT, 8], stack=moe)
        cmp_ = sb("cmp", [2, TT * 64], stack=moe)
        gm = sb("gm", [2, TT, 8], stack=moe)
        t8 = sb("t8", [TT, 8], stack=moe)
        wsum = sb("wsum", [2, TT], stack=moe)
        tmp2 = sg[:, :, :].rearrange("p t c -> p (t c)")
        xeh, xel = xhi[:, :, 0:SLOTS], xlo[:, :, 0:SLOTS]
        moe.close()
        fin = ExitStack()
        fnw = sb("fnw", [D], stack=fin)
        xo = sb("xo", [TT, D], stack=fin)
        fin.close()

        pb = [ctx.enter_context(nc.psum_tensor(f"pb{i}", [P, 512], fp32)) for i in range(8)]

        full = [sem(f"slot_full{i}") for i in range(RING)]
        pe_unit = sem("pe_unit")
        x_lo = [sem(f"x_lo{j}") for j in range(3)]
        slots_taken = sem("slots_taken")
        layer_done = sem("layer_done")
        ada_full = [sem(f"ada_full{i}") for i in range(ADA_BUFS)]
        first_in = [sem(f"first_in{i}") for i in range(3)]
        ada_zero = sem("ada_zero")
        ada_bias = sem("ada_bias")
        ada_prod = sem("ada_prod")
        ada_sum = sem("ada_sum")
        ada_taken = sem("ada_taken")
        params_in = sem("params_in")
        const_in = sem("const_in")
        silu_c = sem("silu_c")
        out_sem = sem("out_stored")
        eps_ready = sem("eps_ready")
        fin_sq = sem("fin_sq")
        fin_dve = sem("fin_dve")

        S = {n: sem(n) for n in SIGNALS}

        def ring_unit(u):
            return ring[:, slot_of(u), :]

        def wait_unit(eng, l, u, it=0):
            eng.wait_ge(full[slot_of(u)], l * per_layer(slot_of(u)) + filled(u) + it * weight_of(u))

        def wait_pe_unit(eng, l, u):
            eng.wait_ge(pe_unit, l * N_PE + u + 1)

        def wait_split(eng, l, j, n):
            eng.wait_ge(x_lo[j], l * N_X + (N_X + 1) + n)

        def overflow_pass(eng, l, expert, after=None):
            eng.wait_ge(S["over"], 1)
            flag = eng.value_load(over[0:1, 0:1], min_val=0, max_val=1)
            with eng.If(flag > 0):
                with eng.Fori(0, E) as e:
                    expert(l, e)
                if after:
                    after()

        block = ctx.enter_context(nc.Block())

        @block.sync
        def _(sp):
            w_in = a["w_in"].rearrange("l (p k) n -> l p k n", p=P)
            w_out = a["w_out"].rearrange("l (k p) n -> l p k n", p=P)
            gate_w, up_w = (a[n].rearrange("l e (p k) n -> (l e) p (k n)", p=P) for n in ("exp_gate", "exp_up"))
            down_w = a["exp_down"].rearrange("l e (k p) n -> (l e) p k n", p=P)
            sh_g, sh_u = (a[n].rearrange("l (p k) n -> l p (k n)", p=P) for n in ("sh_gate", "sh_up"))
            sh_d = a["sh_down"].rearrange("l (k p) n -> l p k n", p=P)

            def slot_free(l, u, it=0):
                q = u - RING
                while q in PADS:
                    q -= RING
                before = l
                if q < 0:
                    q, before = q + UNITS, l - 1
                if not isinstance(it, int):
                    n, j = divmod(u - U_MOE, 3)
                    wait_split(sp, l, j, X_IT * it + (n - X_IT))
                elif q < N_PE:
                    wait_pe_unit(sp, l, q)
                else:
                    n, j = divmod(q - U_MOE, 3)
                    wait_split(sp, before, j, n)
                sp.sem_inc(slots_taken, 1)

            def pair_unit(l, u, src):
                slot_free(l, u)
                sp.dma_start(ring_unit(u).rearrange("p (k c) -> p k c", k=2), src).then_inc(full[slot_of(u)], 16)

            def expert_units(l, n, it, g, up, down):
                u = U_MOE + 3 * n
                for half in range(2):
                    slot_free(l, u + half, it)
                    dst, c = ring_unit(u + half), 1024 * half
                    sp.dma_start(dst[:, 0:1024], g[:, c:c + 1024]).then_inc(full[slot_of(u + half)], 16)
                    sp.dma_start(dst[:, 1024:2048], up[:, c:c + 1024]).then_inc(full[slot_of(u + half)], 16)
                slot_free(l, u + 2, it)
                sp.dma_start(ring_unit(u + 2).rearrange("p (k c) -> p k c", k=2),
                             down).then_inc(full[slot_of(u + 2)], 16)

            def routed(l, n, it=0):
                e = l * E + X_IT * it + (n - 1)
                expert_units(l, n, it, gate_w[e], up_w[e], down_w[e])

            def overflow_loads(l, e):
                sp.wait_ge(S["over_x"], 4 * e + 4)
                sp.sem_inc(slots_taken, 1)
                ex = l * E + e
                for half in range(2):
                    c = 1024 * half
                    sp.dma_start(ring[:, half, 0:1024], gate_w[ex][:, c:c + 1024]).then_inc(S["over_full"], 16)
                    sp.dma_start(ring[:, half, 1024:2048], up_w[ex][:, c:c + 1024]).then_inc(S["over_full"], 16)
                sp.dma_start(ring[:, 2, :].rearrange("p (k c) -> p k c", k=2), down_w[ex]).then_inc(S["over_full"], 16)

            def overflow_loaded():
                sp.wait_ge(S["over_full"], 16 * 5 * E)
                sp.wait_ge(S["over_x"], 4 * E + 4)

            ada_l0 = a["ada_w"][0].rearrange("(p k) (g c) -> g p k c", p=P, g=6)
            for part in range(3):
                if part == 2:
                    sp.wait_ge(ada_sum, KD)
                for k in range(0, KD, 2):
                    sp.dma_start(ada_first[:, part % 2, k:k + 2, :], ada_l0[part, :, k:k + 2, :]).then_inc(first_in[part], 16)
            for j in range(3):
                sp.sem_inc(x_lo[j], N_X)
            with sp.Fori(0, L) as l:
                for i, c in enumerate(W_COLS):
                    n = SSD_HEADS if c == C_DT else 256
                    slot_free(l, U_W + i)
                    sp.dma_start(ring_unit(U_W + i)[:, 0:KD * n].rearrange("p (k c) -> p k c", k=KD),
                                 w_in[l, :, :, c:c + n]).then_inc(full[slot_of(U_W + i)], 16)
                for i in range(8):
                    pair_unit(l, U_OUT + i, w_out[l, :, 2 * i:2 * i + 2, :])
                expert_units(l, 0, 0, sh_g[l], sh_u[l], sh_d[l])
                for n in range(1, X_IT + 1):
                    routed(l, n)
                with sp.Fori(1, N_IT) as it:
                    for n in range(1, X_IT + 1):
                        routed(l, n, it)
                for n in range(LAST, E + 1):
                    routed(l, n)
                overflow_pass(sp, l, overflow_loads, overflow_loaded)
                sp.sem_inc(S["end_sp"], 1)
            sp.wait_ge(fin_dve, 5)
            sp.dma_start(out.rearrange("b (t p) d -> p (b t) d", p=P), xo[:, :, :]).then_inc(out_sem, 16)
            sp.wait_ge(out_sem, 16)

        @block.scalar
        def _(act):
            A = nc.scalar.activation
            for i, t in enumerate((ident, tri, neg, ones)):
                act.dma_start(t[:, :], a["consts"][:, P * i:P * i + P]).then_inc(const_in, 16)
            act.dma_start(lt8[:, :], a["consts"][:, 4 * P:4 * P + 64]).then_inc(const_in, 16)
            act.dma_start(iota[:, :], a["consts"][:, 4 * P + 64:5 * P + 64]).then_inc(const_in, 16)
            act.dma_start(masks[:, :, :], a["masks"].rearrange("p (l t) -> p l t", l=LEVELS)).then_inc(const_in, 16)
            act.dma_start(craw[:, :], a["c"].rearrange("b (p k) -> (b p) k", p=P)).then_inc(const_in, 16)
            act.dma_start(x[:, :, :], a["x"].rearrange("b (t p) d -> p (b t) d", p=P)).then_inc(const_in, 16)
            act.wait_ge(const_in, 16 * 9)
            A(cact[:, :], craw[:, :], ACT.Silu).then_inc(silu_c, 1)

            def small_params(l):
                rows = [(R_CW, 48, a["ssd_conv_w"][l].rearrange("w (c p) -> (w c) p", p=P)),
                        (R_CB, 12, a["ssd_conv_b"][l].rearrange("(c p) -> c p", p=P)),
                        (R_LCW, 16, a["lru_conv_w"][l].rearrange("w (c p) -> (w c) p", p=P))]
                rows += [(r, n, a[k][l].rearrange("(c p) -> c p", p=P)) for r, n, k in (
                    (R_LCB, 4, "lru_conv_b"), (R_BA, 4, "lru_ba"), (R_BX, 4, "lru_bx"), (R_LAM, 4, "lru_lambda"),
                    (R_LNW, 4, "lru_norm_w"), (R_HNW, 4, "hg_norm_w"), (R_SNW, 8, "ssd_norm_w"))]
                rows.append((R_LB, 4 * L, a["hg_lower_bounds"].rearrange("l (c p) -> (l c) p", p=P)))
                for r, n, src in rows:
                    act.dma_start(prow[r:r + n, l, :], src).then_inc(params_in, 16)
                for i, k in enumerate(("norm_mix_w", "norm_ffn_w")):
                    act.dma_start(pall[:, l, KD * i:KD * i + KD],
                                  a[k][l].rearrange("(p k) -> p k", p=P)).then_inc(params_in, 16)
                for i, k in enumerate(("ssd_dt_bias", "ssd_a_log", "ssd_d")):
                    c = 2 * KD + SSD_HEADS * i
                    act.dma_start(pall[:, l, c:c + SSD_HEADS], a[k][l].partition_broadcast(P)).then_inc(params_in, 16)
                act.dma_start(pall[:, l, P - E:P], a["router_bias"][l].partition_broadcast(P)).then_inc(params_in, 16)

            def block_weights(l):
                act.wait_ge(S["bd_zero"], 1)
                for i, k in enumerate(("lru_wa", "lru_wx")):
                    w = a[k][l].rearrange("(j b) i o -> b i j o", b=2)
                    for b in range(2):
                        act.dma_start(bd[64 * b:64 * b + 64, i, :, 64 * b:64 * b + 64], w[b]).then_inc(S["bd_in"], 16)

            def rms(src, done):
                for t in range(TT):
                    A(sqj[:, t, :], src[:, t, :], ACT.Square, accum_out=ss[:, t:t + 1]).then_inc(done, 1)
                act.wait_ge(done, TT)
                A(ss[:, 2:4], ss[:, 0:2], ACT.Sqrt, scale=1.0 / D, bias=eps[:, :]).then_inc(done, 1)

            def split_hi(l, j, n, n0, it):
                wait_unit(act, l, U_MOE + 3 * n0 + j, it)
                if not (isinstance(n, int) and n == 0):
                    act.wait_ge(S[f"x_used{j}"], n)
                A(whi[j][:, :], ring_unit(U_MOE + 3 * n0 + j), ACT.Copy).then_inc(S[f"x_hi{j}"], 1)

            def silu_gate(n, tiles=1):
                act.wait_ge(S["x_used1"], n + 1)
                for t in range(tiles):
                    A(sg[:, t, :], pb[4 + t][:, 0:DE], ACT.Silu).then_inc(S["silu_g"], 1)

            def tokens_hi(n, half):
                act.wait_ge(S["gathered"], 2 * (n - 1) + half + 1)
                A(xeh[:, 4 * half:4 * half + 4, :], pb[5][:, :].rearrange("p (k s) -> p k s", k=4),
                  ACT.Copy).then_inc(S["xe_hi"], 1)

            def put_copy(n):
                act.wait_ge(S["pick_turned"], n)
                if not isinstance(n, int) or n > 1:
                    act.wait_ge(S["h_spread"], n)
                A(put[:, :], pb[7][:, 0:T], ACT.Copy).then_inc(S["put_ready"], 1)

            def row_hi(n):
                act.wait_ge(S["h_ready"], TT + n)
                A(hhi[:, :], h[:, 0, :], ACT.Copy).then_inc(S["row_hi"], 1)

            def hidden_hi(n):
                act.wait_ge(S["h_spread"], n + 1)
                A(hTh[:, :, :], pb[6][:, :].rearrange("p (k t) -> p k t", k=2), ACT.Copy).then_inc(S["h_hi"], 1)

            for l in range(L):
                small_params(l)
            act.wait_ge(eps_ready, 1)
            with act.Fori(0, L) as l:
                block_weights(l)
                rms(x, S["ss_mix"])
                def from_unit(i, dst, func, **kw):
                    wait_pe_unit(act, l, U_W + i)
                    return A(dst, pb[i % W_BANKS][:, :], func, **kw)

                for i in range(6):
                    act.wait_ge(S["conv"], 2 * i + 2)
                    A(xbcT[:, 2 * i:2 * i + 2, :], xbcT[:, 2 * i:2 * i + 2, :], ACT.Silu).then_inc(S["xbc_ready"], 1)
                act.wait_ge(S["dt_in"], 2)
                A(dts[:, 1, :], dts[:, 1, :], ACT.Exp).then_inc(S["dt_exp"], 1)
                act.wait_ge(S["pnow"], 1)
                A(hb[:, 1, :], hb[:, 1, :], ACT.Exp).then_inc(S["dt_exp"], 1)
                act.wait_ge(S["lb_in"], L)
                A(lbs[:, :, :], lbs[:, :, :], ACT.Exp).then_inc(S["lb_exp"], 1)
                act.wait_ge(S["lam_in"], 1)
                A(lruc[:, 1, :], lruc[:, 0, :], ACT.Exp).then_inc(S["lam_exp"], 1)
                act.wait_ge(S["dt_exp"], 2)
                A(dts[:, 1, :], dts[:, 1, :], ACT.Ln, bias=1.0).then_inc(S["dt_exp"], 1)
                act.wait_ge(S["lam_exp"], 1)
                A(lruc[:, 1, :], lruc[:, 1, :], ACT.Ln, bias=1.0).then_inc(S["lam_exp"], 1)
                for i in range(2):
                    from_unit(W_HF + i, qkg[:, 1, 2 * i:2 * i + 2, :], ACT.Sigmoid, scale=-1.0).then_inc(S["w_act"], 1)
                for i in range(2):
                    from_unit(W_HQ + i, qkg[:, 0, 2 * i:2 * i + 2, :], ACT.Silu).then_inc(S["w_act"], 1)
                act.wait_ge(S["dec_in"], 1)
                A(dts[:, 0, :], dts[:, 4, :], ACT.Exp).then_inc(S["eacum"], 1)
                A(dts[:, 5, :], dts[:, 5, :], ACT.Exp).then_inc(S["dec"], 1)
                act.wait_ge(S["cb_done"], 1)
                A(cb[:, :, :], pb[4][:, :], ACT.Copy).then_inc(S["cb_ready"], 1)
                act.wait_ge(S["btok_done"], 1)
                A(btok[:, :, :], pb[5][:, 0:2 * P], ACT.Copy).then_inc(S["btok_ready"], 1)
                for i in range(4):
                    act.wait_ge(S["xs_turned"], i + 1)
                    A(xh[:, i // 2, 512 * (i % 2):512 * (i % 2) + 512], pb[(6, 7, 4, 5)[i]][:, :],
                      ACT.Copy).then_inc(S["xh_ready"], 1)
                for i in range(4):
                    wait_pe_unit(act, l, U_W + W_Z + i)
                    A(z[:, :, 256 * i:256 * i + 256], pb[(W_Z + i) % W_BANKS][:, :].rearrange("p (t c) -> p t c", t=TT),
                      ACT.Silu).then_inc(S["w_act"], 1)
                for g in range(2):
                    act.wait_ge(S["st_done"], g + 1)
                    A(stT[:, g, :], pb[3][:, :], ACT.Copy).then_inc(S["st_ready"], 1)
                for q in range(8):
                    act.wait_ge(S["diff_sub"], q + 1)
                    A(mdec[:, q % 2, :, :], mdec[:, q % 2, :, :], ACT.Exp).then_inc(S["diff_exp"], 1)
                act.wait_ge(S["y_gated"], 2)
                for i in range(4):
                    half = slice(512 * (i % 2), 512 * (i % 2) + 512)
                    A(xh[:, i // 2, half], y[:, i // 2, half], ACT.Square,
                      accum_out=ss[:, i:i + 1]).then_inc(S["y_sq"], 1)
                act.wait_ge(S["y_sq"], 4)
                A(ss[:, :], ss[:, :], ACT.Sqrt, scale=1.0 / 512, bias=eps[:, :]).then_inc(S["y_sq"], 1)
                act.wait_ge(S["k_ready"], 1)
                act.wait_ge(S["st_done"], 2)
                A(bT, qkg[:, 1, :, :], ACT.Ln, scale=-1.0, bias=1.0).then_inc(S["logf"], 1)

                def decay(i):
                    act.wait_ge(S["lev_in"], 2 * i)
                    A(lev_e[i % 2], lev_e[i % 2], ACT.Exp).then_inc(S["lev_exp"], 1)

                for i in range(6):
                    decay(i + 1)
                    k = i % 2
                    if i < 2:
                        wait_pe_unit(act, l, U_W + W_HV + k)
                        A(v[:, :, 256 * k:256 * k + 256],
                          pb[(W_HV + k) % W_BANKS][:, :].rearrange("p (t c) -> p t c", t=TT),
                          ACT.Copy).then_inc(S["w_act"], 1)
                    elif i < 4:
                        from_unit(W_LG + k, lru_g[:, 2 * k:2 * k + 2, :], ACT.Gelu_apprx_tanh).then_inc(S["w_act"], 1)
                    else:
                        from_unit(W_HG + k, qkg[:, 2, 2 * k:2 * k + 2, :], ACT.Silu).then_inc(S["w_act"], 1)
                decay(LEVELS - 1)
                act.wait_ge(S["gate_mm"], 1)
                for k, dst, r in ((0, lru_r, R_BA), (1, lru_i, R_BX)):
                    for j in range(LRU_J):
                        A(dst[:, j, :], pb[2 * k + j // 2][:, T * (j % 2):T * (j % 2) + T], ACT.Sigmoid,
                          bias=pcol[:, r + j:r + j + 1]).then_inc(S["gate_sig"], 1)
                decay(LEVELS)
                act.wait_ge(S["gate_sig"], 8)
                act.wait_ge(S["lruc_ready"], 1)
                for j in range(LRU_J):
                    A(lru_v[:, j, :], lru_r[:, j, :], ACT.Tanh, scale=lruc[:, 2, j:j + 1]).then_inc(S["lru_tanh"], 1)
                act.wait_ge(S["cross_done"], 1)
                A(cross, pb[4][:, :], ACT.Copy).then_inc(S["cross_ready"], 1)
                for j in range(LRU_J):
                    A(lru_a[:, j, :], lru_r[:, j, :], ACT.Exp, scale=lruc[:, 3, j:j + 1]).then_inc(S["lru_exp"], 1)
                act.wait_ge(S["o_done"], 1)
                for i in range(2):
                    A(lev_e[0][:, 2 * i:2 * i + 2, :], pb[4 + i][:, :], ACT.Square).then_inc(S["o_sq"], 1)
                act.wait_ge(S["lru_w"], 1)
                A(lru_u, lru_u, ACT.Sqrt).then_inc(S["lru_sqrt"], 1)
                act.wait_ge(S["o_sum"], 1)
                for i in range(2):
                    A(lev_e[1][:, 2 * i:2 * i + 2, :], pb[6 + i][:, :], ACT.Sqrt, scale=1.0 / P,
                      bias=eps[:, :]).then_inc(S["o_root"], 1)
                act.wait_ge(S["lru_y"], 1)
                A(lru_v, lru_r, ACT.Square).then_inc(S["lru_sq"], 1)
                act.wait_ge(S["lru_sum"], 1)
                A(tmp[:, 0:T], pb[4][:, 0:T], ACT.Sqrt, scale=1.0 / 512, bias=eps[:, :]).then_inc(S["lru_root"], 1)

                act.wait_ge(S["x_mid"], 4)
                act.dma_start(rw[:, :, :], a["router_w"][l].rearrange("(p k) e -> p k e", p=P)).then_inc(S["router_in"], 16)
                rms2 = S["ss_ffn"]
                for t in range(TT):
                    A(xn2[:, t, :], x[:, t, :], ACT.Square, accum_out=ss[:, t:t + 1]).then_inc(rms2, 1)
                act.wait_ge(rms2, TT)
                A(ss[:, 2:4], ss[:, 0:2], ACT.Sqrt, scale=1.0 / D, bias=eps[:, :]).then_inc(rms2, 1)
                for j in range(4):
                    act.wait_ge(S["h2_ready"], 2 * j + 2)
                    A(xhi[:, 2 * j:2 * j + 2, :], h2T[:, 2 * j:2 * j + 2, :], ACT.Copy).then_inc(S["x_hi"], 1)
                act.wait_ge(S["logits"], 1)
                A(sc[:, :, :], pb[7][:, 0:TT * E], ACT.Sigmoid).then_inc(S["scores"], 1)
                for j in range(4):
                    act.wait_ge(S["rows_turned"], j + 1)
                    A(xth[:, j // 2, 512 * (j % 2):512 * (j % 2) + 512], pb[j][:, :], ACT.Copy).then_inc(S["xt_hi"], 1)
                split_hi(l, 0, 0, 0, 0)
                split_hi(l, 1, 0, 0, 0)
                split_hi(l, 0, 1, 1, 0)
                silu_gate(0, TT)
                tokens_hi(1, 0)
                tokens_hi(1, 1)
                split_hi(l, 1, 1, 1, 0)

                def expert_step(n, n0, it, last=False):
                    split_hi(l, 2, n - 1, n0 - 1, it)
                    hidden_hi(n - 1)
                    if not last:
                        tokens_hi(n + 1, 0)
                    put_copy(n)
                    if not last:
                        split_hi(l, 0, n + 1, n0 + 1, it)
                    silu_gate(n)
                    if not last:
                        tokens_hi(n + 1, 1)
                    row_hi(n)
                    if not last:
                        split_hi(l, 1, n + 1, n0 + 1, it)

                for r in range(X_IT):
                    expert_step(1 + r, 1 + r, 0)
                with act.Fori(1, N_IT) as it:
                    for r in range(X_IT):
                        expert_step(X_IT * it + 1 + r, 1 + r, it)
                for n in range(LAST, E + 1):
                    expert_step(n, n, 0, last=n == E)
                split_hi(l, 2, E, E, 0)
                hidden_hi(E)

                def overflow(l, e):
                    act.wait_ge(S["over_pe"], 5 * e + 2)
                    for half in range(2):
                        A(h2T[:, 4 * half:4 * half + 4, 0:SLOTS], pb[(5, 7)[half]][:, :].rearrange("p (k s) -> p k s", k=4),
                          ACT.Copy).then_inc(S["over_act"], 1)
                    act.wait_ge(S["over_pe"], 5 * e + 3)
                    act.wait_ge(S["over_dve"], 3 * e + 1)
                    A(put[:, :], pb[6][:, 0:T], ACT.Copy).then_inc(S["over_act"], 1)
                    act.wait_ge(S["over_pe"], 5 * e + 4)
                    A(sg[:, 0, :], pb[4][:, 0:DE], ACT.Silu).then_inc(S["over_act"], 1)

                overflow_pass(act, l, overflow)
                act.sem_inc(S["end_act"], 1)
                act.wait_ge(layer_done, l + 1)

            act.dma_start(fnw[:, :], a["final_norm_w"].partition_broadcast(P)).then_inc(const_in, 16)
            for t in range(TT):
                A(xo[:, t, :], x[:, t, :], ACT.Square, accum_out=ss[:, t:t + 1]).then_inc(fin_sq, 1)
            act.wait_ge(fin_sq, TT)
            A(ss[:, 2:4], ss[:, 0:2], ACT.Sqrt, scale=1.0 / D, bias=eps[:, :]).then_inc(fin_sq, 1)

        @block.gpsimd
        def _(pool):
            G = nc.gpsimd
            w = a["ada_w"].rearrange("l (p k) (g c) -> l g p k c", p=P, g=6)
            bias = a["ada_b"].rearrange("l (i c) -> (l i) c", i=2)

            def load(l, i, v):
                pool.dma_start(ada_w[:, v % ADA_BUFS, :],
                               w[l, 3 * i + v // KD, :, v % KD, :]).then_inc(ada_full[v % ADA_BUFS], 16)

            def clear_sums(b):
                G.memset(ada_acc[:, :, :], 0.0).then_inc(ada_zero, 1)
                pool.wait_ge(ada_zero, b + 1)
                pool.dma_start(ada_acc[0:1, :, :].rearrange("o g c -> o (g c)"), bias[b:b + 1, :] if isinstance(b, int)
                               else bias[bass.ds(b, 1), :]).then_inc(ada_bias, 16)

            def ada_block(l, i, last=False):
                b = 2 * l + i
                pool.wait_ge(ada_taken, b)
                clear_sums(b)
                done = ADA_STEPS * (b - 1)
                for v in range(ADA_STEPS):
                    part, k, buf = v // KD, v % KD, ada_w[:, v % ADA_BUFS, :]
                    pool.wait_ge(ada_full[v % ADA_BUFS],
                                 16 * (ADA_STEPS // ADA_BUFS * (b - 1) + v // ADA_BUFS + 1))
                    G.tensor_scalar(buf, buf, cact[:, k:k + 1], None, ALU.mult).then_inc(ada_prod, 1)
                    pool.wait_ge(ada_prod, done + v + 1)
                    if v == 0:
                        pool.wait_ge(ada_bias, 16 * b + 16)
                    if v % KD:
                        pool.wait_ge(ada_sum, ADA_STEPS * b + v)
                    G.tensor_tensor(ada_acc[:, part, :], ada_acc[:, part, :], buf, ALU.add).then_inc(ada_sum, 1)
                    nxt = v + ADA_BUFS
                    if nxt < ADA_STEPS or not last:
                        pool.wait_ge(ada_sum, ADA_STEPS * b + v + 1)
                        nl, ni = (l, i) if nxt < ADA_STEPS else (l, 1) if i == 0 else (l + 1, 0)
                        load(nl, ni, nxt % ADA_STEPS)

            clear_sums(0)
            pool.wait_ge(ada_sum, ADA_STEPS)
            for v in range(ADA_BUFS):
                load(0, 1, v)
            pool.wait_ge(silu_c, 1)
            with pool.Fori(1, L) as l:
                ada_block(l - 1, 1)
                ada_block(l, 0)
            ada_block(L - 1, 1, last=True)

        @block.vector
        def _(dve):
            V = nc.vector
            order = [0]

            def link(ins):
                order[0] += 1
                ins.then_inc(S["dve_order"], 1)
                dve.wait_ge(S["dve_order"], order[0])

            def own(ins, s, value):
                ins.then_inc(s, 1)
                dve.wait_ge(s, value)

            def normed(src, dst, root, ready):
                dve.wait_ge(root, TT + 1)
                link(V.reciprocal(rstd[:, :], ss[:, 2:4]))
                for t in range(TT):
                    V.tensor_scalar(dst[:, t, :], src[:, t, :], rstd[:, t:t + 1], None, ALU.mult).then_inc(ready, 1)

            def modulation(i, bank):
                dve.wait_ge(S["ada_cols"], i + 1)
                V.tensor_copy(modc[:, i, 1, :], bank[:, 0:KD]).then_inc(S["modc_s"], 1)
                own(V.scalar_tensor_tensor(modc[:, i, 0, :], bank[:, KD:2 * KD], 1.0, norm_w[:, i, :], ALU.add, ALU.mult),
                    S["modc"], i + 1)
                dve.wait_ge(S["modc_s"], i + 1)

            def conv(i, dst, w_row, chunks, b_row, done):
                for s in range(4):
                    for c in range(2):
                        ch = chunks + c
                        src = pb[i % W_BANKS][:, T * c:T * c + T]
                        acc = dst[:, ch, :]
                        wc = w_row[0] + w_row[1] * (3 - s) + ch
                        w = pcol[:, wc:wc + 1]
                        if s == 0:
                            ins = V.tensor_scalar(acc, src, w, pcol[:, b_row + ch:b_row + ch + 1], ALU.mult, ALU.add)
                        else:
                            ins = V.scalar_tensor_tensor(acc[:, s:T], src[:, 0:T - s], w, acc[:, s:T], ALU.mult, ALU.add)
                        if s < 3:
                            order[0] += 1
                            ins.then_inc(S["dve_order"], 1)
                        else:
                            ins.then_inc(done, 1)
                    if s < 3:
                        dve.wait_ge(S["dve_order"], order[0])

            def split_lo(l, j, n, n0, it):
                dve.wait_ge(S[f"x_hi{j}"], n + 1)
                V.tensor_tensor(wlo[j][:, :], ring_unit(U_MOE + 3 * n0 + j), whi[j][:, :].bitcast(fp32),
                                ALU.subtract).then_inc(x_lo[j], 1)

            def hidden(n):
                dve.wait_ge(S["silu_g"], n + TT)
                dve.wait_ge(S["wslot"], n)
                V.scalar_tensor_tensor(h[:, 0, :], sg[:, 0, :], wslot[:, 0:1], pb[4][:, DE:2 * DE],
                                       ALU.mult, ALU.mult).then_inc(S["h_ready"], 1)

            def row_lo(n):
                dve.wait_ge(S["row_hi"], n)
                dve.wait_ge(S["h_ready"], TT + n)
                V.tensor_tensor(hlo[:, :], h[:, 0, :], hhi[:, :].bitcast(fp32), ALU.subtract).then_inc(S["row_lo"], 1)

            def tokens_lo(n, half):
                dve.wait_ge(S["xe_hi"], 2 * (n - 1) + half + 1)
                V.tensor_tensor(xel[:, 4 * half:4 * half + 4, :], pb[5][:, :].rearrange("p (k s) -> p k s", k=4),
                                xeh[:, 4 * half:4 * half + 4, :].bitcast(fp32), ALU.subtract).then_inc(S["xe_lo"], 1)

            def column(tile, t, n):
                return tile[:, t, n:n + 1] if isinstance(n, int) else tile[:, t, bass.ds(n, 1)]

            def make_pick(n):
                if not isinstance(n, int) or n > 1:
                    dve.wait_ge(S["pick_turned"], n - 1)
                for t in range(TT):
                    V.tensor_scalar(pick[:, t, :], iota[:, :], column(place, t, n), None, ALU.is_equal).then_inc(S["pick"], 1)

            def slot_weights(n):
                dve.wait_ge(S["pick_turned"], n)
                dve.wait_ge(S["h_ready"], TT + n - 1)
                V.tensor_copy(wslot[:, :], pb[7][:, T:T + 1]).then_inc(S["wslot"], 1)

            def hidden_lo(n):
                dve.wait_ge(S["h_hi"], n + 1)
                V.tensor_tensor(hTl[:, :, :], pb[6][:, :].rearrange("p (k t) -> p k t", k=2), hTh[:, :, :].bitcast(fp32),
                                ALU.subtract).then_inc(S["h_lo"], 1)

            V.memset(eps[:, :], EPS).then_inc(eps_ready, 1)
            dve.wait_ge(const_in, 16 * 9)
            dve.wait_ge(silu_c, 1)
            dve.wait_ge(ada_bias, 16)
            for v in range(ADA_STEPS):
                part, k = divmod(v, KD)
                if k == 0:
                    dve.wait_ge(first_in[part], 64)
                V.scalar_tensor_tensor(ada_acc[:, part, :], ada_first[:, part % 2, k, :], cact[:, k:k + 1],
                                       ada_acc[:, part, :], ALU.mult, ALU.add).then_inc(ada_sum, 1)
                dve.wait_ge(ada_sum, v + 1)
            dve.wait_ge(params_in, 16 * 17 * L)
            with dve.Fori(0, L) as l:
                order[0] = 0
                V.memset(bd[:, :, :, :], 0.0).then_inc(S["bd_zero"], 1)
                V.tensor_copy(prow_now[0:R_END, :],
                              prow[0:R_END, bass.ds(l, 1), :].rearrange("r l p -> r (l p)")).then_inc(S["prow_ready"], 1)
                dve.wait_ge(S["params_turned"], 1)
                own(V.tensor_copy(pcol[:, :], pb[1][:, 0:R_END]), S["pcol"], 1)
                own(V.tensor_copy(pnow[:, :], pall[:, bass.ds(l, 1), :].rearrange("p l c -> p (l c)")), S["pnow"], 1)
                modulation(0, pb[0])
                normed(x, xn, S["ss_mix"], S["xn_ready"])
                for kk in range(KD):
                    dve.wait_ge(S["h_chunks"], kk // 2 + 1)
                    V.tensor_scalar(hT[:, kk, :], pb[4 + kk // 2][:, T * (kk % 2):T * (kk % 2) + T],
                                    modc[:, 0, 0, kk:kk + 1], modc[:, 0, 1, kk:kk + 1], ALU.mult,
                                    ALU.add).then_inc(S["hT_ready"], 1)
                dve.wait_ge(ada_taken, 2 * l + 1)
                for i in range(2):
                    V.tensor_copy(gates[:, 0, 512 * i:512 * i + 512], pb[2 + i][:, :]).then_inc(S["gates_m"], 1)

                lb = pcol[:, R_LB:R_LB + L * HG_H].rearrange("p (l h) -> p l h", l=L)
                link(V.tensor_copy(lbt[:, 0, :], lb[:, 0, :]))
                for i in range(1, L):
                    link(V.tensor_tensor(lbt[:, 0, :], lbt[:, 0, :], lb[:, i, :], ALU.max))
                for i in range(L):
                    V.tensor_tensor(lbs[:, i, :], lb[:, i, :], lbt[:, 0, :], ALU.subtract).then_inc(S["lb_in"], 1)
                lam = pcol[:, R_LAM:R_LAM + LRU_J]
                V.scalar_tensor_tensor(lruc[:, 0, :], lam, -1.0, lam, ALU.mult, ALU.min).then_inc(S["lam_in"], 1)

                for i in range(6):
                    wait_pe_unit(dve, l, U_W + i)
                    conv(i, xbcT, (R_CW, CH_XBC), 2 * i, R_CB, S["conv"])
                wait_pe_unit(dve, l, U_W + W_DT)
                s2 = lambda i: dts[:, i, :].rearrange("p (t h) -> p t h", t=TT)
                own(V.tensor_tensor(s2(0), pb[W_DT % W_BANKS][:, 0:32].rearrange("p (t h) -> p t h", t=TT),
                                    bcast(hb[:, 0, :], 1, TT), ALU.add), S["dt_in"], 1)
                V.scalar_tensor_tensor(dts[:, 1, :], dts[:, 0, :], -1.0, dts[:, 0, :], ALU.mult,
                                       ALU.min).then_inc(S["dt_in"], 1)
                dve.wait_ge(S["lb_exp"], 1)
                link(V.tensor_copy(lbt[:, 1, :], lbs[:, 0, :]))
                link(V.tensor_copy(lbt[:, 2, :], lbs[:, 0, :]))
                for i in range(1, L):
                    link(V.tensor_tensor(lbt[:, 1, :], lbt[:, 1, :], lbs[:, i, :], ALU.add))
                link(V.reciprocal(lbt[:, 1, :], lbt[:, 1, :]))
                link(V.tensor_tensor(lbs[:, :, :], lbs[:, :, :], bcast(lbt[:, 1, :], 1, L), ALU.mult))
                link(V.tensor_copy(lbt[:, 2, :], lbs[:, 0, :]))
                for i in range(1, L):
                    link(V.tensor_tensor(lbs[:, i, :], lbs[:, i, :], lbs[:, i - 1, :], ALU.add))
                link(V.tensor_tensor(lbs[:, :, :], lbs[:, :, :], bcast(lbt[:, 2, :], 1, L), ALU.subtract))
                link(V.tensor_scalar(lbs[:, :, :], lbs[:, :, :], -1.0, 1.0, ALU.mult, ALU.add))
                link(V.tensor_copy(omlb[:, :], lbs[:, bass.ds(l, 1), :].rearrange("p l h -> p (l h)")))
                dve.wait_ge(S["lam_exp"], 2)
                link(V.tensor_scalar(lruc[:, 0, :], lam, -1.0, 0.0, ALU.mult, ALU.max))
                link(V.tensor_tensor(lruc[:, 1, :], lruc[:, 0, :], lruc[:, 1, :], ALU.add))
                link(V.tensor_scalar(lruc[:, 2, :], lruc[:, 1, :], 8.0, None, ALU.mult))
                V.tensor_scalar(lruc[:, 3, :], lruc[:, 1, :], -8.0, None, ALU.mult).then_inc(S["lruc_ready"], 1)
                dve.wait_ge(S["dt_exp"], 3)
                link(V.scalar_tensor_tensor(dts[:, 2, :], dts[:, 0, :], 0.0, dts[:, 1, :], ALU.max, ALU.add))
                V.scalar_tensor_tensor(s2(3), s2(2), -1.0, bcast(hb[:, 1, :], 1, TT), ALU.mult,
                                       ALU.mult).then_inc(S["a_ready"], 1)
                dve.wait_ge(S["acum_done"], 1)
                link(V.tensor_copy(dts[:, 4, :], pb[3][:, 0:32]))
                V.tensor_tensor(dts[:, 5, :], pb[3][:, 32:64], dts[:, 4, :], ALU.subtract).then_inc(S["dec_in"], 1)
                dve.wait_ge(S["w_act"], 2)
                V.tensor_tensor(qkg[:, 1, :, :], qkg[:, 1, :, :], bcast(omlb[:, :], 2, T), ALU.mult).then_inc(S["k_ready"], 1)
                heads = lambda ap: ap.rearrange("p (h d) -> p h d", d=SSD_HD)
                for c in range(2):
                    dve.wait_ge(S["xh_ready"], 2 * c + 2)
                    own(V.tensor_tensor(heads(xdt[:, c, :]), heads(xh[:, c, :]),
                                        bcast(dts[:, 2, 16 * c:16 * c + 16], 2, SSD_HD), ALU.mult), S["xdt_ready"], c + 1)
                    if c == 0:
                        dve.wait_ge(S["dec"], 1)
                        V.tensor_tensor(heads(xdec[:, :]), heads(xdt[:, 0, :]), bcast(dts[:, 5, 0:16], 2, SSD_HD),
                                        ALU.mult).then_inc(S["xdec_ready"], 1)
                    link(V.tensor_tensor(heads(y[:, c, :]), heads(xh[:, c, :]), bcast(hb[:, 2, :], 2, SSD_HD), ALU.mult))

                dve.wait_ge(S["cb_ready"], 1)

                def diff(q):
                    c, h0 = q // 4, 4 * (q % 4)
                    dve.wait_ge(S["diff_done"], q + 1)
                    if q >= 2:
                        dve.wait_ge(S["ydiag"], q - 1)
                    V.tensor_tensor(mdec[:, q % 2, :, :], pb[4 + q % 2][:, :].rearrange("p (h t) -> p h t", h=4),
                                    bcast(dts[:, 4, 16 * c + h0:16 * c + h0 + 4], 2, P), ALU.subtract).then_inc(S["diff_sub"], 1)

                def masked(q):
                    c, g = q // 4, (q % 4) // 2
                    dve.wait_ge(S["diff_exp"], q + 1)
                    V.tensor_tensor(mdec[:, q % 2, :, :], mdec[:, q % 2, :, :], bcast(cb[:, 2 * c + g, :], 1, 4),
                                    ALU.mult).then_inc(S["m_ready"], 1)

                def y_group(i):
                    c, g = divmod(i, 2)
                    part = y[:, c, 512 * g:512 * g + 512]
                    dve.wait_ge(S["ydiag"], 2 * i + 2)
                    own(V.tensor_tensor(part, part, pb[6 + i % 2][:, :], ALU.add), S["y_taken"], i + 1)
                    if c == 1:
                        dve.wait_ge(S["yoff"], g + 1)
                        dve.wait_ge(S["eacum"], 1)
                        own(V.tensor_tensor(heads(tmp[:, :]), heads(pb[3][:, :]),
                                            bcast(dts[:, 0, 16 + 8 * g:24 + 8 * g], 2, SSD_HD), ALU.mult), S["yoff_taken"], g + 1)
                        link(V.tensor_tensor(part, part, tmp[:, :], ALU.add))

                for q in range(9):
                    if q < 8:
                        diff(q)
                    if q:
                        masked(q - 1)
                    if q in (3, 5, 7):
                        y_group((q - 3) // 2)
                y_group(3)

                def conv_lx(i):
                    wait_pe_unit(dve, l, U_W + W_LX + i)
                    conv(W_LX + i, lru_x, (R_LCW, LRU_J), 2 * i, R_LCB, S["conv_lx"])

                dve.wait_ge(S["w_act"], 8)
                for c in range(2):
                    own(V.tensor_tensor(y[:, c, :], y[:, c, :], z[:, c, :], ALU.mult), S["y_gated"], c + 1)
                link(V.memset(attn, 0.0))
                dve.wait_ge(S["y_sq"], 5)
                link(V.reciprocal(ss[:, :], ss[:, :]))
                for i in range(4):
                    part = y[:, i // 2, 512 * (i % 2):512 * (i % 2) + 512]
                    V.tensor_scalar(part, part, ss[:, i:i + 1], None, ALU.mult).then_inc(S["y_norm"], 1)
                conv_lx(0)
                for i in range(4):
                    c, g = divmod(i, 2)
                    dve.wait_ge(S["y_turned"], i + 1)
                    V.tensor_tensor(yT[:, 4 * g:4 * g + 4, P * c:P * c + P],
                                    pb[4 + i][:, :].rearrange("p (k t) -> p k t", k=4),
                                    bcast(pcol[:, R_SNW + 4 * g:R_SNW + 4 * g + 4], 2, P), ALU.mult).then_inc(S["yT_ready"], 1)

                q_, k_, g_ = (qkg[:, i, :, :] for i in range(3))
                dve.wait_ge(S["logf"], 1)
                for hd in range(HG_H):
                    for t in range(TT):
                        seg = bT[:, hd, P * t:P * t + P]
                        order[0] += 1
                        V.tensor_tensor_scan(seg, ones[:, :], seg, 0.0, ALU.mult, ALU.add).then_inc(S["dve_order"], 1)
                dve.wait_ge(S["w_act"], 4)
                for i in range(2):
                    for src, buf in ((q_, lev_q), (k_, lev_k)):
                        order[0] += 1
                        V.tensor_copy(buf[i], src).then_inc(S["dve_order"], 1)
                dve.wait_ge(S["dve_order"], order[0])
                halves = lambda ap, m: ap.rearrange("p h (b s m) -> p (h b) s m", s=2, m=m)

                def level_in(i):
                    m = 1 << (i - 1)
                    e, b = halves(lev_e[i % 2], m), halves(bT, m)
                    r = b[:, :, 0, m - 1:m]
                    r = r.broadcast_to(list(r.shape[:2]) + [m])
                    if i >= 3:
                        dve.wait_ge(S["lev_ready"], 2 * (i - 2))
                    V.tensor_tensor(e[:, :, 1, :], b[:, :, 1, :], r, ALU.subtract).then_inc(S["lev_in"], 1)
                    V.tensor_tensor(e[:, :, 0, :], r, b[:, :, 0, :], ALU.subtract).then_inc(S["lev_in"], 1)

                def level_out(i):
                    m = 1 << (i - 1)
                    e, lq, lk = (halves(ap, m) for ap in (lev_e[i % 2], lev_q[i % 2], lev_k[i % 2]))
                    dve.wait_ge(S["lev_exp"], i)
                    if i >= 3:
                        dve.wait_ge(S["att_done"], i - 1)
                    V.tensor_tensor(lq[:, :, 1, :], halves(q_, m)[:, :, 1, :], e[:, :, 1, :], ALU.mult).then_inc(S["lev_ready"], 1)
                    V.tensor_tensor(lk[:, :, 0, :], halves(k_, m)[:, :, 0, :], e[:, :, 0, :], ALU.mult).then_inc(S["lev_ready"], 1)

                def take(i):
                    dve.wait_ge(S["att_done"], i + 1)
                    for j in range(2):
                        V.copy_predicated(attn[:, 4 * j:4 * j + 4, :], bcast(masks[:, i, :], 1, 4),
                                          pb[4 + 2 * (i % 2) + j][:, :].rearrange("p (g t) -> p g t", g=4)).then_inc(S["att_taken"], 1)

                e, lq, lk = lev_e[0], lev_q[0], lev_k[0]
                level_in(1)
                conv_lx(1)
                for i in range(1, LEVELS):
                    if i + 1 < LEVELS:
                        level_in(i + 1)
                    else:
                        r = bT[:, :, P - 1:P].broadcast_to([P, HG_H, P])
                        dve.wait_ge(S["lev_ready"], 2 * (LEVELS - 2))
                        V.tensor_copy(e[:, :, P:T], bT[:, :, P:T]).then_inc(S["lev_in"], 1)
                        V.tensor_tensor(e[:, :, 0:P], r, bT[:, :, 0:P], ALU.subtract).then_inc(S["lev_in"], 1)
                    take(i - 1)
                    level_out(i)
                take(LEVELS - 1)
                dve.wait_ge(S["lev_exp"], LEVELS)
                dve.wait_ge(S["att_done"], LEVELS - 1)
                V.tensor_tensor(lq[:, :, P:T], q_[:, :, P:T], e[:, :, P:T], ALU.mult).then_inc(S["lev_ready"], 1)
                V.tensor_tensor(lk[:, :, 0:P], k_[:, :, 0:P], e[:, :, 0:P], ALU.mult).then_inc(S["lev_ready"], 1)
                dve.wait_ge(S["lru_tanh"], LRU_J)
                link(V.tensor_scalar(lru_u, lru_v, 1.0, None, ALU.add))
                link(V.reciprocal(lru_u, lru_u))
                flat = lambda ap: ap.rearrange("p j t -> p (j t)")
                V.scalar_tensor_tensor(flat(lru_u), flat(lru_v), 2.0, flat(lru_u), ALU.mult, ALU.mult).then_inc(S["lru_w"], 1)
                dve.wait_ge(S["gate_sig"], 8)
                link(V.tensor_tensor(lru_i, lru_i, lru_x[:, :, :], ALU.mult))
                for i in range(2):
                    e2 = lev_e[1][:, 2 * i:2 * i + 2, :]
                    dve.wait_ge(S["o_root"], i + 1)
                    link(V.reciprocal(e2, e2))
                    link(V.tensor_tensor(lev_q[0][:, 2 * i:2 * i + 2, :], pb[4 + i][:, :].rearrange("p (h t) -> p h t", h=2),
                                         e2, ALU.mult))
                dve.wait_ge(S["w_act"], 14)
                for hd in range(HG_H):
                    V.scalar_tensor_tensor(yT[:, 8 + hd, :], lev_q[0][:, hd, :], pcol[:, R_HNW + hd:R_HNW + hd + 1],
                                           g_[:, hd, :], ALU.mult, ALU.mult).then_inc(S["yT_ready"], 1)

                dve.wait_ge(S["lru_sqrt"], 1)
                link(V.tensor_tensor(lru_u, lru_u, lru_i, ALU.mult))
                dve.wait_ge(S["lru_exp"], LRU_J)
                link(V.memset(lru_a[:, :, 0:1], 0.0))
                link(V.tensor_tensor_scan(flat(lru_r), flat(lru_a), flat(lru_u), 0.0, ALU.mult, ALU.add))
                own(V.tensor_tensor(lru_r, lru_r, lru_g[:, :, :], ALU.mult), S["lru_y"], 1)
                dve.wait_ge(S["lru_root"], 1)
                link(V.reciprocal(tmp[:, 0:T], tmp[:, 0:T]))
                link(V.tensor_tensor(lru_i, lru_r, bcast(tmp[:, 0:T], 1, LRU_J), ALU.mult))
                V.tensor_tensor(yT[:, 12:16, :], lru_i, bcast(pcol[:, R_LNW:R_LNW + LRU_J], 2, T),
                                ALU.mult).then_inc(S["yT_ready"], 1)

                modulation(1, pb[5])
                dve.wait_ge(ada_taken, 2 * l + 2)
                for i in range(2):
                    V.tensor_copy(gates[:, 1, 512 * i:512 * i + 512], pb[6 + i][:, :]).then_inc(S["gates_f"], 1)
                wait_pe_unit(dve, l, U_OUT + 7)
                dve.wait_ge(S["gates_m"], 2)
                for i in range(4):
                    t, half = divmod(i, 2)
                    cols = slice(512 * half, 512 * half + 512)
                    link(V.tensor_tensor(tmp[:, :], pb[i][:, :], gates[:, 0, cols], ALU.mult))
                    own(V.tensor_tensor(x[:, t, cols], x[:, t, cols], tmp[:, :], ALU.add), S["x_mid"], i + 1)

                normed(x, xn2, S["ss_ffn"], S["xn2_ready"])
                for kk in range(KD):
                    dve.wait_ge(S["h2_chunks"], kk // 2 + 1)
                    V.tensor_scalar(h2T[:, kk, :], pb[kk // 2][:, T * (kk % 2):T * (kk % 2) + T],
                                    modc[:, 1, 0, kk:kk + 1], modc[:, 1, 1, kk:kk + 1], ALU.mult,
                                    ALU.add).then_inc(S["h2_ready"], 1)
                for j in range(4):
                    dve.wait_ge(S["x_hi"], j + 1)
                    V.tensor_tensor(xlo[:, 2 * j:2 * j + 2, :], h2T[:, 2 * j:2 * j + 2, :],
                                    xhi[:, 2 * j:2 * j + 2, :].bitcast(fp32), ALU.subtract).then_inc(S["x_lo"], 1)
                for j in range(4):
                    dve.wait_ge(S["xt_hi"], j + 1)
                    part = (slice(None), j // 2, slice(512 * (j % 2), 512 * (j % 2) + 512))
                    V.tensor_tensor(xtl[part], pb[j][:, :], xth[part].bitcast(fp32), ALU.subtract).then_inc(S["xt_lo"], 1)
                split_lo(l, 0, 0, 0, 0)
                split_lo(l, 1, 0, 0, 0)
                dve.wait_ge(S["scores"], 1)
                link(V.tensor_tensor(sel[:, :, :], sc[:, :, :], bcast(rbias[:, :], 1, TT), ALU.add))
                for t in range(TT):
                    for g in range(8):
                        order[0] += 1
                        V.max(m8[:, t, g, :], sel[:, t, 8 * g:8 * g + 8]).then_inc(S["dve_order"], 1)
                dve.wait_ge(S["dve_order"], order[0])
                link(V.tensor_tensor(gsc[:, :, :], m8[:, :, :, 0], m8[:, :, :, 1], ALU.add))
                c0, c1 = (cmp_[:, i, :].rearrange("p (t i j) -> p t i j", t=TT, i=8) for i in range(2))
                other, self_ = bcast(gsc[:, :, :], 2, 8), bcast(gsc[:, :, :], 3, 8)
                link(V.tensor_tensor(c0, other, self_, ALU.is_equal))
                link(V.tensor_tensor(c0, c0, bcast(lt8[:, :].rearrange("p (i j) -> p i j", i=8), 1, TT), ALU.mult))
                link(V.tensor_tensor(c1, other, self_, ALU.is_gt))
                link(V.tensor_tensor(c0, c0, c1, ALU.add))
                link(V.tensor_reduce(gm[:, 0, :, :], c0, AXL.X, ALU.add))
                link(V.tensor_scalar(gm[:, 0, :, :], gm[:, 0, :, :], 3.5, None, ALU.is_lt))
                link(V.tensor_scalar(gm[:, 1, :, :], gm[:, 0, :, :], 1.0e4, -1.0e4, ALU.mult, ALU.add))
                by_group = lambda ap: ap.rearrange("p t (g e) -> p (t g) e", g=8)
                flat_g = lambda i: bcast(gm[:, i, :, :].rearrange("p t g -> p (t g)"), 2, 8)
                link(V.tensor_tensor(by_group(sel[:, :, :]), by_group(sel[:, :, :]), flat_g(0), ALU.mult))
                link(V.tensor_tensor(by_group(sel[:, :, :]), by_group(sel[:, :, :]), flat_g(1), ALU.add))
                for t in range(TT):
                    link(V.max(t8[:, t, :], sel[:, t, :]))
                    link(V.match_replace(rep[:, t, :], in_to_replace=t8[:, t, :], in_values=sel[:, t, :], imm_value=-3.0e4))
                own(V.tensor_tensor(chosen[:, :, :], rep[:, :, :], sel[:, :, :], ALU.not_equal), S["chosen"], 1)
                link(V.tensor_tensor(rep[:, :, :], chosen[:, :, :], sc[:, :, :], ALU.mult))
                link(V.tensor_reduce(wsum[:, 0, :], rep[:, :, :], AXL.X, ALU.add))
                link(V.reciprocal(wsum[:, 1, :], wsum[:, 0, :]))
                for t in range(TT):
                    V.tensor_scalar(wts[:, t, 1:E + 1], rep[:, t, :], wsum[:, 1, t:t + 1], SCALE, ALU.mult,
                                    ALU.mult).then_inc(S["wts"], 1)
                dve.wait_ge(S["placed"], 1)
                link(V.memset(place[:, :, :], -1.0))
                link(V.tensor_tensor(place[:, :, 1:E + 1], pb[7][:, 0:TT * E].rearrange("p (t e) -> p t e", t=TT),
                                     chosen[:, :, :], ALU.mult))
                link(V.tensor_scalar(place[:, :, 1:E + 1], place[:, :, 1:E + 1], -1.0, None, ALU.add))
                link(V.tensor_scalar(place2[:, :, :], place[:, :, :], float(-SLOTS), None, ALU.add))
                link(V.tensor_copy(counts[:, 0:E], pb[7][:, TT * E:(TT + 1) * E]))
                link(V.tensor_reduce(counts[:, E:E + 1], counts[:, 0:E], AXL.X, ALU.max))
                link(V.tensor_scalar(counts[:, E + 1:E + 2], counts[:, E:E + 1], SLOTS + 0.5, None, ALU.is_gt))
                own(V.tensor_copy(over[:, :], counts[:, E + 1:E + 2]), S["over"], 1)
                make_pick(1)
                split_lo(l, 0, 1, 1, 0)
                dve.wait_ge(S["silu_g"], TT)
                for t in range(TT):
                    V.tensor_tensor(h[:, t, :], sg[:, t, :], pb[4 + t][:, DE:2 * DE], ALU.mult).then_inc(S["h_ready"], 1)
                tokens_lo(1, 0)
                tokens_lo(1, 1)
                slot_weights(1)
                make_pick(2)
                split_lo(l, 1, 1, 1, 0)

                def expert_step(n, n0, it, last=False):
                    split_lo(l, 2, n - 1, n0 - 1, it)
                    hidden_lo(n - 1)
                    if not last:
                        tokens_lo(n + 1, 0)
                        split_lo(l, 0, n + 1, n0 + 1, it)
                    hidden(n)
                    if not last:
                        tokens_lo(n + 1, 1)
                        slot_weights(n + 1)
                        make_pick(n + 2)
                    row_lo(n)
                    if not last:
                        split_lo(l, 1, n + 1, n0 + 1, it)

                for r in range(X_IT):
                    expert_step(1 + r, 1 + r, 0)
                with dve.Fori(1, N_IT) as it:
                    for r in range(X_IT):
                        expert_step(X_IT * it + 1 + r, 1 + r, it)
                for n in range(LAST, E + 1):
                    expert_step(n, n, 0, last=n == E)
                split_lo(l, 2, E, E, 0)
                hidden_lo(E)
                dve.wait_ge(S["gates_f"], 2)
                dve.wait_ge(S["x_used2"], N_X)
                for i in range(4):
                    t, half = divmod(i, 2)
                    cols = slice(512 * half, 512 * half + 512)
                    link(V.tensor_tensor(tmp2, pb[i][:, :], gates[:, 1, cols], ALU.mult))
                    link(V.tensor_tensor(x[:, t, cols], x[:, t, cols], tmp2, ALU.add))

                def overflow(l, e):
                    for t in range(TT):
                        V.tensor_scalar(pick[:, t, :], iota[:, :], place2[:, t, bass.ds(e + 1, 1)], None,
                                        ALU.is_equal).then_inc(S["over_pick"], 1)
                    dve.wait_ge(S["over_pe"], 5 * e + 3)
                    V.tensor_copy(wslot[:, :], pb[6][:, T:T + 1]).then_inc(S["over_dve"], 1)
                    dve.wait_ge(S["over_act"], 4 * e + 4)
                    dve.wait_ge(S["over_dve"], 3 * e + 1)
                    V.scalar_tensor_tensor(h[:, 0, :], sg[:, 0, :], wslot[:, 0:1], pb[4][:, DE:2 * DE], ALU.mult,
                                           ALU.mult).then_inc(S["over_dve"], 1)
                    dve.wait_ge(S["over_pe"], 5 * e + 5)
                    V.tensor_copy(xn2[:, 0, 0:512], pb[6][:, :]).then_inc(S["over_dve"], 1)
                    dve.wait_ge(S["over_down"], e + 1)
                    for i in range(4):
                        t, half = divmod(i, 2)
                        cols = slice(512 * half, 512 * half + 512)
                        V.tensor_tensor(xn2[:, 1, cols], pb[i][:, :], gates[:, 1, cols], ALU.mult).then_inc(S["over_prod"], 1)
                        dve.wait_ge(S["over_prod"], 4 * e + i + 1)
                        V.tensor_tensor(x[:, t, cols], x[:, t, cols], xn2[:, 1, cols], ALU.add).then_inc(S["over_x"], 1)
                        dve.wait_ge(S["over_x"], 4 * e + 4 + i + 1)

                dve.sem_inc(S["over_x"], 4)
                overflow_pass(dve, l, overflow)
                dve.wait_ge(S["end_pe"], 1)
                dve.wait_ge(S["end_act"], 1)
                dve.wait_ge(S["end_sp"], 1)
                for s in S.values():
                    dve.sem_clear(s)
                dve.sem_inc(layer_done, 1)

            dve.wait_ge(fin_sq, TT + 1)
            V.reciprocal(rstd[:, :], ss[:, 2:4]).then_inc(fin_dve, 1)
            dve.wait_ge(fin_dve, 1)
            for t in range(TT):
                V.tensor_scalar(xo[:, t, :], x[:, t, :], rstd[:, t:t + 1], None, ALU.mult).then_inc(fin_dve, 1)
            dve.wait_ge(fin_dve, 3)
            dve.wait_ge(const_in, 16 * 10)
            for t in range(TT):
                V.tensor_tensor(xo[:, t, :], xo[:, t, :], fnw[:, :], ALU.mult).then_inc(fin_dve, 1)

        @block.tensor
        def _(pe):
            M, TR = nc.tensor.matmul, nc.tensor.transpose

            def ada(l, i, cols_bank, row_banks):
                pe.wait_ge(ada_sum, ADA_STEPS * (2 * l + i + 1))
                for c in range(2 * KD):
                    ins = M(cols_bank[:, c:c + 1], ada_acc[:, c // KD, c % KD::KD], ones[:, 0:1], start=True, stop=True)
                ins.then_inc(S["ada_cols"], 1)
                for half in range(2):
                    ins = M(row_banks[half][:, :], ones[:, :], ada_acc[:, 2, 512 * half:512 * half + 512],
                            start=True, stop=True)
                ins.then_inc(ada_taken, 1)

            def turn(src, dst_banks, ready, done):
                pe.wait_ge(ready, TT)
                for kk in range(KD):
                    for t in range(TT):
                        c = T * (kk % 2) + P * t
                        ins = TR(dst_banks[kk // 2][:, c:c + P], src[:, t, kk::KD], ident[:, :])
                    if kk % 2:
                        ins.then_inc(done, 1)

            emptied = []
            n_act = 0
            for i in range(N_W):
                if i < W_DT:
                    emptied.append(("conv", 2 * i + 2))
                elif i == W_DT:
                    emptied.append(("dt_in", 1))
                elif W_LX <= i < W_HV:
                    emptied.append(("conv_lx", 2 * (i - W_LX) + 2))
                else:
                    n_act += 1
                    emptied.append(("w_act", n_act))

            def project(l, i):
                u = U_W + i
                bank = pb[i % W_BANKS]
                if i >= W_BANKS:
                    pe.wait_ge(S[emptied[i - W_BANKS][0]], emptied[i - W_BANKS][1])
                wait_unit(pe, l, u)
                if W_COLS[i] in range(C_Z, C_Z + SSD_IN) or W_COLS[i] in range(C_HV, C_HV + 512) or i == W_DT:
                    n = SSD_HEADS if i == W_DT else 256
                    for t in range(TT):
                        for k in range(KD):
                            ins = M(bank[:, n * t:n * t + n], hT[:, k, P * t:P * t + P],
                                    ring_unit(u)[:, n * k:n * k + n], start=k == 0, stop=k == KD - 1)
                else:
                    for c in range(2):
                        for k in range(KD):
                            w = ring_unit(u)[:, 256 * k + P * c:256 * k + P * c + P]
                            ins = M(bank[:, T * c:T * c + T], w, hT[:, k, :], start=k == 0, stop=k == KD - 1)
                ins.then_inc(pe_unit, 1)

            def gate_up(l, n, half, tiles=1):
                wait_split(pe, l, half, n)
                wh, wl = (w[half][:, :].rearrange("p (g k c) -> p g k c", g=2, k=4) for w in (whi, wlo))
                for k in range(4):
                    for t in range(tiles):
                        xs = slice(P * t, P * t + P)
                        kk = 4 * half + k
                        first, last = half == 0 and k == 0, half == 1 and k == 3
                        bank = pb[4 + t][:, :]
                        M(bank, xhi[:, kk, xs], wh[:, :, k, :], start=first, stop=False)
                        M(bank, xhi[:, kk, xs], wl[:, :, k, :], start=False, stop=False)
                        ins = M(bank, xlo[:, kk, xs], wh[:, :, k, :], start=False, stop=last)
                ins.then_inc(S[f"x_used{half}"], 1)

            def gather_half(bank, half):
                for k in range(4):
                    for t in range(TT):
                        for part in (xth, xtl):
                            ins = M(bank[:, P * k:P * k + P], part[:, t, P * (4 * half + k):P * (4 * half + k) + P], pick[:, t, :],
                                    start=t == 0 and part is xth, stop=t == TT - 1 and part is xtl)
                return ins

            def gather(n, half):
                pe.wait_ge(S["pick"], TT * n)
                if half or not isinstance(n, int) or n > 1:
                    pe.wait_ge(S["xe_lo"], 2 * (n - 1) + half)
                gather_half(pb[5], half).then_inc(S["gathered"], 1)

            def turn_pick(bank, wcol):
                for t in range(TT):
                    TR(bank[:, P * t:P * t + P], pick[:, t, :].bitcast(fp32), ident[:, :])
                for t in range(TT):
                    ins = M(bank[:, T:T + 1], pick[:, t, :].bitcast(fp32), wcol(t), start=t == 0, stop=t == TT - 1)
                return ins

            def turned(n):
                if not isinstance(n, int) or n > 1:
                    pe.wait_ge(S["put_ready"], n - 1)
                    pe.wait_ge(S["wslot"], n - 1)
                turn_pick(pb[7], lambda t: wts[:, t, n:n + 1] if isinstance(n, int)
                          else wts[:, t, bass.ds(n, 1)]).then_inc(S["pick_turned"], 1)

            def turn_hidden():
                pe.wait_ge(S["h_ready"], TT)
                for hc in range(2):
                    for t in range(TT):
                        ins = TR(pb[6][:, T * hc + P * t:T * hc + P * t + P], h[:, t, P * hc:P * hc + P], ident[:, :])
                ins.then_inc(S["h_spread"], 1)

            def spread(n):
                pe.wait_ge(S["row_lo"], n)
                pe.wait_ge(S["put_ready"], n)
                for hc in range(2):
                    for part in (hhi, hlo):
                        ins = M(pb[6][:, T * hc:T * hc + T], part[:, P * hc:P * hc + P], put[:, :],
                                start=part is hhi, stop=part is hlo)
                ins.then_inc(S["h_spread"], 1)

            def down(l, n, first=False, last=False):
                wait_split(pe, l, 2, n)
                pe.wait_ge(S["h_lo"], n + 1)
                wh, wl = (w[2][:, :].rearrange("p (k c) -> p k c", k=2) for w in (whi, wlo))
                for hc in range(2):
                    for t in range(TT):
                        for half in range(2):
                            ts, cs = slice(P * t, P * t + P), slice(512 * half, 512 * half + 512)
                            acc = pb[2 * t + half][:, :]
                            M(acc, hTh[:, hc, ts], wh[:, hc, cs], start=first and hc == 0, stop=False)
                            M(acc, hTh[:, hc, ts], wl[:, hc, cs], start=False, stop=False)
                            ins = M(acc, hTl[:, hc, ts], wh[:, hc, cs], start=False, stop=last and hc == 1)
                ins.then_inc(S["x_used2"], 1)

            pe.wait_ge(const_in, 16 * 9)
            pe.wait_ge(params_in, 16 * 17 * L)
            with pe.Fori(0, L) as l:
                pe.wait_ge(S["prow_ready"], 1)
                TR(pb[1][:, 0:R_END], prow_now[0:R_END, :],
                   ident[0:R_END, 0:R_END]).then_inc(S["params_turned"], 1)
                ada(l, 0, pb[0], (pb[2], pb[3]))
                turn(xn, pb[4:8], S["xn_ready"], S["h_chunks"])
                pe.wait_ge(S["modc_s"], 1)
                pe.wait_ge(S["modc"], 1)
                pe.wait_ge(S["pcol"], 1)
                pe.wait_ge(S["hT_ready"], KD)
                pe.wait_ge(S["gates_m"], 2)
                for i in range(W_HQ + 2):
                    project(l, i)

                pe.wait_ge(S["a_ready"], 1)
                M(pb[3][:, 0:32], tri[:, :], dts[:, 3, :], start=True, stop=True)
                M(pb[3][:, 32:64], ones[:, :], dts[:, 3, :], start=True, stop=True).then_inc(S["acum_done"], 1)
                pe.wait_ge(S["xbc_ready"], 6)
                chunk = lambda c: slice(P * c, P * c + P)
                for c in range(2):
                    for g in range(2):
                        i = 2 * c + g
                        ins = M(pb[4][:, P * i:P * i + P], xbcT[:, 8 + g, chunk(c)], xbcT[:, 10 + g, chunk(c)],
                                start=True, stop=True)
                ins.then_inc(S["cb_done"], 1)
                for g in range(2):
                    ins = TR(pb[5][:, P * g:P * g + P], xbcT[:, 8 + g, chunk(0)], ident[:, :])
                ins.then_inc(S["btok_done"], 1)
                for i in range(4):
                    c, half = divmod(i, 2)
                    if i == 2:
                        pe.wait_ge(S["cb_ready"], 1)
                    if i == 3:
                        pe.wait_ge(S["btok_ready"], 1)
                    for j in range(4):
                        ins = TR(pb[(6, 7, 4, 5)[i]][:, P * j:P * j + P], xbcT[:, 4 * half + j, chunk(c)], ident[:, :])
                    ins.then_inc(S["xs_turned"], 1)
                for i in range(W_Z, W_Z + 4):
                    project(l, i)
                pe.wait_ge(S["xdec_ready"], 1)
                pe.wait_ge(S["btok_ready"], 1)
                pe.wait_ge(S["dec_in"], 1)
                for g in range(2):
                    if g:
                        pe.wait_ge(S["st_ready"], g)
                    M(pb[3][:, :], btok[:, g, :], xdec[:, 512 * g:512 * g + 512], start=True,
                      stop=True).then_inc(S["st_done"], 1)
                pe.wait_ge(S["xh_ready"], 4)

                def diff(q):
                    c, h0 = q // 4, 4 * (q % 4)
                    bank = pb[4 + q % 2]
                    if q >= 2:
                        pe.wait_ge(S["diff_sub"], q - 1)
                    M(bank[:, :].rearrange("p (h t) -> p h t", h=4), ident[:, :], bcast(neg[:, :], 1, 4), start=True,
                      stop=False, skip_group_check=True)
                    for j in range(4):
                        ac = dts[:, 3, 16 * c + h0 + j:16 * c + h0 + j + 1].broadcast_to([P, P])
                        ins = M(bank[:, P * j:P * j + P], ac, tri[:, :], start=False, stop=True, skip_group_check=True)
                    ins.then_inc(S["diff_done"], 1)

                def y_diag(q):
                    c, h0, i = q // 4, 4 * (q % 4), q // 2
                    if i >= 2 and q % 2 == 0:
                        pe.wait_ge(S["y_taken"], i - 1)
                    pe.wait_ge(S["m_ready"], q + 1)
                    pe.wait_ge(S["xdt_ready"], c + 1)
                    for j in range(4):
                        hd = h0 + j
                        o = SSD_HD * (hd % 8)
                        ins = M(pb[6 + i % 2][:, o:o + SSD_HD], mdec[:, q % 2, j, :],
                                xdt[:, c, SSD_HD * hd:SSD_HD * hd + SSD_HD], start=True, stop=True)
                    ins.then_inc(S["ydiag"], 1)

                def y_off(g):
                    pe.wait_ge(S["st_ready"], 2)
                    if g:
                        pe.wait_ge(S["yoff_taken"], g)
                    M(pb[3][:, :], xbcT[:, 10 + g, chunk(1)], stT[:, g, :], start=True, stop=True).then_inc(S["yoff"], 1)

                for q in range(9):
                    if q < 8:
                        diff(q)
                    if q == 5:
                        y_off(0)
                    if q:
                        y_diag(q - 1)
                y_off(1)
                project(l, W_LX)
                for i in range(4):
                    c, g = divmod(i, 2)
                    pe.wait_ge(S["y_norm"], i + 1)
                    pe.wait_ge(S["y_taken"], 4)
                    for j in range(4):
                        o = 512 * g + P * j
                        ins = TR(pb[4 + i][:, P * j:P * j + P], y[:, c, o:o + P], ident[:, :])
                    ins.then_inc(S["y_turned"], 1)

                project(l, W_LX + 1)

                def level(i):
                    lq, lk = (qkg[:, 0, :, :], qkg[:, 1, :, :]) if i == 0 else (lev_q[i % 2], lev_k[i % 2])
                    if i:
                        pe.wait_ge(S["lev_ready"], 2 * i)
                    if i < 2:
                        pe.wait_ge(S["yT_ready"], 4)
                    else:
                        pe.wait_ge(S["att_taken"], 2 * i - 2)
                    for hd in range(HG_H):
                        for t in range(TT):
                            o = P * (2 * (hd % 2) + t)
                            ins = M(pb[4 + 2 * (i % 2) + hd // 2][:, o:o + P], lk[:, hd, chunk(t)], lq[:, hd, chunk(t)],
                                    start=True, stop=True)
                    ins.then_inc(S["att_done"], 1)

                def project_out(i):
                    wait_unit(pe, l, U_OUT + i)
                    for k2 in range(2):
                        k = 2 * i + k2
                        for t in range(TT):
                            for half in range(2):
                                c = 1024 * k2 + 512 * half
                                ins = M(pb[2 * t + half][:, :], yT[:, k, chunk(t)], ring_unit(U_OUT + i)[:, c:c + 512],
                                        start=k == 0, stop=k == KY - 1)
                    ins.then_inc(pe_unit, 1)

                pe.wait_ge(S["k_ready"], 1)
                pe.wait_ge(S["w_act"], 4)
                for i in range(6):
                    level(i)
                    project(l, W_HV + i)
                pe.wait_ge(S["conv_lx"], 4)
                pe.wait_ge(S["bd_in"], 16 * 4)
                pe.wait_ge(S["w_act"], 14)
                pe.wait_ge(S["yoff_taken"], 2)
                for k in range(2):
                    for j in range(LRU_J):
                        o = T * (j % 2)
                        ins = M(pb[2 * k + j // 2][:, o:o + T], bd[:, k, j, :], lru_x[:, j, :], start=True, stop=True)
                ins.then_inc(S["gate_mm"], 1)
                level(6)
                level(7)
                pe.wait_ge(S["gate_sig"], 8)
                project_out(0)
                pe.wait_ge(S["lev_ready"], 2 * LEVELS)
                pe.wait_ge(S["att_taken"], 2 * LEVELS - 2)
                for hd in range(HG_H):
                    ins = M(pb[4][:, P * hd:P * hd + P], lev_k[0][:, hd, chunk(0)], lev_q[0][:, hd, chunk(1)],
                            start=True, stop=True)
                ins.then_inc(S["cross_done"], 1)
                project_out(1)
                pe.wait_ge(S["att_taken"], 2 * LEVELS)
                pe.wait_ge(S["cross_ready"], 1)
                for hd in range(HG_H):
                    vh = v[:, :, P * hd:P * hd + P]
                    o = T * (hd % 2)
                    bank = pb[4 + hd // 2]
                    M(bank[:, o:o + P], vh[:, 0, :], attn[:, 2 * hd, :], start=True, stop=True)
                    M(bank[:, o + P:o + T], vh[:, 1, :], attn[:, 2 * hd + 1, :], start=True, stop=False)
                    ins = M(bank[:, o + P:o + T], vh[:, 0, :], cross[:, hd, :], start=False, stop=True)
                ins.then_inc(S["o_done"], 1)
                project_out(2)
                for i in range(2):
                    pe.wait_ge(S["o_sq"], i + 1)
                    ins = M(pb[6 + i][:, :].rearrange("p (h t) -> p h t", h=2), ones[:, :], lev_e[0][:, 2 * i:2 * i + 2, :],
                            start=True, stop=True)
                ins.then_inc(S["o_sum"], 1)
                project_out(3)
                pe.wait_ge(S["yT_ready"], 8)
                project_out(4)
                ada(l, 1, pb[5], (pb[6], pb[7]))
                project_out(5)
                pe.wait_ge(S["lru_sq"], 1)
                for j in range(LRU_J):
                    ins = M(pb[4][:, 0:T], ones[:, :], lru_v[:, j, :], start=j == 0, stop=j == LRU_J - 1)
                ins.then_inc(S["lru_sum"], 1)
                pe.wait_ge(S["yT_ready"], 9)
                project_out(6)
                project_out(7)

                pe.wait_ge(S["modc_s"], 2)
                pe.wait_ge(S["gates_f"], 2)
                pe.wait_ge(S["lru_root"], 1)
                turn(xn2, pb[0:4], S["xn2_ready"], S["h2_chunks"])
                pe.wait_ge(S["router_in"], 16)
                pe.wait_ge(S["h2_ready"], KD)
                pe.wait_ge(S["x_mid"], 4)
                for t in range(TT):
                    for k in range(KD):
                        ins = M(pb[7][:, E * t:E * t + E], h2T[:, k, chunk(t)], rw[:, k, :], start=k == 0, stop=k == KD - 1)
                ins.then_inc(S["logits"], 1)
                pe.wait_ge(S["x_lo"], 4)
                for t in range(TT):
                    for half in range(2):
                        for k in range(4):
                            ins = TR(pb[2 * t + half][:, P * k:P * k + P], h2T[:, 4 * half + k, chunk(t)], ident[:, :])
                        ins.then_inc(S["rows_turned"], 1)
                gate_up(l, 0, 0, TT)
                gate_up(l, 0, 1, TT)
                pe.wait_ge(S["chosen"], 1)
                M(pb[7][:, 0:E], tri[:, :], chosen[:, 0, :], start=True, stop=True)
                M(pb[7][:, E:2 * E], tri[:, :], chosen[:, 1, :], start=True, stop=False)
                M(pb[7][:, E:2 * E], ones[:, :], chosen[:, 0, :], start=False, stop=True)
                M(pb[7][:, 2 * E:3 * E], ones[:, :], chosen[:, 0, :], start=True, stop=False)
                M(pb[7][:, 2 * E:3 * E], ones[:, :], chosen[:, 1, :], start=False, stop=True).then_inc(S["placed"], 1)
                pe.wait_ge(S["wts"], TT)
                pe.wait_ge(S["over"], 1)
                pe.wait_ge(S["h_ready"], TT)
                pe.wait_ge(S["xt_lo"], 4)
                gather(1, 0)
                gather(1, 1)
                turned(1)

                def expert_step(n, first=False, last=False):
                    if not (isinstance(n, int) and n == 1):
                        pe.wait_ge(S["h_ready"], TT + n - 1)
                    gate_up(l, n, 0)
                    if first:
                        turn_hidden()
                    else:
                        spread(n - 1)
                    if not last:
                        gather(n + 1, 0)
                    gate_up(l, n, 1)
                    if not last:
                        gather(n + 1, 1)
                        turned(n + 1)
                    down(l, n - 1, first=first)

                for n in range(1, X_IT + 1):
                    expert_step(n, first=n == 1)
                with pe.Fori(1, N_IT) as it:
                    for r in range(X_IT):
                        expert_step(X_IT * it + 1 + r)
                for n in range(LAST, E + 1):
                    expert_step(n, last=n == E)
                spread(E)
                down(l, E, last=True)

                def overflow(l, e):
                    pe.wait_ge(S["over_pick"], TT * e + TT)
                    pe.wait_ge(S["over_x"], 4 * e + 4)
                    for half in range(2):
                        gather_half(pb[(5, 7)[half]], half).then_inc(S["over_pe"], 1)
                    turn_pick(pb[6], lambda t: wts[:, t, bass.ds(e + 1, 1)]).then_inc(S["over_pe"], 1)
                    pe.wait_ge(S["over_act"], 4 * e + 2)
                    pe.wait_ge(S["over_full"], 16 * (5 * e + 5))
                    for k in range(KD):
                        w = ring[:, k // 4, :].rearrange("p (g k c) -> p g k c", g=2, k=4)
                        ins = M(pb[4][:, :], h2T[:, k, 0:SLOTS], w[:, :, k % 4, :], start=k == 0, stop=k == KD - 1)
                    ins.then_inc(S["over_pe"], 1)
                    pe.wait_ge(S["over_act"], 4 * e + 3)
                    pe.wait_ge(S["over_dve"], 3 * e + 2)
                    for hc in range(2):
                        ins = M(pb[6][:, T * hc:T * hc + T], h[:, 0, P * hc:P * hc + P], put[:, :].bitcast(fp32),
                                start=True, stop=True)
                    ins.then_inc(S["over_pe"], 1)
                    pe.wait_ge(S["over_dve"], 3 * e + 3)
                    for t in range(TT):
                        for half in range(2):
                            for hc in range(2):
                                ins = M(pb[2 * t + half][:, :], xn2[:, 0, T * hc + P * t:T * hc + P * t + P],
                                        ring[:, 2, 1024 * hc + 512 * half:1024 * hc + 512 * half + 512],
                                        start=hc == 0, stop=hc == 1)
                    ins.then_inc(S["over_down"], 1)

                overflow_pass(pe, l, overflow)
                pe.sem_inc(S["end_pe"], 1)
                pe.wait_ge(layer_done, l + 1)


SIGNALS = """ada_cols prow_ready pnow bd_zero bd_in params_turned pcol modc_s modc ss_mix xn_ready h_chunks hT_ready
    gates_m gates_f lb_in lb_exp lam_in lam_exp lruc_ready conv xbc_ready conv_lx w_act
    dt_in dt_exp a_ready acum_done dec_in dec eacum k_ready cb_done cb_ready btok_done btok_ready
    xs_turned xh_ready xdt_ready xdec_ready st_done st_ready diff_done diff_sub diff_exp m_ready ydiag yoff
    y_taken yoff_taken y_gated y_sq y_norm y_turned yT_ready logf lev_in lev_exp lev_ready att_done att_taken
    cross_done cross_ready o_done o_sq o_sum o_root gate_mm gate_sig lru_tanh lru_exp lru_w lru_sqrt lru_y lru_sq
    lru_sum lru_root x_mid router_in ss_ffn xn2_ready h2_chunks h2_ready x_hi x_lo logits scores
    x_hi0 x_hi1 x_hi2 x_used0 x_used1 x_used2 silu_g h_ready h_spread h_hi h_lo
    rows_turned xt_hi xt_lo chosen placed wts over pick pick_turned put_ready wslot gathered xe_hi xe_lo row_hi row_lo
    over_x over_full over_pe over_act over_dve over_pick over_down over_prod dve_order end_pe end_act end_sp""".split()


def kernel(**inputs):
    import numpy as np
    import concourse.bacc as bacc
    from concourse.bass_utils import run_bass_kernel_spmd

    i = np.arange(P)
    part, col = i[:, None], i[None, :]
    consts = np.concatenate([
        (part == col).astype(np.float32),
        (part <= col).astype(np.float32),
        np.where(col < part, np.float32(NEG), np.float32(0)),
        np.ones((P, P), np.float32),
        np.broadcast_to((np.arange(8)[None, :] < np.arange(8)[:, None]).astype(np.float32).reshape(1, 64), (P, 64)),
        np.broadcast_to(i[None, :].astype(np.float32), (P, P)),
    ], axis=1)
    masks = [part == col]
    for level in range(1, LEVELS):
        m = 1 << (level - 1)
        masks.append((part // (2 * m) == col // (2 * m)) & (part // m % 2 == 0) & (col // m % 2 == 1))
    masks = np.concatenate(masks, axis=1).astype(np.uint32)

    nc = bacc.Bacc("TRN2", target_bir_lowering=False, num_devices=1)
    arrays = {f"in_{k}": np.ascontiguousarray(v) for k, v in inputs.items()}
    arrays["in_consts"] = np.ascontiguousarray(consts)
    arrays["in_masks"] = np.ascontiguousarray(masks)
    aps = {k[3:]: nc.dram_tensor(k, v.shape, mybir.dt.from_np(v.dtype), kind="ExternalInput").ap()
           for k, v in arrays.items()}
    out = nc.dram_tensor("out", (1, T, D), fp32, kind="ExternalOutput").ap()
    build(nc, aps, out)
    got = run_bass_kernel_spmd(nc, [arrays], core_ids=[0])
    return got.results[0]["out"]
```

```python
import concourse.bass as bass
from concourse import mybir
from contextlib import ExitStack

fp32 = mybir.dt.float32
fp32r = mybir.dt.float32r
uint32 = mybir.dt.uint32
ALU = mybir.AluOpType
ACT = mybir.ActivationFunctionType
AXL = mybir.AxisListType

P = 128
L, T, D = 2, 256, 1024
TT = T // P
KD = D // P
EPS = 1e-6
SSD_IN, SSD_HEADS, SSD_HD, SSD_N = 1024, 16, 64, 128
CH_XBC = (SSD_IN + 4 * SSD_N) // P
HG_H = 4
LRU_J = 4
D_IN = 5648
C_Z, C_XBC, C_DT = 0, SSD_IN, SSD_IN + CH_XBC * P
C_HQ = C_DT + SSD_HEADS
C_HF, C_HV, C_HG, C_LG, C_LX = (C_HQ + 512 * i for i in range(1, 6))
KY = 16
E, DE = 64, 256
SCALE = 2.5
NEG = -1.0e30

RING = 6
W_COLS = ([C_XBC + 256 * i for i in range(6)] + [C_DT] + [C_HF, C_HF + 256, C_HQ, C_HQ + 256]
          + [C_Z + 256 * i for i in range(4)] + [C_LX, C_LX + 256, C_HV, C_HV + 256, C_LG, C_LG + 256,
                                                 C_HG, C_HG + 256])
N_W = len(W_COLS)
U_W = 0
U_OUT = U_W + N_W
U_MOE = U_OUT + 8 + 2
UNITS = U_MOE + 3 * (E + 1)
PADS = (U_OUT + 8, U_OUT + 9)
assert UNITS % RING == 0
(W_XBC, W_DT, W_HF, W_HQ, W_Z, W_LX, W_HV, W_LG, W_HG) = 0, 6, 7, 9, 11, 15, 17, 19, 21
DVE_UNITS = list(range(W_XBC, W_DT + 1)) + [W_LX, W_LX + 1]
W_BANKS = 3

R_CW, R_CB, R_LCW, R_LCB, R_BA, R_BX, R_LAM, R_LNW, R_HNW, R_SNW, R_LB, R_END = (
    0, 48, 60, 76, 80, 84, 88, 92, 96, 100, 108, 116)
LEVELS = 8


N_PE = U_OUT + 8
N_X = E + 1
SLOTS = P
PAIR_UNITS = (("gate_up", 0, 0), ("gate_up", 1, 0), ("gate_up", 0, 1), ("gate_up", 1, 1), ("down", 0, 0), ("down", 1, 0))
PAIRS = E // 2
assert len(PAIR_UNITS) == RING
ADA_STEPS = 3 * KD
ADA_BUFS = 3


def slot_of(u):
    return u % RING


def weight_of(u):
    r = u - U_MOE
    gate_up = 0 <= r < 2 or r >= 3 and PAIR_UNITS[(r - 3) % 6][0] == "gate_up"
    return 0 if u in PADS else 32 if gate_up else 16


def filled(u):
    return sum(weight_of(q) for q in range(slot_of(u), u + 1, RING))


def per_layer(s):
    return sum(weight_of(q) for q in range(s, UNITS, RING))


def build(nc, a, out):
    ctx = ExitStack()
    with ctx:
        def sem(name):
            return ctx.enter_context(nc.semaphore(name))

        def sb(name, shape, dt=fp32, stack=ctx):
            return stack.enter_context(nc.sbuf_tensor(name, [P] + shape, dt))

        def bcast(ap, axis, n):
            shape = list(ap.shape)
            shape.insert(axis, n)
            return ap.unsqueeze(axis).broadcast_to(shape)

        ring = sb("ring", [RING, 2048])
        x = sb("x", [TT, D])
        ident = sb("ident", [P])
        tri = sb("tri", [P])
        neg = sb("neg", [P])
        ones = sb("ones", [P])
        lt8 = sb("lt8", [64])
        iota = sb("iota", [SLOTS])
        masks = sb("masks", [LEVELS, P], uint32)
        cact = sb("cact", [KD])
        craw = sb("craw", [KD])
        prow = sb("prow", [L, P])
        prow_now = sb("prow_now", [P])
        pcol = sb("pcol", [R_END])
        pall = sb("pall", [L, P])
        pnow = sb("pnow", [P])
        norm_w = pnow[:, 0:2 * KD].rearrange("p (i k) -> p i k", i=2)
        hb = pnow[:, 2 * KD:2 * KD + 3 * SSD_HEADS].rearrange("p (i h) -> p i h", i=3)
        rbias = pnow[:, P - E:P]
        ada_w = sb("ada_w", [ADA_BUFS, D])
        ada_acc = sb("ada_acc", [3, D])
        gates = sb("gates", [2, D])
        modc = sb("modc", [2, 2, KD])
        lbs = sb("lbs", [L, HG_H])
        lbt = sb("lbt", [4, HG_H])
        omlb = sb("omlb", [HG_H])
        lruc = sb("lruc", [4, LRU_J])
        ss = sb("ss", [4])
        rstd = sb("rstd", [2])
        eps = sb("eps", [1])

        mix = ExitStack()
        hT = sb("hT", [KD, T], stack=mix)
        yT = sb("yT", [KY, T], stack=mix)
        z = sb("z", [TT, SSD_IN], stack=mix)
        start = ExitStack()
        ada_first = sb("ada_first", [2, KD, D], stack=start)
        start.close()
        xbcT = sb("xbcT", [CH_XBC, T], stack=mix)
        xh = sb("xh", [TT, SSD_IN], stack=mix)
        xdt = sb("xdt", [TT, SSD_IN], stack=mix)
        y = sb("y", [TT, SSD_IN], stack=mix)
        xdec = sb("xdec", [SSD_IN], stack=mix)
        mdec = sb("mdec", [2, 4, P], stack=mix)
        cb = sb("cb", [4, P], stack=mix)
        btok = sb("btok", [2, P], stack=mix)
        stT = sb("stT", [2, 512], stack=mix)
        dts = sb("dts", [6, 32], stack=mix)
        qkg = sb("qkg", [3, HG_H, T], stack=mix)
        v = sb("v", [TT, 512], stack=mix)
        bd = sb("bd", [2, LRU_J, P], stack=mix)
        xn = z
        bT = xdec[:, :].rearrange("p (h t) -> p h t", h=HG_H)
        lev_e, lev_q, lev_k = ([buf[:, i, :].rearrange("p (h t) -> p h t", h=HG_H) for i in range(2)]
                               for buf in (xh, xdt, y))
        attn = z[:, 0, :].rearrange("p (g t) -> p g t", g=8)
        cross = z[:, 1, 0:512].rearrange("p (h t) -> p h t", h=HG_H)
        lru_x = stT[:, :, :].rearrange("p g (j t) -> p (g j) t", t=T)
        lru_g = mdec[:, :, :, :].rearrange("p i j c -> p (i j c)").rearrange("p (j t) -> p j t", t=T)
        lru_r, lru_i, lru_v = (xbcT[:, 4 * i:4 * i + 4, :] for i in range(3))
        lru_a, lru_u = hT[:, 0:4, :], hT[:, 4:8, :]
        tmp = sb("tmp", [512], stack=mix)
        sqj = yT[:, :, :].rearrange("p (i k) t -> p i (k t)", k=4)
        mix.close()
        moe = ExitStack()
        xhi = sb("xhi", [KD, T], fp32r, moe)
        xlo = sb("xlo", [KD, T], fp32r, moe)
        turning = ExitStack()
        h2T = sb("h2T", [KD, T], stack=turning)
        turning.close()
        yhi = sb("yhi", [D], fp32r, moe)
        ylo = sb("ylo", [D], fp32r, moe)
        before = ExitStack()
        xn2 = sb("xn2", [TT, D], stack=before)
        before.close()
        whi = [sb(f"whi{i}", [2048], fp32r, moe) for i in range(3)]
        wlo = [sb(f"wlo{i}", [2048], fp32r, moe) for i in range(3)]
        hTh = sb("hTh", [2, T], fp32r, moe)
        hTl = sb("hTl", [2, T], fp32r, moe)
        sg = sb("sg", [TT, DE], stack=moe)
        h = sb("h", [TT, DE], stack=moe)
        rw = sb("rw", [KD, E], stack=moe)
        sc = sb("sc", [TT, E], stack=moe)
        sel = sb("sel", [TT, E], stack=moe)
        rep = sb("rep", [TT, E], stack=moe)
        chosen = sb("chosen", [TT, E], stack=moe)
        wts = sb("wts", [TT, E + 2], stack=moe)
        place = sb("place", [TT, E + 2], stack=moe)
        place2 = sb("place2", [TT, E + 2], stack=moe)
        counts = sb("counts", [E + 2], stack=moe)
        over = sb("over", [4], uint32, moe)
        over_g = sb("over_g", [2, E // 8], uint32, moe)
        over_e = sb("over_e", [2, E], uint32, moe)
        pairc = sb("pairc", [3, E], stack=moe)
        mine = sb("mine", [E + 2], stack=moe)
        rank = sb("rank", [1], stack=moe)
        pick0 = sb("pick0", [TT, SLOTS], stack=moe)
        xth = sb("xth", [TT, D], fp32r, moe)
        xtl = sb("xtl", [TT, D], fp32r, moe)
        pick = sb("pick", [TT, SLOTS], fp32r, moe)
        put = sb("put", [T], fp32r, moe)
        wslot = sb("wslot", [2], stack=moe)
        m8 = sb("m8", [TT, 8, 8], stack=moe)
        gsc = sb("gsc", [TT, 8], stack=moe)
        cmp_ = sb("cmp", [2, TT * 64], stack=moe)
        gm = sb("gm", [2, TT, 8], stack=moe)
        t8 = sb("t8", [TT, 8], stack=moe)
        wsum = sb("wsum", [2, TT], stack=moe)
        tmp2 = sg[:, :, :].rearrange("p t c -> p (t c)")
        xeh, xel = xhi[:, :, 0:SLOTS], xlo[:, :, 0:SLOTS]
        moe.close()
        fin = ExitStack()
        fnw = sb("fnw", [D], stack=fin)
        xo = sb("xo", [TT, D], stack=fin)
        fin.close()

        pb = [ctx.enter_context(nc.psum_tensor(f"pb{i}", [P, 512], fp32)) for i in range(8)]

        full = [sem(f"slot_full{i}") for i in range(RING)]
        pe_unit = sem("pe_unit")
        x_lo = [sem(f"x_lo{j}") for j in range(3)]
        slots_taken = sem("slots_taken")
        layer_done = sem("layer_done")
        ada_full = [sem(f"ada_full{i}") for i in range(ADA_BUFS)]
        first_in = [sem(f"first_in{i}") for i in range(3)]
        ada_zero = sem("ada_zero")
        ada_bias = sem("ada_bias")
        ada_prod = sem("ada_prod")
        ada_sum = sem("ada_sum")
        ada_taken = sem("ada_taken")
        params_in = sem("params_in")
        const_in = sem("const_in")
        silu_c = sem("silu_c")
        out_sem = sem("out_stored")
        eps_ready = sem("eps_ready")
        fin_sq = sem("fin_sq")
        fin_dve = sem("fin_dve")

        S = {n: sem(n) for n in SIGNALS}

        def ring_unit(u):
            return ring[:, slot_of(u), :]

        def wait_unit(eng, l, u, it=0):
            eng.wait_ge(full[slot_of(u)], l * per_layer(slot_of(u)) + filled(u) + it * weight_of(u))

        def wait_pe_unit(eng, l, u):
            eng.wait_ge(pe_unit, l * N_PE + u + 1)

        def wait_split(eng, l, j, n):
            eng.wait_ge(x_lo[j], l * N_X + (N_X + 1) + n)

        def overflow_pass(eng, l, expert, skip, between=None, after=None):
            eng.wait_ge(S["over"], 1)

            def chunk_pass(c):
                with eng.Fori(0, E // 8) as g:
                    group = eng.value_load(over_g[0:1, c, bass.ds(g, 1)], min_val=0, max_val=1)
                    with eng.If(group > 0):
                        with eng.Fori(0, 8) as i:
                            one = eng.value_load(over_e[0:1, c, bass.ds(8 * g + i, 1)], min_val=0, max_val=1)
                            with eng.If(one > 0):
                                expert(l, 8 * g + i, E * c + 8 * g + i)
                            with eng.If(one < 1):
                                skip(E * c + 8 * g + i, 1)
                    with eng.If(group < 1):
                        skip(E * c + 8 * g, 8)

            first = eng.value_load(over[0:1, 0:1], min_val=0, max_val=1)
            with eng.If(first > 0):
                chunk_pass(0)
                second = eng.value_load(over[0:1, 1:2], min_val=0, max_val=1)
                with eng.If(second > 0):
                    if between:
                        between()
                    chunk_pass(1)
                    if after:
                        after(2)
                if after:
                    after(1)

        block = ctx.enter_context(nc.Block())

        @block.sync
        def _(sp):
            w_in = a["w_in"].rearrange("l (p k) n -> l p k n", p=P)
            w_out = a["w_out"].rearrange("l (k p) n -> l p k n", p=P)
            gate_w, up_w = (a[n].rearrange("l e (p k) n -> (l e) p (k n)", p=P) for n in ("exp_gate", "exp_up"))
            down_w = a["exp_down"].rearrange("l e (k p) n -> (l e) p k n", p=P)
            sh_g, sh_u = (a[n].rearrange("l (p k) n -> l p (k n)", p=P) for n in ("sh_gate", "sh_up"))
            sh_d = a["sh_down"].rearrange("l (k p) n -> l p k n", p=P)

            def slot_free(l, u, it=0):
                q = u - RING
                while q in PADS:
                    q -= RING
                before = l
                if q < 0:
                    q, before = q + UNITS, l - 1
                if not isinstance(it, int):
                    n, j = divmod(u - U_MOE, 3)
                    wait_split(sp, l, j, 2 * it + (n - 2))
                elif q < N_PE:
                    wait_pe_unit(sp, l, q)
                else:
                    n, j = divmod(q - U_MOE, 3)
                    wait_split(sp, before, j, n)
                sp.sem_inc(slots_taken, 1)

            def pair_unit(l, u, src):
                slot_free(l, u)
                sp.dma_start(ring_unit(u).rearrange("p (k c) -> p k c", k=2), src).then_inc(full[slot_of(u)], 16)

            def gate_up_unit(l, u, it, g, up, half):
                slot_free(l, u, it)
                dst, c = ring_unit(u), 1024 * half
                sp.dma_start(dst[:, 0:1024], g[:, c:c + 1024]).then_inc(full[slot_of(u)], 16)
                sp.dma_start(dst[:, 1024:2048], up[:, c:c + 1024]).then_inc(full[slot_of(u)], 16)

            def down_unit(l, u, it, down):
                slot_free(l, u, it)
                sp.dma_start(ring_unit(u).rearrange("p (k c) -> p k c", k=2), down).then_inc(full[slot_of(u)], 16)

            def pair_units(l, j, j0=0):
                it = 0 if isinstance(j, int) else j
                for q, (kind, side, half) in enumerate(PAIR_UNITS):
                    e = l * E + 2 * j + side
                    u = U_MOE + 3 + RING * j0 + q
                    if kind == "gate_up":
                        gate_up_unit(l, u, it, gate_w[e], up_w[e], half)
                    else:
                        down_unit(l, u, it, down_w[e])

            def overflow_loads(l, e, i):
                sp.wait_ge(S["over_x"], 4 * i + 4)
                sp.sem_inc(slots_taken, 1)
                ex = l * E + e
                for half in range(2):
                    c = 1024 * half
                    sp.dma_start(ring[:, half, 0:1024], gate_w[ex][:, c:c + 1024]).then_inc(S["over_full"], 16)
                    sp.dma_start(ring[:, half, 1024:2048], up_w[ex][:, c:c + 1024]).then_inc(S["over_full"], 16)
                sp.dma_start(ring[:, 2, :].rearrange("p (k c) -> p k c", k=2), down_w[ex]).then_inc(S["over_full"], 16)

            def overflow_skip(i, n):
                sp.wait_ge(S["over_x"], 4 * i + 4)
                sp.sem_inc(S["over_full"], 16 * 5 * n)

            def overflow_loaded(chunks):
                sp.wait_ge(S["over_full"], 16 * 5 * E * chunks)
                sp.wait_ge(S["over_x"], 4 * E * chunks + 4)
                sp.sem_inc(slots_taken, 1)

            ada_l0 = a["ada_w"][0].rearrange("(p k) (g c) -> g p k c", p=P, g=6)
            for part in range(3):
                if part == 2:
                    sp.wait_ge(ada_sum, KD)
                for k in range(0, KD, 2):
                    sp.dma_start(ada_first[:, part % 2, k:k + 2, :], ada_l0[part, :, k:k + 2, :]).then_inc(first_in[part], 16)
            for j in range(3):
                sp.sem_inc(x_lo[j], N_X)
            with sp.Fori(0, L) as l:
                for i, c in enumerate(W_COLS):
                    n = SSD_HEADS if c == C_DT else 256
                    slot_free(l, U_W + i)
                    sp.dma_start(ring_unit(U_W + i)[:, 0:KD * n].rearrange("p (k c) -> p k c", k=KD),
                                 w_in[l, :, :, c:c + n]).then_inc(full[slot_of(U_W + i)], 16)
                for i in range(8):
                    pair_unit(l, U_OUT + i, w_out[l, :, 2 * i:2 * i + 2, :])
                for half in range(2):
                    gate_up_unit(l, U_MOE + half, 0, sh_g[l], sh_u[l], half)
                down_unit(l, U_MOE + 2, 0, sh_d[l])
                pair_units(l, 0)
                with sp.Fori(1, PAIRS - 1) as j:
                    pair_units(l, j)
                pair_units(l, PAIRS - 1, PAIRS - 1)
                overflow_pass(sp, l, overflow_loads, overflow_skip, after=overflow_loaded)
                sp.sem_inc(S["end_sp"], 1)
            sp.wait_ge(fin_dve, 5)
            sp.dma_start(out.rearrange("b (t p) d -> p (b t) d", p=P), xo[:, :, :]).then_inc(out_sem, 16)
            sp.wait_ge(out_sem, 16)

        @block.scalar
        def _(act):
            A = nc.scalar.activation
            for i, t in enumerate((ident, tri, neg, ones)):
                act.dma_start(t[:, :], a["consts"][:, P * i:P * i + P]).then_inc(const_in, 16)
            act.dma_start(lt8[:, :], a["consts"][:, 4 * P:4 * P + 64]).then_inc(const_in, 16)
            act.dma_start(iota[:, :], a["consts"][:, 4 * P + 64:5 * P + 64]).then_inc(const_in, 16)
            act.dma_start(masks[:, :, :], a["masks"].rearrange("p (l t) -> p l t", l=LEVELS)).then_inc(const_in, 16)
            act.dma_start(craw[:, :], a["c"].rearrange("b (p k) -> (b p) k", p=P)).then_inc(const_in, 16)
            act.dma_start(x[:, :, :], a["x"].rearrange("b (t p) d -> p (b t) d", p=P)).then_inc(const_in, 16)
            act.wait_ge(const_in, 16 * 9)
            A(cact[:, :], craw[:, :], ACT.Silu).then_inc(silu_c, 1)

            def small_params(l):
                rows = [(R_CW, 48, a["ssd_conv_w"][l].rearrange("w (c p) -> (w c) p", p=P)),
                        (R_CB, 12, a["ssd_conv_b"][l].rearrange("(c p) -> c p", p=P)),
                        (R_LCW, 16, a["lru_conv_w"][l].rearrange("w (c p) -> (w c) p", p=P))]
                rows += [(r, n, a[k][l].rearrange("(c p) -> c p", p=P)) for r, n, k in (
                    (R_LCB, 4, "lru_conv_b"), (R_BA, 4, "lru_ba"), (R_BX, 4, "lru_bx"), (R_LAM, 4, "lru_lambda"),
                    (R_LNW, 4, "lru_norm_w"), (R_HNW, 4, "hg_norm_w"), (R_SNW, 8, "ssd_norm_w"))]
                rows.append((R_LB, 4 * L, a["hg_lower_bounds"].rearrange("l (c p) -> (l c) p", p=P)))
                for r, n, src in rows:
                    act.dma_start(prow[r:r + n, l, :], src).then_inc(params_in, 16)
                for i, k in enumerate(("norm_mix_w", "norm_ffn_w")):
                    act.dma_start(pall[:, l, KD * i:KD * i + KD],
                                  a[k][l].rearrange("(p k) -> p k", p=P)).then_inc(params_in, 16)
                for i, k in enumerate(("ssd_dt_bias", "ssd_a_log", "ssd_d")):
                    c = 2 * KD + SSD_HEADS * i
                    act.dma_start(pall[:, l, c:c + SSD_HEADS], a[k][l].partition_broadcast(P)).then_inc(params_in, 16)
                act.dma_start(pall[:, l, P - E:P], a["router_bias"][l].partition_broadcast(P)).then_inc(params_in, 16)

            def block_weights(l):
                act.wait_ge(S["prow_ready"], 1)
                for i, k in enumerate(("lru_wa", "lru_wx")):
                    w = a[k][l].rearrange("(j b) i o -> b i j o", b=2)
                    for b in range(2):
                        act.dma_start(bd[64 * b:64 * b + 64, i, :, 64 * b:64 * b + 64], w[b]).then_inc(S["bd_in"], 16)

            def rms(src, done):
                for t in range(TT):
                    A(sqj[:, t, :], src[:, t, :], ACT.Square, accum_out=ss[:, t:t + 1]).then_inc(done, 1)
                act.wait_ge(done, TT)
                A(ss[:, 2:4], ss[:, 0:2], ACT.Sqrt, scale=1.0 / D, bias=eps[:, :]).then_inc(done, 1)

            def split_hi(l, j, n, n0, it):
                wait_unit(act, l, U_MOE + 3 * n0 + j, it)
                if not (isinstance(n, int) and n == 0):
                    act.wait_ge(S[f"x_used{j}"], n)
                A(whi[j][:, :], ring_unit(U_MOE + 3 * n0 + j), ACT.Copy).then_inc(S[f"x_hi{j}"], 1)

            def silu_gate(side):
                A(sg[:, side, :], pb[4 + side][:, 0:DE], ACT.Silu).then_inc(S["silu_g"], 1)

            def tokens_hi(j, half):
                act.wait_ge(S["gathered"], 2 * j + half + 1)
                A(xeh[:, 4 * half:4 * half + 4, :], pb[6 + half][:, :].rearrange("p (k s) -> p k s", k=4),
                  ACT.Copy).then_inc(S["xe_hi"], 1)

            def put_copy(j):
                act.wait_ge(S["pick_turned"], j + 1)
                act.wait_ge(S["wslot"], j + 1)
                A(put[:, :], pb[6][:, 0:T], ACT.Copy).then_inc(S["put_ready"], 1)

            def hidden_hi(i):
                act.wait_ge(S["h_turned"], i + 1)
                A(hTh[:, :, :], pb[4][:, :].rearrange("p (k t) -> p k t", k=2), ACT.Copy).then_inc(S["h_hi"], 1)

            def sums_hi(j):
                act.wait_ge(S["x_used2"], 2 * j + 3)
                for half in range(2):
                    A(yhi[:, 512 * half:512 * half + 512], pb[6 + half][:, :], ACT.Copy).then_inc(S["y_hi"], 1)

            for l in range(L):
                small_params(l)
            act.wait_ge(eps_ready, 1)
            with act.Fori(0, L) as l:
                block_weights(l)
                rms(x, S["ss_mix"])
                def from_unit(i, dst, func, **kw):
                    wait_pe_unit(act, l, U_W + i)
                    return A(dst, pb[i % W_BANKS][:, :], func, **kw)

                for i in range(6):
                    act.wait_ge(S["conv"], 2 * i + 2)
                    A(xbcT[:, 2 * i:2 * i + 2, :], xbcT[:, 2 * i:2 * i + 2, :], ACT.Silu).then_inc(S["xbc_ready"], 1)
                act.wait_ge(S["dt_in"], 2)
                A(dts[:, 1, :], dts[:, 1, :], ACT.Exp).then_inc(S["dt_exp"], 1)
                act.wait_ge(S["pnow"], 1)
                A(hb[:, 1, :], hb[:, 1, :], ACT.Exp).then_inc(S["dt_exp"], 1)
                act.wait_ge(S["lb_in"], L)
                A(lbs[:, :, :], lbs[:, :, :], ACT.Exp).then_inc(S["lam_exp"], 1)
                act.wait_ge(S["lam_in"], 1)
                A(lruc[:, 1, :], lruc[:, 0, :], ACT.Exp).then_inc(S["lam_exp"], 1)
                act.wait_ge(S["dt_exp"], 2)
                A(dts[:, 1, :], dts[:, 1, :], ACT.Ln, bias=1.0).then_inc(S["dt_exp"], 1)
                act.wait_ge(S["lam_exp"], 2)
                A(lruc[:, 1, :], lruc[:, 1, :], ACT.Ln, bias=1.0).then_inc(S["lam_exp"], 1)
                for i in range(2):
                    from_unit(W_HF + i, qkg[:, 1, 2 * i:2 * i + 2, :], ACT.Sigmoid, scale=-1.0).then_inc(S["w_act"], 1)
                for i in range(2):
                    from_unit(W_HQ + i, qkg[:, 0, 2 * i:2 * i + 2, :], ACT.Silu).then_inc(S["w_act"], 1)
                act.wait_ge(S["dec_in"], 1)
                A(dts[:, 0, :], dts[:, 4, :], ACT.Exp).then_inc(S["eacum"], 1)
                A(dts[:, 5, :], dts[:, 5, :], ACT.Exp).then_inc(S["eacum"], 1)
                act.wait_ge(S["cb_done"], 1)
                A(cb[:, :, :], pb[4][:, :], ACT.Copy).then_inc(S["cb_ready"], 1)
                act.wait_ge(S["btok_done"], 1)
                A(btok[:, :, :], pb[5][:, 0:2 * P], ACT.Copy).then_inc(S["btok_ready"], 1)
                for i in range(4):
                    act.wait_ge(S["xs_turned"], i + 1)
                    A(xh[:, i // 2, 512 * (i % 2):512 * (i % 2) + 512], pb[(6, 7, 4, 5)[i]][:, :],
                      ACT.Copy).then_inc(S["xh_ready"], 1)
                for i in range(4):
                    wait_pe_unit(act, l, U_W + W_Z + i)
                    A(z[:, :, 256 * i:256 * i + 256], pb[(W_Z + i) % W_BANKS][:, :].rearrange("p (t c) -> p t c", t=TT),
                      ACT.Silu).then_inc(S["w_act"], 1)
                for g in range(2):
                    act.wait_ge(S["st_done"], g + 1)
                    A(stT[:, g, :], pb[3][:, :], ACT.Copy).then_inc(S["st_ready"], 1)
                for q in range(8):
                    act.wait_ge(S["diff_sub"], q + 1)
                    A(mdec[:, q % 2, :, :], mdec[:, q % 2, :, :], ACT.Exp).then_inc(S["diff_exp"], 1)
                act.wait_ge(S["y_gated"], 2)
                for i in range(4):
                    half = slice(512 * (i % 2), 512 * (i % 2) + 512)
                    A(xh[:, i // 2, half], y[:, i // 2, half], ACT.Square,
                      accum_out=ss[:, i:i + 1]).then_inc(S["y_sq"], 1)
                act.wait_ge(S["y_sq"], 4)
                A(ss[:, :], ss[:, :], ACT.Sqrt, scale=1.0 / 512, bias=eps[:, :]).then_inc(S["y_sq"], 1)
                act.wait_ge(S["k_ready"], 1)
                act.wait_ge(S["st_done"], 2)
                A(bT, qkg[:, 1, :, :], ACT.Ln, scale=-1.0, bias=1.0).then_inc(S["logf"], 1)

                def decay(i):
                    act.wait_ge(S["lev_in"], 2 * i)
                    A(lev_e[i % 2], lev_e[i % 2], ACT.Exp).then_inc(S["lev_exp"], 1)

                for i in range(6):
                    decay(i + 1)
                    k = i % 2
                    if i < 2:
                        wait_pe_unit(act, l, U_W + W_HV + k)
                        A(v[:, :, 256 * k:256 * k + 256],
                          pb[(W_HV + k) % W_BANKS][:, :].rearrange("p (t c) -> p t c", t=TT),
                          ACT.Copy).then_inc(S["w_act"], 1)
                    elif i < 4:
                        from_unit(W_LG + k, lru_g[:, 2 * k:2 * k + 2, :], ACT.Gelu_apprx_tanh).then_inc(S["w_act"], 1)
                    else:
                        from_unit(W_HG + k, qkg[:, 2, 2 * k:2 * k + 2, :], ACT.Silu).then_inc(S["w_act"], 1)
                decay(LEVELS - 1)
                act.wait_ge(S["gate_mm"], 1)
                for k, dst, r in ((0, lru_r, R_BA), (1, lru_i, R_BX)):
                    for j in range(LRU_J):
                        A(dst[:, j, :], pb[2 * k + j // 2][:, T * (j % 2):T * (j % 2) + T], ACT.Sigmoid,
                          bias=pcol[:, r + j:r + j + 1]).then_inc(S["gate_sig"], 1)
                decay(LEVELS)
                act.wait_ge(S["gate_sig"], 8)
                act.wait_ge(S["lruc_ready"], 1)
                for j in range(LRU_J):
                    A(lru_v[:, j, :], lru_r[:, j, :], ACT.Tanh, scale=lruc[:, 2, j:j + 1]).then_inc(S["lru_tanh"], 1)
                act.wait_ge(S["cross_done"], 1)
                A(cross, pb[4][:, :], ACT.Copy).then_inc(S["cross_ready"], 1)
                for j in range(LRU_J):
                    A(lru_a[:, j, :], lru_r[:, j, :], ACT.Exp, scale=lruc[:, 3, j:j + 1]).then_inc(S["lru_tanh"], 1)
                act.wait_ge(S["o_done"], 1)
                for i in range(2):
                    A(lev_e[0][:, 2 * i:2 * i + 2, :], pb[4 + i][:, :], ACT.Square).then_inc(S["o_sq"], 1)
                act.wait_ge(S["lru_w"], 1)
                A(lru_u, lru_u, ACT.Sqrt).then_inc(S["lru_sqrt"], 1)
                act.wait_ge(S["o_sum"], 1)
                for i in range(2):
                    A(lev_e[1][:, 2 * i:2 * i + 2, :], pb[6 + i][:, :], ACT.Sqrt, scale=1.0 / P,
                      bias=eps[:, :]).then_inc(S["o_root"], 1)
                act.wait_ge(S["lru_y"], 1)
                A(lru_v, lru_r, ACT.Square).then_inc(S["lru_sq"], 1)
                act.wait_ge(S["lru_sum"], 1)
                A(tmp[:, 0:T], pb[4][:, 0:T], ACT.Sqrt, scale=1.0 / 512, bias=eps[:, :]).then_inc(S["lru_root"], 1)

                act.wait_ge(S["x_mid"], 4)
                act.dma_start(rw[:, :, :], a["router_w"][l].rearrange("(p k) e -> p k e", p=P)).then_inc(S["router_in"], 16)
                rms2 = S["ss_ffn"]
                for t in range(TT):
                    A(xn2[:, t, :], x[:, t, :], ACT.Square, accum_out=ss[:, t:t + 1]).then_inc(rms2, 1)
                act.wait_ge(rms2, TT)
                A(ss[:, 2:4], ss[:, 0:2], ACT.Sqrt, scale=1.0 / D, bias=eps[:, :]).then_inc(rms2, 1)
                for j in range(4):
                    act.wait_ge(S["h2_ready"], 2 * j + 2)
                    A(xhi[:, 2 * j:2 * j + 2, :], h2T[:, 2 * j:2 * j + 2, :], ACT.Copy).then_inc(S["x_hi"], 1)
                act.wait_ge(S["logits"], 1)
                A(sc[:, :, :], pb[7][:, 0:TT * E], ACT.Sigmoid).then_inc(S["scores"], 1)
                for j in range(4):
                    act.wait_ge(S["rows_turned"], j + 1)
                    A(xth[:, j // 2, 512 * (j % 2):512 * (j % 2) + 512], pb[j][:, :], ACT.Copy).then_inc(S["xt_hi"], 1)
                split_hi(l, 0, 0, 0, 0)
                split_hi(l, 1, 0, 0, 0)
                split_hi(l, 2, 0, 0, 0)
                act.wait_ge(S["x_used1"], 1)
                silu_gate(0)
                silu_gate(1)
                hidden_hi(0)
                split_hi(l, 0, 1, 1, 0)
                split_hi(l, 1, 1, 1, 0)
                tokens_hi(0, 0)
                tokens_hi(0, 1)

                def pair_step(j, j0, first=False, last=False):
                    it = 0 if isinstance(j, int) else j
                    third = lambda i: (2 * j + i, 2 * j0 + i)
                    if not first:
                        sums_hi(j - 1)
                    split_hi(l, 2, *third(1), it)
                    split_hi(l, 0, *third(2), it)
                    split_hi(l, 1, *third(2), it)
                    put_copy(j)
                    act.wait_ge(S["x_used2"], 2 * j + 2)
                    silu_gate(0)
                    split_hi(l, 2, *third(2), it)
                    act.wait_ge(S["x_used0"], 2 * j + 3)
                    silu_gate(1)
                    if not last:
                        tokens_hi(j + 1, 0)
                    hidden_hi(j + 1)
                    if not last:
                        tokens_hi(j + 1, 1)
                        split_hi(l, 0, *third(3), it)
                        split_hi(l, 1, *third(3), it)

                pair_step(0, 0, first=True)
                with act.Fori(1, PAIRS - 1) as j:
                    pair_step(j, 0)
                pair_step(PAIRS - 1, PAIRS - 1, last=True)
                sums_hi(PAIRS - 1)

                def overflow(l, e, i):
                    act.wait_ge(S["over_pe"], 5 * i + 2)
                    for half in range(2):
                        A(h2T[:, 4 * half:4 * half + 4, 0:SLOTS], pb[(5, 7)[half]][:, :].rearrange("p (k s) -> p k s", k=4),
                          ACT.Copy).then_inc(S["over_act"], 1)
                    act.wait_ge(S["over_pe"], 5 * i + 3)
                    act.wait_ge(S["over_dve"], 3 * i + 1)
                    A(put[:, :], pb[6][:, 0:T], ACT.Copy).then_inc(S["over_act"], 1)
                    act.wait_ge(S["over_pe"], 5 * i + 4)
                    A(sg[:, 0, :], pb[4][:, 0:DE], ACT.Silu).then_inc(S["over_act"], 1)


                def overflow_skip(i, n):
                    act.wait_ge(S["over_x"], 4 * i + 4)
                    act.sem_inc(S["over_act"], 4 * n)

                overflow_pass(act, l, overflow, overflow_skip)
                act.sem_inc(S["end_act"], 1)
                act.wait_ge(layer_done, l + 1)

            act.dma_start(fnw[:, :], a["final_norm_w"].partition_broadcast(P)).then_inc(const_in, 16)
            for t in range(TT):
                A(xo[:, t, :], x[:, t, :], ACT.Square, accum_out=ss[:, t:t + 1]).then_inc(fin_sq, 1)
            act.wait_ge(fin_sq, TT)
            A(ss[:, 2:4], ss[:, 0:2], ACT.Sqrt, scale=1.0 / D, bias=eps[:, :]).then_inc(fin_sq, 1)

        @block.gpsimd
        def _(pool):
            G = nc.gpsimd
            w = a["ada_w"].rearrange("l (p k) (g c) -> l g p k c", p=P, g=6)
            bias = a["ada_b"].rearrange("l (i c) -> (l i) c", i=2)

            def load(l, i, v):
                pool.dma_start(ada_w[:, v % ADA_BUFS, :],
                               w[l, 3 * i + v // KD, :, v % KD, :]).then_inc(ada_full[v % ADA_BUFS], 16)

            def clear_sums(b):
                G.memset(ada_acc[:, :, :], 0.0).then_inc(ada_zero, 1)
                pool.wait_ge(ada_zero, b + 1)
                pool.dma_start(ada_acc[0:1, :, :].rearrange("o g c -> o (g c)"), bias[b:b + 1, :] if isinstance(b, int)
                               else bias[bass.ds(b, 1), :]).then_inc(ada_bias, 16)

            def ada_block(l, i, last=False):
                b = 2 * l + i
                pool.wait_ge(ada_taken, b)
                clear_sums(b)
                done = ADA_STEPS * (b - 1)
                for v in range(ADA_STEPS):
                    part, k, buf = v // KD, v % KD, ada_w[:, v % ADA_BUFS, :]
                    pool.wait_ge(ada_full[v % ADA_BUFS],
                                 16 * (ADA_STEPS // ADA_BUFS * (b - 1) + v // ADA_BUFS + 1))
                    G.tensor_scalar(buf, buf, cact[:, k:k + 1], None, ALU.mult).then_inc(ada_prod, 1)
                    pool.wait_ge(ada_prod, done + v + 1)
                    if v == 0:
                        pool.wait_ge(ada_bias, 16 * b + 16)
                    if v % KD:
                        pool.wait_ge(ada_sum, ADA_STEPS * b + v)
                    G.tensor_tensor(ada_acc[:, part, :], ada_acc[:, part, :], buf, ALU.add).then_inc(ada_sum, 1)
                    nxt = v + ADA_BUFS
                    if nxt < ADA_STEPS or not last:
                        pool.wait_ge(ada_sum, ADA_STEPS * b + v + 1)
                        nl, ni = (l, i) if nxt < ADA_STEPS else (l, 1) if i == 0 else (l + 1, 0)
                        load(nl, ni, nxt % ADA_STEPS)

            clear_sums(0)
            pool.wait_ge(ada_sum, ADA_STEPS)
            for v in range(ADA_BUFS):
                load(0, 1, v)
            pool.wait_ge(silu_c, 1)
            with pool.Fori(1, L) as l:
                ada_block(l - 1, 1)
                ada_block(l, 0)
            ada_block(L - 1, 1, last=True)

        @block.vector
        def _(dve):
            V = nc.vector
            order = [0]

            def link(ins):
                order[0] += 1
                ins.then_inc(S["dve_order"], 1)
                dve.wait_ge(S["dve_order"], order[0])

            def own(ins, s, value):
                ins.then_inc(s, 1)
                dve.wait_ge(s, value)

            def normed(src, dst, root, ready):
                dve.wait_ge(root, TT + 1)
                link(V.reciprocal(rstd[:, :], ss[:, 2:4]))
                for t in range(TT):
                    V.tensor_scalar(dst[:, t, :], src[:, t, :], rstd[:, t:t + 1], None, ALU.mult).then_inc(ready, 1)

            def modulation(i, bank):
                dve.wait_ge(S["ada_cols"], i + 1)
                V.tensor_copy(modc[:, i, 1, :], bank[:, 0:KD]).then_inc(S["modc_s"], 1)
                own(V.scalar_tensor_tensor(modc[:, i, 0, :], bank[:, KD:2 * KD], 1.0, norm_w[:, i, :], ALU.add, ALU.mult),
                    S["modc"], i + 1)
                dve.wait_ge(S["modc_s"], i + 1)

            def conv(i, dst, w_row, chunks, b_row, done):
                for s in range(4):
                    for c in range(2):
                        ch = chunks + c
                        src = pb[i % W_BANKS][:, T * c:T * c + T]
                        acc = dst[:, ch, :]
                        wc = w_row[0] + w_row[1] * (3 - s) + ch
                        w = pcol[:, wc:wc + 1]
                        if s == 0:
                            ins = V.tensor_scalar(acc, src, w, pcol[:, b_row + ch:b_row + ch + 1], ALU.mult, ALU.add)
                        else:
                            ins = V.scalar_tensor_tensor(acc[:, s:T], src[:, 0:T - s], w, acc[:, s:T], ALU.mult, ALU.add)
                        if s < 3:
                            order[0] += 1
                            ins.then_inc(S["dve_order"], 1)
                        else:
                            ins.then_inc(done, 1)
                    if s < 3:
                        dve.wait_ge(S["dve_order"], order[0])

            def split_lo(l, j, n, n0, it):
                dve.wait_ge(S[f"x_hi{j}"], n + 1)
                V.tensor_tensor(wlo[j][:, :], ring_unit(U_MOE + 3 * n0 + j), whi[j][:, :].bitcast(fp32),
                                ALU.subtract).then_inc(x_lo[j], 1)

            def hidden(j, side):
                dve.wait_ge(S["silu_g"], TT + 2 * j + side + 1)
                dve.wait_ge(S["wslot"], j + 1)
                V.scalar_tensor_tensor(h[:, side, :], sg[:, side, :], wslot[:, side:side + 1], pb[4 + side][:, DE:2 * DE],
                                       ALU.mult, ALU.mult).then_inc(S["h_ready"], 1)

            def tokens_lo(j, half):
                dve.wait_ge(S["xe_hi"], 2 * j + half + 1)
                V.tensor_tensor(xel[:, 4 * half:4 * half + 4, :], pb[6 + half][:, :].rearrange("p (k s) -> p k s", k=4),
                                xeh[:, 4 * half:4 * half + 4, :].bitcast(fp32), ALU.subtract).then_inc(S["xe_lo"], 1)

            def column(tile, t, n):
                return tile[:, t, n:n + 1] if isinstance(n, int) else tile[:, t, bass.ds(n, 1)]

            def make_pick(j):
                if not isinstance(j, int) or j > 0:
                    dve.wait_ge(S["pick_turned"], j)
                for t in range(TT):
                    V.tensor_scalar(pick0[:, t, :], iota[:, :], column(place, t, 2 * j + 1), None,
                                    ALU.is_equal).then_inc(S["pick0"], 1)
                dve.wait_ge(S["pick0"], TT * (j + 1))
                for t in range(TT):
                    V.scalar_tensor_tensor(pick[:, t, :], iota[:, :], column(place, t, 2 * j + 2), pick0[:, t, :],
                                           ALU.is_equal, ALU.add).then_inc(S["pick"], 1)

            def slot_weights(j):
                dve.wait_ge(S["pick_turned"], j + 1)
                dve.wait_ge(S["h_ready"], TT + 2 * j)
                own_slots = mine[:, 2 * j + 1:2 * j + 3] if isinstance(j, int) else mine[:, bass.ds(2 * j + 1, 2)]
                V.tensor_tensor(wslot[:, :], pb[6][:, T:T + 2], own_slots, ALU.mult).then_inc(S["wslot"], 1)

            def hidden_lo(i):
                dve.wait_ge(S["h_hi"], i + 1)
                V.tensor_tensor(hTl[:, :, :], pb[4][:, :].rearrange("p (k t) -> p k t", k=2), hTh[:, :, :].bitcast(fp32),
                                ALU.subtract).then_inc(S["h_lo"], 1)

            def sums_lo(j):
                for half in range(2):
                    c = slice(512 * half, 512 * half + 512)
                    dve.wait_ge(S["y_hi"], 2 * j + half + 1)
                    V.tensor_tensor(ylo[:, c], pb[6 + half][:, :], yhi[:, c].bitcast(fp32), ALU.subtract).then_inc(S["y_lo"], 1)

            V.memset(eps[:, :], EPS).then_inc(eps_ready, 1)
            dve.wait_ge(const_in, 16 * 9)
            dve.wait_ge(silu_c, 1)
            dve.wait_ge(ada_bias, 16)
            for v in range(ADA_STEPS):
                part, k = divmod(v, KD)
                if k == 0:
                    dve.wait_ge(first_in[part], 64)
                V.scalar_tensor_tensor(ada_acc[:, part, :], ada_first[:, part % 2, k, :], cact[:, k:k + 1],
                                       ada_acc[:, part, :], ALU.mult, ALU.add).then_inc(ada_sum, 1)
                dve.wait_ge(ada_sum, v + 1)
            dve.wait_ge(params_in, 16 * 17 * L)
            with dve.Fori(0, L) as l:
                order[0] = 0
                V.memset(bd[:, :, :, :], 0.0).then_inc(S["prow_ready"], 1)
                V.tensor_copy(prow_now[0:R_END, :],
                              prow[0:R_END, bass.ds(l, 1), :].rearrange("r l p -> r (l p)")).then_inc(S["prow_ready"], 1)
                dve.wait_ge(S["params_turned"], 1)
                own(V.tensor_copy(pcol[:, :], pb[1][:, 0:R_END]), S["pcol"], 1)
                own(V.tensor_copy(pnow[:, :], pall[:, bass.ds(l, 1), :].rearrange("p l c -> p (l c)")), S["pnow"], 1)
                modulation(0, pb[0])
                normed(x, xn, S["ss_mix"], S["xn_ready"])
                for kk in range(KD):
                    dve.wait_ge(S["h_chunks"], kk // 2 + 1)
                    V.tensor_scalar(hT[:, kk, :], pb[4 + kk // 2][:, T * (kk % 2):T * (kk % 2) + T],
                                    modc[:, 0, 0, kk:kk + 1], modc[:, 0, 1, kk:kk + 1], ALU.mult,
                                    ALU.add).then_inc(S["hT_ready"], 1)
                dve.wait_ge(ada_taken, 2 * l + 1)
                for i in range(2):
                    V.tensor_copy(gates[:, 0, 512 * i:512 * i + 512], pb[2 + i][:, :]).then_inc(S["gates_m"], 1)

                lb = pcol[:, R_LB:R_LB + L * HG_H].rearrange("p (l h) -> p l h", l=L)
                link(V.tensor_copy(lbt[:, 0, :], lb[:, 0, :]))
                for i in range(1, L):
                    link(V.tensor_tensor(lbt[:, 0, :], lbt[:, 0, :], lb[:, i, :], ALU.max))
                for i in range(L):
                    V.tensor_tensor(lbs[:, i, :], lb[:, i, :], lbt[:, 0, :], ALU.subtract).then_inc(S["lb_in"], 1)
                lam = pcol[:, R_LAM:R_LAM + LRU_J]
                V.scalar_tensor_tensor(lruc[:, 0, :], lam, -1.0, lam, ALU.mult, ALU.min).then_inc(S["lam_in"], 1)

                for i in range(6):
                    wait_pe_unit(dve, l, U_W + i)
                    conv(i, xbcT, (R_CW, CH_XBC), 2 * i, R_CB, S["conv"])
                wait_pe_unit(dve, l, U_W + W_DT)
                s2 = lambda i: dts[:, i, :].rearrange("p (t h) -> p t h", t=TT)
                own(V.tensor_tensor(s2(0), pb[W_DT % W_BANKS][:, 0:32].rearrange("p (t h) -> p t h", t=TT),
                                    bcast(hb[:, 0, :], 1, TT), ALU.add), S["dt_in"], 1)
                V.scalar_tensor_tensor(dts[:, 1, :], dts[:, 0, :], -1.0, dts[:, 0, :], ALU.mult,
                                       ALU.min).then_inc(S["dt_in"], 1)
                dve.wait_ge(S["lam_exp"], 1)
                link(V.tensor_copy(lbt[:, 1, :], lbs[:, 0, :]))
                link(V.tensor_copy(lbt[:, 2, :], lbs[:, 0, :]))
                for i in range(1, L):
                    link(V.tensor_tensor(lbt[:, 1, :], lbt[:, 1, :], lbs[:, i, :], ALU.add))
                link(V.reciprocal(lbt[:, 1, :], lbt[:, 1, :]))
                link(V.tensor_tensor(lbs[:, :, :], lbs[:, :, :], bcast(lbt[:, 1, :], 1, L), ALU.mult))
                link(V.tensor_copy(lbt[:, 2, :], lbs[:, 0, :]))
                for i in range(1, L):
                    link(V.tensor_tensor(lbs[:, i, :], lbs[:, i, :], lbs[:, i - 1, :], ALU.add))
                link(V.tensor_tensor(lbs[:, :, :], lbs[:, :, :], bcast(lbt[:, 2, :], 1, L), ALU.subtract))
                link(V.tensor_scalar(lbs[:, :, :], lbs[:, :, :], -1.0, 1.0, ALU.mult, ALU.add))
                link(V.tensor_copy(omlb[:, :], lbs[:, bass.ds(l, 1), :].rearrange("p l h -> p (l h)")))
                dve.wait_ge(S["lam_exp"], 3)
                link(V.tensor_scalar(lruc[:, 0, :], lam, -1.0, 0.0, ALU.mult, ALU.max))
                link(V.tensor_tensor(lruc[:, 1, :], lruc[:, 0, :], lruc[:, 1, :], ALU.add))
                link(V.tensor_scalar(lruc[:, 2, :], lruc[:, 1, :], 8.0, None, ALU.mult))
                V.tensor_scalar(lruc[:, 3, :], lruc[:, 1, :], -8.0, None, ALU.mult).then_inc(S["lruc_ready"], 1)
                dve.wait_ge(S["dt_exp"], 3)
                link(V.scalar_tensor_tensor(dts[:, 2, :], dts[:, 0, :], 0.0, dts[:, 1, :], ALU.max, ALU.add))
                V.scalar_tensor_tensor(s2(3), s2(2), -1.0, bcast(hb[:, 1, :], 1, TT), ALU.mult,
                                       ALU.mult).then_inc(S["a_ready"], 1)
                dve.wait_ge(S["acum_done"], 1)
                link(V.tensor_copy(dts[:, 4, :], pb[3][:, 0:32]))
                V.tensor_tensor(dts[:, 5, :], pb[3][:, 32:64], dts[:, 4, :], ALU.subtract).then_inc(S["dec_in"], 1)
                dve.wait_ge(S["w_act"], 2)
                V.tensor_tensor(qkg[:, 1, :, :], qkg[:, 1, :, :], bcast(omlb[:, :], 2, T), ALU.mult).then_inc(S["k_ready"], 1)
                heads = lambda ap: ap.rearrange("p (h d) -> p h d", d=SSD_HD)
                for c in range(2):
                    dve.wait_ge(S["xh_ready"], 2 * c + 2)
                    own(V.tensor_tensor(heads(xdt[:, c, :]), heads(xh[:, c, :]),
                                        bcast(dts[:, 2, 16 * c:16 * c + 16], 2, SSD_HD), ALU.mult), S["xdt_ready"], c + 1)
                    if c == 0:
                        dve.wait_ge(S["eacum"], 2)
                        V.tensor_tensor(heads(xdec[:, :]), heads(xdt[:, 0, :]), bcast(dts[:, 5, 0:16], 2, SSD_HD),
                                        ALU.mult).then_inc(S["xdec_ready"], 1)
                    link(V.tensor_tensor(heads(y[:, c, :]), heads(xh[:, c, :]), bcast(hb[:, 2, :], 2, SSD_HD), ALU.mult))

                dve.wait_ge(S["cb_ready"], 1)

                def diff(q):
                    c, h0 = q // 4, 4 * (q % 4)
                    dve.wait_ge(S["diff_done"], q + 1)
                    if q >= 2:
                        dve.wait_ge(S["ydiag"], q - 1)
                    V.tensor_tensor(mdec[:, q % 2, :, :], pb[4 + q % 2][:, :].rearrange("p (h t) -> p h t", h=4),
                                    bcast(dts[:, 4, 16 * c + h0:16 * c + h0 + 4], 2, P), ALU.subtract).then_inc(S["diff_sub"], 1)

                def masked(q):
                    c, g = q // 4, (q % 4) // 2
                    dve.wait_ge(S["diff_exp"], q + 1)
                    V.tensor_tensor(mdec[:, q % 2, :, :], mdec[:, q % 2, :, :], bcast(cb[:, 2 * c + g, :], 1, 4),
                                    ALU.mult).then_inc(S["m_ready"], 1)

                def y_group(i):
                    c, g = divmod(i, 2)
                    part = y[:, c, 512 * g:512 * g + 512]
                    dve.wait_ge(S["ydiag"], 2 * i + 2)
                    own(V.tensor_tensor(part, part, pb[6 + i % 2][:, :], ALU.add), S["y_taken"], i + 1)
                    if c == 1:
                        dve.wait_ge(S["yoff"], g + 1)
                        dve.wait_ge(S["eacum"], 1)
                        own(V.tensor_tensor(heads(tmp[:, :]), heads(pb[3][:, :]),
                                            bcast(dts[:, 0, 16 + 8 * g:24 + 8 * g], 2, SSD_HD), ALU.mult), S["yoff_taken"], g + 1)
                        link(V.tensor_tensor(part, part, tmp[:, :], ALU.add))

                for q in range(9):
                    if q < 8:
                        diff(q)
                    if q:
                        masked(q - 1)
                    if q in (3, 5, 7):
                        y_group((q - 3) // 2)
                y_group(3)

                def conv_lx(i):
                    wait_pe_unit(dve, l, U_W + W_LX + i)
                    conv(W_LX + i, lru_x, (R_LCW, LRU_J), 2 * i, R_LCB, S["conv_lx"])

                dve.wait_ge(S["w_act"], 8)
                for c in range(2):
                    own(V.tensor_tensor(y[:, c, :], y[:, c, :], z[:, c, :], ALU.mult), S["y_gated"], c + 1)
                link(V.memset(attn, 0.0))
                dve.wait_ge(S["y_sq"], 5)
                link(V.reciprocal(ss[:, :], ss[:, :]))
                for i in range(4):
                    part = y[:, i // 2, 512 * (i % 2):512 * (i % 2) + 512]
                    V.tensor_scalar(part, part, ss[:, i:i + 1], None, ALU.mult).then_inc(S["y_norm"], 1)
                conv_lx(0)
                for i in range(4):
                    c, g = divmod(i, 2)
                    dve.wait_ge(S["y_turned"], i + 1)
                    V.tensor_tensor(yT[:, 4 * g:4 * g + 4, P * c:P * c + P],
                                    pb[4 + i][:, :].rearrange("p (k t) -> p k t", k=4),
                                    bcast(pcol[:, R_SNW + 4 * g:R_SNW + 4 * g + 4], 2, P), ALU.mult).then_inc(S["yT_ready"], 1)

                q_, k_, g_ = (qkg[:, i, :, :] for i in range(3))
                dve.wait_ge(S["logf"], 1)
                for hd in range(HG_H):
                    for t in range(TT):
                        seg = bT[:, hd, P * t:P * t + P]
                        order[0] += 1
                        V.tensor_tensor_scan(seg, ones[:, :], seg, 0.0, ALU.mult, ALU.add).then_inc(S["dve_order"], 1)
                dve.wait_ge(S["w_act"], 4)
                for i in range(2):
                    for src, buf in ((q_, lev_q), (k_, lev_k)):
                        order[0] += 1
                        V.tensor_copy(buf[i], src).then_inc(S["dve_order"], 1)
                dve.wait_ge(S["dve_order"], order[0])
                halves = lambda ap, m: ap.rearrange("p h (b s m) -> p (h b) s m", s=2, m=m)

                def level_in(i):
                    m = 1 << (i - 1)
                    e, b = halves(lev_e[i % 2], m), halves(bT, m)
                    r = b[:, :, 0, m - 1:m]
                    r = r.broadcast_to(list(r.shape[:2]) + [m])
                    if i >= 3:
                        dve.wait_ge(S["lev_ready"], 2 * (i - 2))
                    V.tensor_tensor(e[:, :, 1, :], b[:, :, 1, :], r, ALU.subtract).then_inc(S["lev_in"], 1)
                    V.tensor_tensor(e[:, :, 0, :], r, b[:, :, 0, :], ALU.subtract).then_inc(S["lev_in"], 1)

                def level_out(i):
                    m = 1 << (i - 1)
                    e, lq, lk = (halves(ap, m) for ap in (lev_e[i % 2], lev_q[i % 2], lev_k[i % 2]))
                    dve.wait_ge(S["lev_exp"], i)
                    if i >= 3:
                        dve.wait_ge(S["att_done"], i - 1)
                    V.tensor_tensor(lq[:, :, 1, :], halves(q_, m)[:, :, 1, :], e[:, :, 1, :], ALU.mult).then_inc(S["lev_ready"], 1)
                    V.tensor_tensor(lk[:, :, 0, :], halves(k_, m)[:, :, 0, :], e[:, :, 0, :], ALU.mult).then_inc(S["lev_ready"], 1)

                def take(i):
                    dve.wait_ge(S["att_done"], i + 1)
                    for j in range(2):
                        V.copy_predicated(attn[:, 4 * j:4 * j + 4, :], bcast(masks[:, i, :], 1, 4),
                                          pb[4 + 2 * (i % 2) + j][:, :].rearrange("p (g t) -> p g t", g=4)).then_inc(S["att_taken"], 1)

                e, lq, lk = lev_e[0], lev_q[0], lev_k[0]
                level_in(1)
                conv_lx(1)
                for i in range(1, LEVELS):
                    if i + 1 < LEVELS:
                        level_in(i + 1)
                    else:
                        r = bT[:, :, P - 1:P].broadcast_to([P, HG_H, P])
                        dve.wait_ge(S["lev_ready"], 2 * (LEVELS - 2))
                        V.tensor_copy(e[:, :, P:T], bT[:, :, P:T]).then_inc(S["lev_in"], 1)
                        V.tensor_tensor(e[:, :, 0:P], r, bT[:, :, 0:P], ALU.subtract).then_inc(S["lev_in"], 1)
                    take(i - 1)
                    level_out(i)
                take(LEVELS - 1)
                dve.wait_ge(S["lev_exp"], LEVELS)
                dve.wait_ge(S["att_done"], LEVELS - 1)
                V.tensor_tensor(lq[:, :, P:T], q_[:, :, P:T], e[:, :, P:T], ALU.mult).then_inc(S["lev_ready"], 1)
                V.tensor_tensor(lk[:, :, 0:P], k_[:, :, 0:P], e[:, :, 0:P], ALU.mult).then_inc(S["lev_ready"], 1)
                dve.wait_ge(S["lru_tanh"], LRU_J)
                link(V.tensor_scalar(lru_u, lru_v, 1.0, None, ALU.add))
                link(V.reciprocal(lru_u, lru_u))
                flat = lambda ap: ap.rearrange("p j t -> p (j t)")
                V.scalar_tensor_tensor(flat(lru_u), flat(lru_v), 2.0, flat(lru_u), ALU.mult, ALU.mult).then_inc(S["lru_w"], 1)
                dve.wait_ge(S["gate_sig"], 8)
                link(V.tensor_tensor(lru_i, lru_i, lru_x[:, :, :], ALU.mult))
                for i in range(2):
                    e2 = lev_e[1][:, 2 * i:2 * i + 2, :]
                    dve.wait_ge(S["o_root"], i + 1)
                    link(V.reciprocal(e2, e2))
                    link(V.tensor_tensor(lev_q[0][:, 2 * i:2 * i + 2, :], pb[4 + i][:, :].rearrange("p (h t) -> p h t", h=2),
                                         e2, ALU.mult))
                dve.wait_ge(S["w_act"], 14)
                for hd in range(HG_H):
                    V.scalar_tensor_tensor(yT[:, 8 + hd, :], lev_q[0][:, hd, :], pcol[:, R_HNW + hd:R_HNW + hd + 1],
                                           g_[:, hd, :], ALU.mult, ALU.mult).then_inc(S["yT_ready"], 1)

                dve.wait_ge(S["lru_sqrt"], 1)
                link(V.tensor_tensor(lru_u, lru_u, lru_i, ALU.mult))
                dve.wait_ge(S["lru_tanh"], 2 * LRU_J)
                link(V.memset(lru_a[:, :, 0:1], 0.0))
                link(V.tensor_tensor_scan(flat(lru_r), flat(lru_a), flat(lru_u), 0.0, ALU.mult, ALU.add))
                own(V.tensor_tensor(lru_r, lru_r, lru_g[:, :, :], ALU.mult), S["lru_y"], 1)
                dve.wait_ge(S["lru_root"], 1)
                link(V.reciprocal(tmp[:, 0:T], tmp[:, 0:T]))
                link(V.tensor_tensor(lru_i, lru_r, bcast(tmp[:, 0:T], 1, LRU_J), ALU.mult))
                V.tensor_tensor(yT[:, 12:16, :], lru_i, bcast(pcol[:, R_LNW:R_LNW + LRU_J], 2, T),
                                ALU.mult).then_inc(S["yT_ready"], 1)

                modulation(1, pb[5])
                dve.wait_ge(ada_taken, 2 * l + 2)
                for i in range(2):
                    V.tensor_copy(gates[:, 1, 512 * i:512 * i + 512], pb[6 + i][:, :]).then_inc(S["gates_f"], 1)
                wait_pe_unit(dve, l, U_OUT + 7)
                dve.wait_ge(S["gates_m"], 2)
                for i in range(4):
                    t, half = divmod(i, 2)
                    cols = slice(512 * half, 512 * half + 512)
                    link(V.tensor_tensor(tmp[:, :], pb[i][:, :], gates[:, 0, cols], ALU.mult))
                    own(V.tensor_tensor(x[:, t, cols], x[:, t, cols], tmp[:, :], ALU.add), S["x_mid"], i + 1)

                normed(x, xn2, S["ss_ffn"], S["xn2_ready"])
                for kk in range(KD):
                    dve.wait_ge(S["h2_chunks"], kk // 2 + 1)
                    V.tensor_scalar(h2T[:, kk, :], pb[kk // 2][:, T * (kk % 2):T * (kk % 2) + T],
                                    modc[:, 1, 0, kk:kk + 1], modc[:, 1, 1, kk:kk + 1], ALU.mult,
                                    ALU.add).then_inc(S["h2_ready"], 1)
                for j in range(4):
                    dve.wait_ge(S["x_hi"], j + 1)
                    V.tensor_tensor(xlo[:, 2 * j:2 * j + 2, :], h2T[:, 2 * j:2 * j + 2, :],
                                    xhi[:, 2 * j:2 * j + 2, :].bitcast(fp32), ALU.subtract).then_inc(S["x_lo"], 1)
                for j in range(4):
                    dve.wait_ge(S["xt_hi"], j + 1)
                    part = (slice(None), j // 2, slice(512 * (j % 2), 512 * (j % 2) + 512))
                    V.tensor_tensor(xtl[part], pb[j][:, :], xth[part].bitcast(fp32), ALU.subtract).then_inc(S["xt_lo"], 1)
                split_lo(l, 0, 0, 0, 0)
                split_lo(l, 1, 0, 0, 0)
                dve.wait_ge(S["scores"], 1)
                link(V.tensor_tensor(sel[:, :, :], sc[:, :, :], bcast(rbias[:, :], 1, TT), ALU.add))
                for t in range(TT):
                    for g in range(8):
                        order[0] += 1
                        V.max(m8[:, t, g, :], sel[:, t, 8 * g:8 * g + 8]).then_inc(S["dve_order"], 1)
                dve.wait_ge(S["dve_order"], order[0])
                link(V.tensor_tensor(gsc[:, :, :], m8[:, :, :, 0], m8[:, :, :, 1], ALU.add))
                c0, c1 = (cmp_[:, i, :].rearrange("p (t i j) -> p t i j", t=TT, i=8) for i in range(2))
                other, self_ = bcast(gsc[:, :, :], 2, 8), bcast(gsc[:, :, :], 3, 8)
                link(V.tensor_tensor(c0, other, self_, ALU.is_equal))
                link(V.tensor_tensor(c0, c0, bcast(lt8[:, :].rearrange("p (i j) -> p i j", i=8), 1, TT), ALU.mult))
                link(V.tensor_tensor(c1, other, self_, ALU.is_gt))
                link(V.tensor_tensor(c0, c0, c1, ALU.add))
                link(V.tensor_reduce(gm[:, 0, :, :], c0, AXL.X, ALU.add))
                link(V.tensor_scalar(gm[:, 0, :, :], gm[:, 0, :, :], 3.5, None, ALU.is_lt))
                link(V.tensor_scalar(gm[:, 1, :, :], gm[:, 0, :, :], 1.0e4, -1.0e4, ALU.mult, ALU.add))
                by_group = lambda ap: ap.rearrange("p t (g e) -> p (t g) e", g=8)
                flat_g = lambda i: bcast(gm[:, i, :, :].rearrange("p t g -> p (t g)"), 2, 8)
                link(V.tensor_tensor(by_group(sel[:, :, :]), by_group(sel[:, :, :]), flat_g(0), ALU.mult))
                link(V.tensor_tensor(by_group(sel[:, :, :]), by_group(sel[:, :, :]), flat_g(1), ALU.add))
                for t in range(TT):
                    link(V.max(t8[:, t, :], sel[:, t, :]))
                    link(V.match_replace(rep[:, t, :], in_to_replace=t8[:, t, :], in_values=sel[:, t, :], imm_value=-3.0e4))
                own(V.tensor_tensor(chosen[:, :, :], rep[:, :, :], sel[:, :, :], ALU.not_equal), S["chosen"], 1)
                link(V.tensor_tensor(rep[:, :, :], chosen[:, :, :], sc[:, :, :], ALU.mult))
                link(V.tensor_reduce(wsum[:, 0, :], rep[:, :, :], AXL.X, ALU.add))
                link(V.reciprocal(wsum[:, 1, :], wsum[:, 0, :]))
                for t in range(TT):
                    V.tensor_scalar(wts[:, t, 1:E + 1], rep[:, t, :], wsum[:, 1, t:t + 1], SCALE, ALU.mult,
                                    ALU.mult).then_inc(S["wts"], 1)
                split_lo(l, 2, 0, 0, 0)
                dve.wait_ge(S["silu_g"], TT)
                for t in range(TT):
                    V.tensor_tensor(h[:, t, :], sg[:, t, :], pb[4 + t][:, DE:2 * DE], ALU.mult).then_inc(S["h_ready"], 1)
                hidden_lo(0)
                dve.wait_ge(S["placed"], 1)
                own_e = slice(1, E + 1)
                link(V.memset(place[:, :, :], -1.0))
                link(V.memset(mine[:, :], 0.0))
                link(V.tensor_tensor(place[:, :, own_e], pb[7][:, 0:TT * E].rearrange("p (t e) -> p t e", t=TT),
                                     chosen[:, :, :], ALU.mult))
                link(V.tensor_copy(counts[:, 0:E], pb[7][:, TT * E:(TT + 1) * E]))
                pairs = lambda ap: ap.rearrange("p (j s) -> p j s", s=2)
                room, left = pairc[:, 0, :], pairc[:, 1, :]
                for side in range(2):
                    link(V.tensor_scalar(pairs(room)[:, :, side], pairs(counts[:, 0:E])[:, :, 1 - side], -1.0, float(SLOTS),
                                         ALU.mult, ALU.add))
                link(V.tensor_scalar(room, room, SLOTS / 2.0, None, ALU.max))
                link(V.tensor_tensor(left, counts[:, 0:E], room, ALU.subtract))
                for c in range(2):
                    link(V.tensor_scalar(pairc[:, 2, :], left, SLOTS * c + 0.5, None, ALU.is_gt))
                    link(V.tensor_copy(over_e[:, c, :], pairc[:, 2, :]))
                    link(V.tensor_reduce(counts[:, E:E + 1], pairc[:, 2, :], AXL.X, ALU.max))
                    link(V.tensor_reduce(gsc[:, 0, :], pairc[:, 2, :].rearrange("p (g e) -> p g e", g=8), AXL.X, ALU.max))
                    link(V.tensor_copy(over_g[:, c, :], gsc[:, 0, :]))
                    link(V.tensor_copy(over[:, c:c + 1], counts[:, E:E + 1]))
                link(V.tensor_tensor(place2[:, :, own_e], place[:, :, own_e], bcast(room, 1, TT), ALU.subtract))
                link(V.tensor_scalar(place2[:, :, own_e], place2[:, :, own_e], -1.0, None, ALU.add))
                link(V.tensor_tensor(rep[:, :, :], place[:, :, own_e], bcast(room, 1, TT), ALU.is_le))
                link(V.tensor_tensor(place[:, :, own_e], place[:, :, own_e], rep[:, :, :], ALU.mult))
                by_pair = lambda side: place[:, :, own_e].rearrange("p t (j s) -> p t j s", s=2)[:, :, :, side]
                link(V.tensor_scalar(by_pair(0), by_pair(0), -1.0, None, ALU.add))
                link(V.tensor_scalar(by_pair(1), by_pair(1), -1.0, float(SLOTS), ALU.mult, ALU.add))
                link(V.tensor_reduce(rank[:, :], tri[:, :], AXL.X, ALU.add))
                link(V.tensor_tensor(left, counts[:, 0:E], room, ALU.min))
                link(V.tensor_scalar(pairs(mine[:, own_e])[:, :, 1], pairs(left)[:, :, 1], rank[:, 0:1], None, ALU.is_ge))
                link(V.tensor_scalar(pairs(left)[:, :, 0], pairs(left)[:, :, 0], rank[:, 0:1], None, ALU.add))
                link(V.tensor_scalar(pairs(mine[:, own_e])[:, :, 0], pairs(left)[:, :, 0], float(SLOTS), None, ALU.is_gt))
                own(V.tensor_copy(over[:, 2:3], over[:, 0:1]), S["over"], 1)
                make_pick(0)
                split_lo(l, 0, 1, 1, 0)
                split_lo(l, 1, 1, 1, 0)
                tokens_lo(0, 0)
                tokens_lo(0, 1)

                def pair_step(j, j0, first=False, last=False):
                    it = 0 if isinstance(j, int) else j
                    third = lambda i: (2 * j + i, 2 * j0 + i)
                    if not first:
                        sums_lo(j - 1)
                    split_lo(l, 2, *third(1), it)
                    split_lo(l, 0, *third(2), it)
                    slot_weights(j)
                    split_lo(l, 1, *third(2), it)
                    if not last:
                        make_pick(j + 1)
                    hidden(j, 0)
                    hidden(j, 1)
                    if not last:
                        tokens_lo(j + 1, 0)
                    hidden_lo(j + 1)
                    if not last:
                        tokens_lo(j + 1, 1)
                    split_lo(l, 2, *third(2), it)
                    if not last:
                        split_lo(l, 0, *third(3), it)
                        split_lo(l, 1, *third(3), it)

                pair_step(0, 0, first=True)
                with dve.Fori(1, PAIRS - 1) as j:
                    pair_step(j, 0)
                pair_step(PAIRS - 1, PAIRS - 1, last=True)
                sums_lo(PAIRS - 1)
                dve.wait_ge(S["gates_f"], 2)
                dve.wait_ge(S["scattered"], PAIRS)
                for i in range(4):
                    t, half = divmod(i, 2)
                    cols = slice(512 * half, 512 * half + 512)
                    link(V.tensor_tensor(tmp2, pb[i][:, :], gates[:, 1, cols], ALU.mult))
                    link(V.tensor_tensor(x[:, t, cols], x[:, t, cols], tmp2, ALU.add))

                def overflow(l, e, i):
                    for t in range(TT):
                        V.tensor_scalar(pick[:, t, :], iota[:, :], place2[:, t, bass.ds(e + 1, 1)], None,
                                        ALU.is_equal).then_inc(S["over_pick"], 1)
                    dve.wait_ge(S["over_pe"], 5 * i + 3)
                    V.tensor_copy(wslot[:, 0:1], pb[6][:, T:T + 1]).then_inc(S["over_dve"], 1)
                    dve.wait_ge(S["over_act"], 4 * i + 4)
                    dve.wait_ge(S["over_dve"], 3 * i + 1)
                    V.scalar_tensor_tensor(h[:, 0, :], sg[:, 0, :], wslot[:, 0:1], pb[4][:, DE:2 * DE], ALU.mult,
                                           ALU.mult).then_inc(S["over_dve"], 1)
                    dve.wait_ge(S["over_pe"], 5 * i + 5)
                    V.tensor_copy(xn2[:, 0, 0:512], pb[6][:, :]).then_inc(S["over_dve"], 1)
                    dve.wait_ge(S["over_down"], i + 1)
                    for n in range(4):
                        t, half = divmod(n, 2)
                        cols = slice(512 * half, 512 * half + 512)
                        V.tensor_tensor(xn2[:, 1, cols], pb[n][:, :], gates[:, 1, cols], ALU.mult).then_inc(S["over_prod"], 1)
                        dve.wait_ge(S["over_prod"], 4 * i + n + 1)
                        dve.wait_ge(S["over_x"], 4 * i + 4 + n)
                        V.tensor_tensor(x[:, t, cols], x[:, t, cols], xn2[:, 1, cols], ALU.add).then_inc(S["over_x"], 1)

                dve.sem_inc(S["over_x"], 4)

                def overflow_skip(i, n):
                    dve.wait_ge(S["over_x"], 4 * i + 4)
                    for name, each in (("over_pick", TT), ("over_dve", 3), ("over_prod", 4), ("over_x", 4)):
                        dve.sem_inc(S[name], each * n)

                def next_places():
                    dve.wait_ge(S["over_down"], E)
                    link(V.tensor_scalar(place2[:, :, 1:E + 1], place2[:, :, 1:E + 1], float(-SLOTS), None, ALU.add))

                def overflow_added(chunks):
                    dve.wait_ge(S["over_x"], 4 * E * chunks + 4)
                    dve.sem_inc(S["over_prod"], 1)

                overflow_pass(dve, l, overflow, overflow_skip, between=next_places, after=overflow_added)
                dve.wait_ge(S["end_pe"], 1)
                dve.wait_ge(S["end_act"], 1)
                dve.wait_ge(S["end_sp"], 1)
                for s in S.values():
                    dve.sem_clear(s)
                dve.sem_inc(layer_done, 1)

            dve.wait_ge(fin_sq, TT + 1)
            V.reciprocal(rstd[:, :], ss[:, 2:4]).then_inc(fin_dve, 1)
            dve.wait_ge(fin_dve, 1)
            for t in range(TT):
                V.tensor_scalar(xo[:, t, :], x[:, t, :], rstd[:, t:t + 1], None, ALU.mult).then_inc(fin_dve, 1)
            dve.wait_ge(fin_dve, 3)
            dve.wait_ge(const_in, 16 * 10)
            for t in range(TT):
                V.tensor_tensor(xo[:, t, :], xo[:, t, :], fnw[:, :], ALU.mult).then_inc(fin_dve, 1)

        @block.tensor
        def _(pe):
            M, TR = nc.tensor.matmul, nc.tensor.transpose

            def ada(l, i, cols_bank, row_banks):
                pe.wait_ge(ada_sum, ADA_STEPS * (2 * l + i + 1))
                for c in range(2 * KD):
                    ins = M(cols_bank[:, c:c + 1], ada_acc[:, c // KD, c % KD::KD], ones[:, 0:1], start=True, stop=True)
                ins.then_inc(S["ada_cols"], 1)
                for half in range(2):
                    ins = M(row_banks[half][:, :], ones[:, :], ada_acc[:, 2, 512 * half:512 * half + 512],
                            start=True, stop=True)
                ins.then_inc(ada_taken, 1)

            def turn(src, dst_banks, ready, done):
                pe.wait_ge(ready, TT)
                for kk in range(KD):
                    for t in range(TT):
                        c = T * (kk % 2) + P * t
                        ins = TR(dst_banks[kk // 2][:, c:c + P], src[:, t, kk::KD], ident[:, :])
                    if kk % 2:
                        ins.then_inc(done, 1)

            emptied = []
            n_act = 0
            for i in range(N_W):
                if i < W_DT:
                    emptied.append(("conv", 2 * i + 2))
                elif i == W_DT:
                    emptied.append(("dt_in", 1))
                elif W_LX <= i < W_HV:
                    emptied.append(("conv_lx", 2 * (i - W_LX) + 2))
                else:
                    n_act += 1
                    emptied.append(("w_act", n_act))

            def project(l, i):
                u = U_W + i
                bank = pb[i % W_BANKS]
                if i >= W_BANKS:
                    pe.wait_ge(S[emptied[i - W_BANKS][0]], emptied[i - W_BANKS][1])
                wait_unit(pe, l, u)
                if W_COLS[i] in range(C_Z, C_Z + SSD_IN) or W_COLS[i] in range(C_HV, C_HV + 512) or i == W_DT:
                    n = SSD_HEADS if i == W_DT else 256
                    for t in range(TT):
                        for k in range(KD):
                            ins = M(bank[:, n * t:n * t + n], hT[:, k, P * t:P * t + P],
                                    ring_unit(u)[:, n * k:n * k + n], start=k == 0, stop=k == KD - 1)
                else:
                    for c in range(2):
                        for k in range(KD):
                            w = ring_unit(u)[:, 256 * k + P * c:256 * k + P * c + P]
                            ins = M(bank[:, T * c:T * c + T], w, hT[:, k, :], start=k == 0, stop=k == KD - 1)
                ins.then_inc(pe_unit, 1)

            def gate_up(l, n, b, half, bank, xs):
                wh, wl = (w[b][:, :].rearrange("p (g k c) -> p g k c", g=2, k=4) for w in (whi, wlo))
                for k in range(4):
                    kk = 4 * half + k
                    first, last = half == 0 and k == 0, half == 1 and k == 3
                    M(bank, xhi[:, kk, xs], wh[:, :, k, :], start=first, stop=False)
                    M(bank, xhi[:, kk, xs], wl[:, :, k, :], start=False, stop=False)
                    ins = M(bank, xlo[:, kk, xs], wh[:, :, k, :], start=False, stop=last)
                return ins

            def pair_gate_up(l, j, side, half):
                q = 2 * half + side
                n, b = 2 * j + 1 + q // 3, q % 3
                wait_split(pe, l, b, n)
                pe.wait_ge(S["xe_lo"], 2 * j + half + 1)
                gate_up(l, n, b, half, pb[4 + side][:, :], slice(0, SLOTS)).then_inc(S[f"x_used{b}"], 1)

            def gather_half(bank, half):
                for k in range(4):
                    for t in range(TT):
                        for part in (xth, xtl):
                            ins = M(bank[:, P * k:P * k + P], part[:, t, P * (4 * half + k):P * (4 * half + k) + P], pick[:, t, :],
                                    start=t == 0 and part is xth, stop=t == TT - 1 and part is xtl)
                return ins

            def gather(j, half):
                pe.wait_ge(S["pick"], TT * (j + 1))
                gather_half(pb[6 + half], half).then_inc(S["gathered"], 1)

            def turn_pick(bank, wcol, n):
                for t in range(TT):
                    TR(bank[:, P * t:P * t + P], pick[:, t, :].bitcast(fp32), ident[:, :])
                for t in range(TT):
                    ins = M(bank[:, T:T + n], pick[:, t, :].bitcast(fp32), wcol(t), start=t == 0, stop=t == TT - 1)
                return ins

            def turned(j):
                turn_pick(pb[6], lambda t: wts[:, t, 2 * j + 1:2 * j + 3] if isinstance(j, int)
                          else wts[:, t, bass.ds(2 * j + 1, 2)], 2).then_inc(S["pick_turned"], 1)

            def turn_hidden(count):
                pe.wait_ge(S["h_ready"], count)
                for i in range(2):
                    for hc in range(2):
                        ins = TR(pb[4][:, T * i + P * hc:T * i + P * hc + P], h[:, i, P * hc:P * hc + P], ident[:, :])
                ins.then_inc(S["h_turned"], 1)

            def products(acc, a_cols, hc, cs, b, start, stop):
                wh, wl = (w[b][:, :].rearrange("p (k c) -> p k c", k=2) for w in (whi, wlo))
                M(acc, hTh[a_cols], wh[:, hc, cs], start=start, stop=False)
                M(acc, hTh[a_cols], wl[:, hc, cs], start=False, stop=False)
                return M(acc, hTl[a_cols], wh[:, hc, cs], start=False, stop=stop)

            def shared_down(l):
                wait_split(pe, l, 2, 0)
                pe.wait_ge(S["h_lo"], 1)
                for hc in range(2):
                    for t in range(TT):
                        for half in range(2):
                            ins = products(pb[2 * t + half][:, :], (slice(None), t, slice(P * hc, P * hc + P)), hc,
                                           slice(512 * half, 512 * half + 512), 2, hc == 0, False)
                ins.then_inc(S["x_used2"], 1)

            def pair_down(l, j, last=False):
                pe.wait_ge(S["h_lo"], j + 2)
                for side in range(2):
                    b = 1 + side
                    wait_split(pe, l, b, 2 * j + 2)
                    for half in range(2):
                        if side == 0 and not last:
                            pe.wait_ge(S["xe_lo"], 2 * j + 3 + half)
                        for hc in range(2):
                            ins = products(pb[6 + half][:, :], (slice(None), side, slice(P * hc, P * hc + P)), hc,
                                           slice(512 * half, 512 * half + 512), b, side + hc == 0, side + hc == 2)
                    ins.then_inc(S[f"x_used{b}"], 1)

            def scatter(j, last=False):
                pe.wait_ge(S["put_ready"], j + 1)
                pe.wait_ge(S["y_lo"], 2 * j + 2)
                for t in range(TT):
                    for half in range(2):
                        for part in (yhi, ylo):
                            ins = M(pb[2 * t + half][:, :], put[:, P * t:P * t + P], part[:, 512 * half:512 * half + 512],
                                    start=False, stop=last and part is ylo)
                ins.then_inc(S["scattered"], 1)

            pe.wait_ge(const_in, 16 * 9)
            pe.wait_ge(params_in, 16 * 17 * L)
            with pe.Fori(0, L) as l:
                pe.wait_ge(S["prow_ready"], 2)
                TR(pb[1][:, 0:R_END], prow_now[0:R_END, :],
                   ident[0:R_END, 0:R_END]).then_inc(S["params_turned"], 1)
                ada(l, 0, pb[0], (pb[2], pb[3]))
                turn(xn, pb[4:8], S["xn_ready"], S["h_chunks"])
                pe.wait_ge(S["modc_s"], 1)
                pe.wait_ge(S["modc"], 1)
                pe.wait_ge(S["pcol"], 1)
                pe.wait_ge(S["hT_ready"], KD)
                pe.wait_ge(S["gates_m"], 2)
                for i in range(W_HQ + 2):
                    project(l, i)

                pe.wait_ge(S["a_ready"], 1)
                M(pb[3][:, 0:32], tri[:, :], dts[:, 3, :], start=True, stop=True)
                M(pb[3][:, 32:64], ones[:, :], dts[:, 3, :], start=True, stop=True).then_inc(S["acum_done"], 1)
                pe.wait_ge(S["xbc_ready"], 6)
                chunk = lambda c: slice(P * c, P * c + P)
                for c in range(2):
                    for g in range(2):
                        i = 2 * c + g
                        ins = M(pb[4][:, P * i:P * i + P], xbcT[:, 8 + g, chunk(c)], xbcT[:, 10 + g, chunk(c)],
                                start=True, stop=True)
                ins.then_inc(S["cb_done"], 1)
                for g in range(2):
                    ins = TR(pb[5][:, P * g:P * g + P], xbcT[:, 8 + g, chunk(0)], ident[:, :])
                ins.then_inc(S["btok_done"], 1)
                for i in range(4):
                    c, half = divmod(i, 2)
                    if i == 2:
                        pe.wait_ge(S["cb_ready"], 1)
                    if i == 3:
                        pe.wait_ge(S["btok_ready"], 1)
                    for j in range(4):
                        ins = TR(pb[(6, 7, 4, 5)[i]][:, P * j:P * j + P], xbcT[:, 4 * half + j, chunk(c)], ident[:, :])
                    ins.then_inc(S["xs_turned"], 1)
                for i in range(W_Z, W_Z + 4):
                    project(l, i)
                pe.wait_ge(S["xdec_ready"], 1)
                pe.wait_ge(S["btok_ready"], 1)
                pe.wait_ge(S["dec_in"], 1)
                for g in range(2):
                    if g:
                        pe.wait_ge(S["st_ready"], g)
                    M(pb[3][:, :], btok[:, g, :], xdec[:, 512 * g:512 * g + 512], start=True,
                      stop=True).then_inc(S["st_done"], 1)
                pe.wait_ge(S["xh_ready"], 4)

                def diff(q):
                    c, h0 = q // 4, 4 * (q % 4)
                    bank = pb[4 + q % 2]
                    if q >= 2:
                        pe.wait_ge(S["diff_sub"], q - 1)
                    M(bank[:, :].rearrange("p (h t) -> p h t", h=4), ident[:, :], bcast(neg[:, :], 1, 4), start=True,
                      stop=False, skip_group_check=True)
                    for j in range(4):
                        ac = dts[:, 3, 16 * c + h0 + j:16 * c + h0 + j + 1].broadcast_to([P, P])
                        ins = M(bank[:, P * j:P * j + P], ac, tri[:, :], start=False, stop=True, skip_group_check=True)
                    ins.then_inc(S["diff_done"], 1)

                def y_diag(q):
                    c, h0, i = q // 4, 4 * (q % 4), q // 2
                    if i >= 2 and q % 2 == 0:
                        pe.wait_ge(S["y_taken"], i - 1)
                    pe.wait_ge(S["m_ready"], q + 1)
                    pe.wait_ge(S["xdt_ready"], c + 1)
                    for j in range(4):
                        hd = h0 + j
                        o = SSD_HD * (hd % 8)
                        ins = M(pb[6 + i % 2][:, o:o + SSD_HD], mdec[:, q % 2, j, :],
                                xdt[:, c, SSD_HD * hd:SSD_HD * hd + SSD_HD], start=True, stop=True)
                    ins.then_inc(S["ydiag"], 1)

                def y_off(g):
                    pe.wait_ge(S["st_ready"], 2)
                    if g:
                        pe.wait_ge(S["yoff_taken"], g)
                    M(pb[3][:, :], xbcT[:, 10 + g, chunk(1)], stT[:, g, :], start=True, stop=True).then_inc(S["yoff"], 1)

                for q in range(9):
                    if q < 8:
                        diff(q)
                    if q == 5:
                        y_off(0)
                    if q:
                        y_diag(q - 1)
                y_off(1)
                project(l, W_LX)
                for i in range(4):
                    c, g = divmod(i, 2)
                    pe.wait_ge(S["y_norm"], i + 1)
                    pe.wait_ge(S["y_taken"], 4)
                    for j in range(4):
                        o = 512 * g + P * j
                        ins = TR(pb[4 + i][:, P * j:P * j + P], y[:, c, o:o + P], ident[:, :])
                    ins.then_inc(S["y_turned"], 1)

                project(l, W_LX + 1)

                def level(i):
                    lq, lk = (qkg[:, 0, :, :], qkg[:, 1, :, :]) if i == 0 else (lev_q[i % 2], lev_k[i % 2])
                    if i:
                        pe.wait_ge(S["lev_ready"], 2 * i)
                    if i < 2:
                        pe.wait_ge(S["yT_ready"], 4)
                    else:
                        pe.wait_ge(S["att_taken"], 2 * i - 2)
                    for hd in range(HG_H):
                        for t in range(TT):
                            o = P * (2 * (hd % 2) + t)
                            ins = M(pb[4 + 2 * (i % 2) + hd // 2][:, o:o + P], lk[:, hd, chunk(t)], lq[:, hd, chunk(t)],
                                    start=True, stop=True)
                    ins.then_inc(S["att_done"], 1)

                def project_out(i):
                    wait_unit(pe, l, U_OUT + i)
                    for k2 in range(2):
                        k = 2 * i + k2
                        for t in range(TT):
                            for half in range(2):
                                c = 1024 * k2 + 512 * half
                                ins = M(pb[2 * t + half][:, :], yT[:, k, chunk(t)], ring_unit(U_OUT + i)[:, c:c + 512],
                                        start=k == 0, stop=k == KY - 1)
                    ins.then_inc(pe_unit, 1)

                pe.wait_ge(S["k_ready"], 1)
                pe.wait_ge(S["w_act"], 4)
                for i in range(6):
                    level(i)
                    project(l, W_HV + i)
                pe.wait_ge(S["conv_lx"], 4)
                pe.wait_ge(S["bd_in"], 16 * 4)
                pe.wait_ge(S["w_act"], 14)
                pe.wait_ge(S["yoff_taken"], 2)
                for k in range(2):
                    for j in range(LRU_J):
                        o = T * (j % 2)
                        ins = M(pb[2 * k + j // 2][:, o:o + T], bd[:, k, j, :], lru_x[:, j, :], start=True, stop=True)
                ins.then_inc(S["gate_mm"], 1)
                level(6)
                level(7)
                pe.wait_ge(S["gate_sig"], 8)
                project_out(0)
                pe.wait_ge(S["lev_ready"], 2 * LEVELS)
                pe.wait_ge(S["att_taken"], 2 * LEVELS - 2)
                for hd in range(HG_H):
                    ins = M(pb[4][:, P * hd:P * hd + P], lev_k[0][:, hd, chunk(0)], lev_q[0][:, hd, chunk(1)],
                            start=True, stop=True)
                ins.then_inc(S["cross_done"], 1)
                project_out(1)
                pe.wait_ge(S["att_taken"], 2 * LEVELS)
                pe.wait_ge(S["cross_ready"], 1)
                for hd in range(HG_H):
                    vh = v[:, :, P * hd:P * hd + P]
                    o = T * (hd % 2)
                    bank = pb[4 + hd // 2]
                    M(bank[:, o:o + P], vh[:, 0, :], attn[:, 2 * hd, :], start=True, stop=True)
                    M(bank[:, o + P:o + T], vh[:, 1, :], attn[:, 2 * hd + 1, :], start=True, stop=False)
                    ins = M(bank[:, o + P:o + T], vh[:, 0, :], cross[:, hd, :], start=False, stop=True)
                ins.then_inc(S["o_done"], 1)
                project_out(2)
                for i in range(2):
                    pe.wait_ge(S["o_sq"], i + 1)
                    ins = M(pb[6 + i][:, :].rearrange("p (h t) -> p h t", h=2), ones[:, :], lev_e[0][:, 2 * i:2 * i + 2, :],
                            start=True, stop=True)
                ins.then_inc(S["o_sum"], 1)
                project_out(3)
                pe.wait_ge(S["yT_ready"], 8)
                project_out(4)
                ada(l, 1, pb[5], (pb[6], pb[7]))
                project_out(5)
                pe.wait_ge(S["lru_sq"], 1)
                for j in range(LRU_J):
                    ins = M(pb[4][:, 0:T], ones[:, :], lru_v[:, j, :], start=j == 0, stop=j == LRU_J - 1)
                ins.then_inc(S["lru_sum"], 1)
                pe.wait_ge(S["yT_ready"], 9)
                project_out(6)
                project_out(7)

                pe.wait_ge(S["modc_s"], 2)
                pe.wait_ge(S["gates_f"], 2)
                pe.wait_ge(S["lru_root"], 1)
                turn(xn2, pb[0:4], S["xn2_ready"], S["h2_chunks"])
                pe.wait_ge(S["router_in"], 16)
                pe.wait_ge(S["h2_ready"], KD)
                pe.wait_ge(S["x_mid"], 4)
                for t in range(TT):
                    for k in range(KD):
                        ins = M(pb[7][:, E * t:E * t + E], h2T[:, k, chunk(t)], rw[:, k, :], start=k == 0, stop=k == KD - 1)
                ins.then_inc(S["logits"], 1)
                pe.wait_ge(S["x_lo"], 4)
                for t in range(TT):
                    for half in range(2):
                        for k in range(4):
                            ins = TR(pb[2 * t + half][:, P * k:P * k + P], h2T[:, 4 * half + k, chunk(t)], ident[:, :])
                        ins.then_inc(S["rows_turned"], 1)
                for half in range(2):
                    wait_split(pe, l, half, 0)
                    for t in range(TT):
                        ins = gate_up(l, 0, half, half, pb[4 + t][:, :], slice(P * t, P * t + P))
                    ins.then_inc(S[f"x_used{half}"], 1)
                pe.wait_ge(S["chosen"], 1)
                M(pb[7][:, 0:E], tri[:, :], chosen[:, 0, :], start=True, stop=True)
                M(pb[7][:, E:2 * E], tri[:, :], chosen[:, 1, :], start=True, stop=False)
                M(pb[7][:, E:2 * E], ones[:, :], chosen[:, 0, :], start=False, stop=True)
                M(pb[7][:, 2 * E:3 * E], ones[:, :], chosen[:, 0, :], start=True, stop=False)
                M(pb[7][:, 2 * E:3 * E], ones[:, :], chosen[:, 1, :], start=False, stop=True).then_inc(S["placed"], 1)
                turn_hidden(TT)
                shared_down(l)
                pe.wait_ge(S["wts"], TT)
                pe.wait_ge(S["over"], 1)
                pe.wait_ge(S["xt_lo"], 4)
                gather(0, 0)
                gather(0, 1)

                def pair_step(j, first=False, last=False):
                    pair_gate_up(l, j, 0, 0)
                    pair_gate_up(l, j, 1, 0)
                    if not first:
                        scatter(j - 1)
                    turned(j)
                    pair_gate_up(l, j, 0, 1)
                    pair_gate_up(l, j, 1, 1)
                    if not last:
                        pe.wait_ge(S["put_ready"], j + 1)
                        gather(j + 1, 0)
                    turn_hidden(TT + 2 * j + 2)
                    if not last:
                        gather(j + 1, 1)
                    pair_down(l, j, last=last)

                pair_step(0, first=True)
                with pe.Fori(1, PAIRS - 1) as j:
                    pair_step(j)
                pair_step(PAIRS - 1, last=True)
                scatter(PAIRS - 1, last=True)

                def overflow(l, e, i):
                    pe.wait_ge(S["over_pick"], TT * i + TT)
                    pe.wait_ge(S["over_x"], 4 * i + 4)
                    for half in range(2):
                        gather_half(pb[(5, 7)[half]], half).then_inc(S["over_pe"], 1)
                    turn_pick(pb[6], lambda t: wts[:, t, bass.ds(e + 1, 1)], 1).then_inc(S["over_pe"], 1)
                    pe.wait_ge(S["over_act"], 4 * i + 2)
                    pe.wait_ge(S["over_full"], 16 * (5 * i + 5))
                    for k in range(KD):
                        w = ring[:, k // 4, :].rearrange("p (g k c) -> p g k c", g=2, k=4)
                        ins = M(pb[4][:, :], h2T[:, k, 0:SLOTS], w[:, :, k % 4, :], start=k == 0, stop=k == KD - 1)
                    ins.then_inc(S["over_pe"], 1)
                    pe.wait_ge(S["over_act"], 4 * i + 3)
                    pe.wait_ge(S["over_dve"], 3 * i + 2)
                    for hc in range(2):
                        ins = M(pb[6][:, T * hc:T * hc + T], h[:, 0, P * hc:P * hc + P], put[:, :].bitcast(fp32),
                                start=True, stop=True)
                    ins.then_inc(S["over_pe"], 1)
                    pe.wait_ge(S["over_dve"], 3 * i + 3)
                    for t in range(TT):
                        for half in range(2):
                            for hc in range(2):
                                ins = M(pb[2 * t + half][:, :], xn2[:, 0, T * hc + P * t:T * hc + P * t + P],
                                        ring[:, 2, 1024 * hc + 512 * half:1024 * hc + 512 * half + 512],
                                        start=hc == 0, stop=hc == 1)
                    ins.then_inc(S["over_down"], 1)

                def overflow_skip(i, n):
                    pe.wait_ge(S["over_x"], 4 * i + 4)
                    pe.sem_inc(S["over_pe"], 5 * n)
                    pe.sem_inc(S["over_down"], n)

                overflow_pass(pe, l, overflow, overflow_skip)
                pe.sem_inc(S["end_pe"], 1)
                pe.wait_ge(layer_done, l + 1)


SIGNALS = """ada_cols prow_ready pnow bd_in params_turned pcol modc_s modc ss_mix xn_ready h_chunks hT_ready
    gates_m gates_f lb_in lam_in lam_exp lruc_ready conv xbc_ready conv_lx w_act
    dt_in dt_exp a_ready acum_done dec_in eacum k_ready cb_done cb_ready btok_done btok_ready
    xs_turned xh_ready xdt_ready xdec_ready st_done st_ready diff_done diff_sub diff_exp m_ready ydiag yoff
    y_taken yoff_taken y_gated y_sq y_norm y_turned yT_ready logf lev_in lev_exp lev_ready att_done att_taken
    cross_done cross_ready o_done o_sq o_sum o_root gate_mm gate_sig lru_tanh lru_w lru_sqrt lru_y lru_sq
    lru_sum lru_root x_mid router_in ss_ffn xn2_ready h2_chunks h2_ready x_hi x_lo logits scores
    x_hi0 x_hi1 x_hi2 x_used0 x_used1 x_used2 silu_g h_ready h_turned h_hi h_lo y_hi y_lo scattered
    rows_turned xt_hi xt_lo chosen placed wts over pick pick_turned put_ready wslot gathered xe_hi xe_lo pick0
    over_x over_full over_pe over_act over_dve over_pick over_down over_prod dve_order end_pe end_act end_sp""".split()


def kernel(**inputs):
    import numpy as np
    import concourse.bacc as bacc
    from concourse.bass_utils import run_bass_kernel_spmd

    i = np.arange(P)
    part, col = i[:, None], i[None, :]
    consts = np.concatenate([
        (part == col).astype(np.float32),
        (part <= col).astype(np.float32),
        np.where(col < part, np.float32(NEG), np.float32(0)),
        np.ones((P, P), np.float32),
        np.broadcast_to((np.arange(8)[None, :] < np.arange(8)[:, None]).astype(np.float32).reshape(1, 64), (P, 64)),
        np.broadcast_to(i[None, :].astype(np.float32), (P, P)),
    ], axis=1)
    masks = [part == col]
    for level in range(1, LEVELS):
        m = 1 << (level - 1)
        masks.append((part // (2 * m) == col // (2 * m)) & (part // m % 2 == 0) & (col // m % 2 == 1))
    masks = np.concatenate(masks, axis=1).astype(np.uint32)

    nc = bacc.Bacc("TRN2", target_bir_lowering=False, num_devices=1)
    arrays = {f"in_{k}": np.ascontiguousarray(v) for k, v in inputs.items()}
    arrays["in_consts"] = np.ascontiguousarray(consts)
    arrays["in_masks"] = np.ascontiguousarray(masks)
    aps = {k[3:]: nc.dram_tensor(k, v.shape, mybir.dt.from_np(v.dtype), kind="ExternalInput").ap()
           for k, v in arrays.items()}
    out = nc.dram_tensor("out", (1, T, D), fp32, kind="ExternalOutput").ap()
    build(nc, aps, out)
    got = run_bass_kernel_spmd(nc, [arrays], core_ids=[0])
    return got.results[0]["out"]
```
